# Optimizing a Trainium2 kernel written in Bass

```python
import math
import jax, jax.numpy as jnp
from jax import lax
import numpy as np

D_MODEL = 1024
BATCH = 1
SEQ = 256
DEPTH = 1

MEM_LEN = 256
CONV_CH = D_MODEL
CONV_K = 31
DIFF_HEADS = D_MODEL // 128
DIFF_HEAD_DIM = 64
DIFF_V_DIM = 2 * DIFF_HEAD_DIM
DIFF_WIDTH = DIFF_HEADS * DIFF_V_DIM
X_HEADS = 4
X_HEAD_DIM = D_MODEL // X_HEADS
X_WIDTH = X_HEADS * X_HEAD_DIM
N_BRANCH = 3
Q_BLOCK = 128

IN_SIZES = (
    2 * CONV_CH,
    CONV_CH,
    DIFF_WIDTH,
    DIFF_WIDTH,
    DIFF_WIDTH,
    DIFF_WIDTH,
    X_WIDTH,
    X_WIDTH,
    N_BRANCH * D_MODEL,
)
IN_COLS = sum(IN_SIZES)
IN_SPLITS = tuple(int(c) for c in np.cumsum(IN_SIZES)[:-1])


def rms_norm(x, g, eps=1e-6):
    xf = x.astype(jnp.float32)
    y = xf * lax.rsqrt(jnp.mean(xf * xf, axis=-1, keepdims=True) + eps)
    return (y * g.astype(jnp.float32)).astype(x.dtype)

def layer_norm(x, g, b, eps=1e-5):
    xf = x.astype(jnp.float32)
    mu = jnp.mean(xf, axis=-1, keepdims=True)
    xc = xf - mu
    y = xc * lax.rsqrt(jnp.mean(xc * xc, axis=-1, keepdims=True) + eps)
    return (y * g.astype(jnp.float32) + b.astype(jnp.float32)).astype(x.dtype)

def alibi_slopes(n_heads):
    return 2.0 ** (-8.0 * jnp.arange(1, n_heads + 1, dtype=jnp.float32) / n_heads)

def lambda_init_for(layer_idx):
    return 0.8 - 0.6 * math.exp(-0.3 * layer_idx)

def conformer_conv_branch(a_glu, gate, dw, dw_b, ln_g, ln_b, w_proj):
    a, b = jnp.split(a_glu, 2, axis=-1)
    u = a * jax.nn.sigmoid(b)
    u = lax.conv_general_dilated(
        u, dw[:, None, :], window_strides=(1,), padding=[(CONV_K - 1, 0)],
        dimension_numbers=("NWC", "WIO", "NWC"), feature_group_count=CONV_CH) + dw_b
    u = layer_norm(u, ln_g, ln_b)
    u = jax.nn.silu(u) * jax.nn.silu(gate)
    return u @ w_proj

def differential_attention_branch(q, k, v, gate, qn_g, kn_g, lq1, lk1, lq2, lk2,
                                  subln_g, w_proj, lambda_init):
    B, S = q.shape[0], q.shape[1]
    H, d = DIFF_HEADS, DIFF_HEAD_DIM
    nb = S // Q_BLOCK
    q = rms_norm(q.reshape(B, S, H, 2, d), qn_g)
    k = rms_norm(k.reshape(B, S, H, 2, d), kn_g)
    kt = k.transpose(0, 2, 3, 1, 4)
    vt = v.reshape(B, S, H, DIFF_V_DIM).transpose(0, 2, 1, 3)
    qb = q.reshape(B, nb, Q_BLOCK, H, 2, d).transpose(1, 0, 3, 4, 2, 5)
    lam = (jnp.exp(jnp.sum(lq1.astype(jnp.float32) * lk1.astype(jnp.float32)))
           - jnp.exp(jnp.sum(lq2.astype(jnp.float32) * lk2.astype(jnp.float32)))
           + lambda_init)
    slopes = alibi_slopes(H)
    scale = DIFF_HEAD_DIM ** -0.5
    kpos = jnp.arange(S)

    def one_block(args):
        qblk, t0 = args
        tpos = t0 + jnp.arange(Q_BLOCK)
        dist = (tpos[:, None] - kpos[None, :]).astype(jnp.float32)
        bias = -slopes[:, None, None] * dist
        s = jnp.einsum("bhmqd,bhmkd->bhmqk", qblk, kt).astype(jnp.float32) * scale
        s = s + bias[None, :, None]
        s = jnp.where(dist >= 0, s, -jnp.inf)
        p = jax.nn.softmax(s, axis=-1)
        a = (p[:, :, 0] - lam * p[:, :, 1]).astype(vt.dtype)
        return jnp.einsum("bhqk,bhkd->bhqd", a, vt)

    o = lax.map(one_block, (qb, jnp.arange(nb) * Q_BLOCK))
    o = o.transpose(1, 0, 3, 2, 4).reshape(B, S, H, DIFF_V_DIM)
    o = rms_norm(o, subln_g) * (1.0 - lambda_init)
    o = o.reshape(B, S, DIFF_WIDTH) * jax.nn.silu(gate)
    return o @ w_proj

def memory_cross_attention_branch(q, gate, mem_h, w_mem_kv, qn_g, kn_g, w_proj):
    B, S = q.shape[0], q.shape[1]
    M = mem_h.shape[1]
    k, v = jnp.split(mem_h @ w_mem_kv, 2, axis=-1)
    q = rms_norm(q.reshape(B, S, X_HEADS, X_HEAD_DIM), qn_g)
    k = rms_norm(k.reshape(B, M, X_HEADS, X_HEAD_DIM), kn_g)
    v = v.reshape(B, M, X_HEADS, X_HEAD_DIM)
    s = jnp.einsum("bshd,bmhd->bhsm", q, k).astype(jnp.float32) * (X_HEAD_DIM ** -0.5)
    p = jax.nn.softmax(s, axis=-1).astype(v.dtype)
    o = jnp.einsum("bhsm,bmhd->bshd", p, v).reshape(B, S, X_WIDTH) * jax.nn.silu(gate)
    return o @ w_proj

def first_inputs(seed: int = 0) -> dict:
    key = jax.random.key(seed)
    ks = jax.random.split(key, 24)
    f32 = jnp.float32
    L, D = DEPTH, D_MODEL

    def nrm(k, shape, scale):
        return jax.random.normal(k, shape, f32) * scale

    def gain(k, shape):
        return 1.0 + 0.05 * jax.random.normal(k, shape, f32)

    return {
        "x": jax.random.normal(ks[0], (BATCH, SEQ, D), f32),
        "mem": jax.random.normal(ks[1], (BATCH, MEM_LEN, D), f32),
        "norm_g": gain(ks[2], (L, D)),
        "mem_norm_g": gain(ks[3], (L, D)),
        "w_in": nrm(ks[4], (L, D, IN_COLS), D ** -0.5),
        "conv_dw": nrm(ks[5], (L, CONV_K, CONV_CH), CONV_K ** -0.5),
        "conv_dw_b": nrm(ks[6], (L, CONV_CH), 0.02),
        "conv_ln_g": gain(ks[7], (L, CONV_CH)),
        "conv_ln_b": nrm(ks[8], (L, CONV_CH), 0.02),
        "w_conv_proj": nrm(ks[9], (L, CONV_CH, D), CONV_CH ** -0.5),
        "diff_qn_g": gain(ks[10], (L, DIFF_HEAD_DIM)),
        "diff_kn_g": gain(ks[11], (L, DIFF_HEAD_DIM)),
        "lambda_q1": nrm(ks[12], (L, DIFF_HEAD_DIM), 0.1),
        "lambda_k1": nrm(ks[13], (L, DIFF_HEAD_DIM), 0.1),
        "lambda_q2": nrm(ks[14], (L, DIFF_HEAD_DIM), 0.1),
        "lambda_k2": nrm(ks[15], (L, DIFF_HEAD_DIM), 0.1),
        "diff_subln_g": gain(ks[16], (L, DIFF_V_DIM)),
        "w_diff_proj": nrm(ks[17], (L, DIFF_WIDTH, D), DIFF_WIDTH ** -0.5),
        "w_mem_kv": nrm(ks[18], (L, D, 2 * X_WIDTH), D ** -0.5),
        "x_qn_g": gain(ks[19], (L, X_HEAD_DIM)),
        "x_kn_g": gain(ks[20], (L, X_HEAD_DIM)),
        "w_x_proj": nrm(ks[21], (L, X_WIDTH, D), X_WIDTH ** -0.5),
        "w_out": nrm(ks[22], (L, D, D), D ** -0.5),
    }

def first_block(x, mem, norm_g, mem_norm_g, w_in, conv_dw, conv_dw_b, conv_ln_g, conv_ln_b,
              w_conv_proj, diff_qn_g, diff_kn_g, lambda_q1, lambda_k1, lambda_q2, lambda_k2,
              diff_subln_g, w_diff_proj, w_mem_kv, x_qn_g, x_kn_g, w_x_proj, w_out):
    B, S, D = x.shape
    for l in range(DEPTH):
        h = rms_norm(x, norm_g[l])
        mem_h = rms_norm(mem, mem_norm_g[l])
        (c_glu, c_gate, d_q, d_k, d_v, d_gate, x_q, x_gate, merge) = jnp.split(
            h @ w_in[l], IN_SPLITS, axis=-1)
        y_conv = conformer_conv_branch(c_glu, c_gate, conv_dw[l], conv_dw_b[l],
                                       conv_ln_g[l], conv_ln_b[l], w_conv_proj[l])
        y_diff = differential_attention_branch(
            d_q, d_k, d_v, d_gate, diff_qn_g[l], diff_kn_g[l], lambda_q1[l], lambda_k1[l],
            lambda_q2[l], lambda_k2[l], diff_subln_g[l], w_diff_proj[l], lambda_init_for(l))
        y_mem = memory_cross_attention_branch(x_q, x_gate, mem_h, w_mem_kv[l],
                                              x_qn_g[l], x_kn_g[l], w_x_proj[l])
        g = jax.nn.sigmoid(merge.reshape(B, S, N_BRANCH, D))
        y = g[:, :, 0] * y_conv + g[:, :, 1] * y_diff + g[:, :, 2] * y_mem
        x = x + y @ w_out[l]
    return x


D_MIX = D_MODEL
SB_HEADS = 8
SB_HEAD_DIM = 64
D_SB = SB_HEADS * SB_HEAD_DIM
D_RG = D_MIX - D_SB
RG_BLOCKS = 8
RG_BLOCK_DIM = D_RG // RG_BLOCKS
CONV_WIDTH = 4
RG_C = 8.0
D_IN_PROJ = 3 * D_SB + 2 * D_RG
PEER_HEADS = 8
PEER_N_KEYS = 128
PEER_N_EXPERTS = PEER_N_KEYS * PEER_N_KEYS
PEER_D_KEY = 256
PEER_HALF = PEER_D_KEY // 2
PEER_TOPK = 16
TOKEN_CHUNK = 128
EPS = 1e-6


def rms_norm_2(x, g):
    xf = x.astype(jnp.float32)
    y = xf * lax.rsqrt(jnp.mean(xf * xf, axis=-1, keepdims=True) + EPS)
    return (y * g.astype(jnp.float32)).astype(x.dtype)

def stick_breaking_attention(q, k, v):
    B, H, S, Dh = q.shape
    nb = S // Q_BLOCK
    scale = Dh ** -0.5
    kpos = jnp.arange(S)

    def block(i):
        q_blk = lax.dynamic_slice_in_dim(q, i * Q_BLOCK, Q_BLOCK, axis=2)
        qpos = i * Q_BLOCK + jnp.arange(Q_BLOCK)
        causal = kpos[None, :] < qpos[:, None]
        z = jnp.einsum('bhqd,bhkd->bhqk', q_blk, k).astype(jnp.float32) * scale
        log_beta = jax.nn.log_sigmoid(z)
        log_one_minus = jnp.where(causal, jax.nn.log_sigmoid(-z), 0.0)
        suffix = lax.cumsum(log_one_minus, axis=3, reverse=True) - log_one_minus
        w = jnp.where(causal, jnp.exp(log_beta + suffix), 0.0)
        return jnp.einsum('bhqk,bhkd->bhqd', w.astype(v.dtype), v)

    out = lax.map(block, jnp.arange(nb))
    return out.transpose(1, 2, 0, 3, 4).reshape(B, H, S, Dh)

def causal_depthwise_conv(x, w, bias):
    S = x.shape[1]
    xp = jnp.pad(x, ((0, 0), (CONV_WIDTH - 1, 0), (0, 0)))
    y = xp[:, 0:S, :] * w[0]
    for j in range(1, CONV_WIDTH):
        y = y + xp[:, j:j + S, :] * w[j]
    return y + bias

def rg_lru(x, w_a, b_a, w_x, b_x, lam):
    B, S, C = x.shape
    xb = x.reshape(B, S, RG_BLOCKS, RG_BLOCK_DIM)
    r = jax.nn.sigmoid(jnp.einsum('bsni,nij->bsnj', xb, w_a).reshape(B, S, C) + b_a)
    i_gate = jax.nn.sigmoid(jnp.einsum('bsni,nij->bsnj', xb, w_x).reshape(B, S, C) + b_x)
    log_a = -RG_C * r.astype(jnp.float32) * jax.nn.softplus(-lam.astype(jnp.float32))
    a = jnp.exp(log_a)
    b = jnp.sqrt(-jnp.expm1(2.0 * log_a)) * (i_gate * x).astype(jnp.float32)

    def step(h, ab):
        a_t, b_t = ab
        h = a_t * h + b_t
        return h, h

    h0 = jnp.zeros((B, C), jnp.float32)
    _, hs = lax.scan(step, h0, (a.transpose(1, 0, 2), b.transpose(1, 0, 2)))
    return hs.transpose(1, 0, 2).astype(x.dtype)

def peer_ffn(x, w_query, sub_keys, expert_u, expert_v):
    B, S, D = x.shape
    T = B * S
    xt = x.reshape(T // TOKEN_CHUNK, TOKEN_CHUNK, D)

    def chunk(xc):
        q = jnp.einsum('td,dhk->thk', xc, w_query)
        q = q.reshape(TOKEN_CHUNK, PEER_HEADS, 2, PEER_HALF)
        s = jnp.einsum('thpk,hpnk->thpn', q, sub_keys).astype(jnp.float32)
        top_s, top_i = lax.top_k(s, PEER_TOPK)
        cand_s = top_s[:, :, 0, :, None] + top_s[:, :, 1, None, :]
        cand_i = top_i[:, :, 0, :, None] * PEER_N_KEYS + top_i[:, :, 1, None, :]
        cand_s = cand_s.reshape(TOKEN_CHUNK, PEER_HEADS, PEER_TOPK * PEER_TOPK)
        cand_i = cand_i.reshape(TOKEN_CHUNK, PEER_HEADS, PEER_TOPK * PEER_TOPK)
        best_s, best_pos = lax.top_k(cand_s, PEER_TOPK)
        idx = jnp.take_along_axis(cand_i, best_pos, axis=-1)
        g = jax.nn.softmax(best_s, axis=-1)
        u = jnp.take(expert_u, idx, axis=0)
        v = jnp.take(expert_v, idx, axis=0)
        act = jax.nn.gelu(jnp.einsum('td,thkd->thk', xc, u))
        return jnp.einsum('thk,thkd->td', (g * act).astype(v.dtype), v)

    y = lax.map(chunk, xt)
    return y.reshape(B, S, D)

def second_inputs(seed: int = 0) -> dict:
    key = jax.random.key(seed)
    ks = jax.random.split(key, 24)
    f32 = jnp.float32

    def nrm(k, shape, scale):
        return jax.random.normal(k, shape, f32) * scale

    def gain(k, shape):
        return 1.0 + 0.02 * jax.random.normal(k, shape, f32)

    u_a = jax.random.uniform(ks[11], (DEPTH, D_RG), f32, 0.9, 0.999)
    a_base = u_a ** (1.0 / RG_C)
    rg_lambda = jnp.log(a_base) - jnp.log1p(-a_base)
    return {
        "x": jax.random.normal(ks[0], (BATCH, SEQ, D_MODEL), f32),
        "norm_mix": gain(ks[1], (DEPTH, D_MODEL)),
        "w_in": nrm(ks[2], (DEPTH, D_MODEL, D_IN_PROJ), D_MODEL ** -0.5),
        "q_norm": gain(ks[3], (DEPTH, SB_HEAD_DIM)),
        "k_norm": gain(ks[4], (DEPTH, SB_HEAD_DIM)),
        "conv_w": nrm(ks[5], (DEPTH, CONV_WIDTH, D_RG), CONV_WIDTH ** -0.5),
        "conv_b": nrm(ks[6], (DEPTH, D_RG), 0.01),
        "rg_w_a": nrm(ks[7], (DEPTH, RG_BLOCKS, RG_BLOCK_DIM, RG_BLOCK_DIM), RG_BLOCK_DIM ** -0.5),
        "rg_b_a": nrm(ks[8], (DEPTH, D_RG), 0.01),
        "rg_w_x": nrm(ks[9], (DEPTH, RG_BLOCKS, RG_BLOCK_DIM, RG_BLOCK_DIM), RG_BLOCK_DIM ** -0.5),
        "rg_b_x": nrm(ks[10], (DEPTH, D_RG), 0.01),
        "rg_lambda": rg_lambda,
        "out_norm_sb": gain(ks[12], (DEPTH, D_SB)),
        "out_norm_rg": gain(ks[13], (DEPTH, D_RG)),
        "w_out": nrm(ks[14], (DEPTH, D_MIX, D_MODEL), D_MIX ** -0.5),
        "norm_ffn": gain(ks[15], (DEPTH, D_MODEL)),
        "peer_w_query": nrm(ks[16], (DEPTH, D_MODEL, PEER_HEADS, PEER_D_KEY), D_MODEL ** -0.5),
        "peer_sub_keys": nrm(ks[17], (DEPTH, PEER_HEADS, 2, PEER_N_KEYS, PEER_HALF), PEER_HALF ** -0.5),
        "peer_u": nrm(ks[18], (DEPTH, PEER_N_EXPERTS, D_MODEL), D_MODEL ** -0.5),
        "peer_v": nrm(ks[19], (DEPTH, PEER_N_EXPERTS, D_MODEL), PEER_HEADS ** -0.5),
    }

def second_block(x, norm_mix, w_in, q_norm, k_norm, conv_w, conv_b, rg_w_a, rg_b_a,
              rg_w_x, rg_b_x, rg_lambda, out_norm_sb, out_norm_rg, w_out, norm_ffn,
              peer_w_query, peer_sub_keys, peer_u, peer_v):
    B, S, _ = x.shape
    for l in range(DEPTH):
        h = rms_norm_2(x, norm_mix[l])
        proj = jnp.einsum('bsd,de->bse', h, w_in[l])
        q = proj[:, :, 0:D_SB]
        k = proj[:, :, D_SB:2 * D_SB]
        v = proj[:, :, 2 * D_SB:3 * D_SB]
        x_rg = proj[:, :, 3 * D_SB:3 * D_SB + D_RG]
        g_rg = proj[:, :, 3 * D_SB + D_RG:D_IN_PROJ]

        def to_heads(t):
            return t.reshape(B, S, SB_HEADS, SB_HEAD_DIM).transpose(0, 2, 1, 3)

        qh = rms_norm_2(to_heads(q), q_norm[l])
        kh = rms_norm_2(to_heads(k), k_norm[l])
        o_sb = stick_breaking_attention(qh, kh, to_heads(v))
        o_sb = o_sb.transpose(0, 2, 1, 3).reshape(B, S, D_SB)

        x_rg = causal_depthwise_conv(x_rg, conv_w[l], conv_b[l])
        o_rg = rg_lru(x_rg, rg_w_a[l], rg_b_a[l], rg_w_x[l], rg_b_x[l], rg_lambda[l])
        o_rg = o_rg * jax.nn.gelu(g_rg)

        mixed = jnp.concatenate(
            [rms_norm_2(o_sb, out_norm_sb[l]), rms_norm_2(o_rg, out_norm_rg[l])], axis=-1)
        x = x + jnp.einsum('bse,ed->bsd', mixed, w_out[l])

        h = rms_norm_2(x, norm_ffn[l])
        x = x + peer_ffn(h, peer_w_query[l], peer_sub_keys[l], peer_u[l], peer_v[l])
    return x


def setup_inputs(seed=0):
    out = dict(first_inputs(seed))
    for name, value in second_inputs(seed + 1).items():
        if name != "x":
            out[name + "_2"] = value
    return out


def reference(
    x, mem, norm_g, mem_norm_g, w_in, conv_dw, conv_dw_b, conv_ln_g, conv_ln_b, w_conv_proj,
    diff_qn_g, diff_kn_g, lambda_q1, lambda_k1, lambda_q2, lambda_k2, diff_subln_g, w_diff_proj,
    w_mem_kv, x_qn_g, x_kn_g, w_x_proj, w_out, norm_mix_2, w_in_2, q_norm_2, k_norm_2, conv_w_2,
    conv_b_2, rg_w_a_2, rg_b_a_2, rg_w_x_2, rg_b_x_2, rg_lambda_2, out_norm_sb_2, out_norm_rg_2,
    w_out_2, norm_ffn_2, peer_w_query_2, peer_sub_keys_2, peer_u_2, peer_v_2,
):
    x = first_block(
        x, mem, norm_g, mem_norm_g, w_in, conv_dw, conv_dw_b, conv_ln_g, conv_ln_b, w_conv_proj,
        diff_qn_g, diff_kn_g, lambda_q1, lambda_k1, lambda_q2, lambda_k2, diff_subln_g,
        w_diff_proj, w_mem_kv, x_qn_g, x_kn_g, w_x_proj, w_out,
    )
    return second_block(
        x, norm_mix_2, w_in_2, q_norm_2, k_norm_2, conv_w_2, conv_b_2, rg_w_a_2, rg_b_a_2,
        rg_w_x_2, rg_b_x_2, rg_lambda_2, out_norm_sb_2, out_norm_rg_2, w_out_2, norm_ffn_2,
        peer_w_query_2, peer_sub_keys_2, peer_u_2, peer_v_2,
    )


_drawn_inputs = setup_inputs


def setup_inputs(seed=0):
    import zlib

    import numpy as np

    out = dict(_drawn_inputs(seed))
    spreads = {}
    factors = {'mem_norm_g': 7.937,
     'conv_dw_b': 3.051,
     'conv_ln_g': 2.833,
     'conv_ln_b': 5.416,
     'diff_qn_g': 2.732,
     'diff_kn_g': 2.849,
     'lambda_q2': 200.0,
     'x_qn_g': 8.0,
     'x_kn_g': 8.0,
     'q_norm_2': 5.853,
     'k_norm_2': 5.684,
     'rg_b_a_2': 37.653,
     'rg_b_x_2': 23.326,
     'out_norm_sb_2': 12.649,
     'out_norm_rg_2': 13.187,
     'norm_ffn_2': 12.388,
     'lambda_q1': 3.922,
     'diff_subln_g': 3.641}
    for name, (base, spread) in spreads.items():
        noise = np.random.default_rng([zlib.crc32(name.encode()), seed]).standard_normal(out[name].shape)
        drawn = base * np.exp(spread * noise) if base else spread * noise
        out[name] = __import__('jax').numpy.asarray(drawn.astype(out[name].dtype))
    for name, factor in factors.items():
        out[name] = (out[name] * factor).astype(out[name].dtype)
    return out
```

```python
from contextlib import ExitStack

import concourse.bass as bass
from concourse import mybir

P = 128
F32 = mybir.dt.float32
U32 = mybir.dt.uint32
ALU = mybir.AluOpType
ACT = mybir.ActivationFunctionType
AX = mybir.AxisListType.X

T = 256
TT = T // P
D = 1024
KT = D // P
SLOT = 512
CONV_K = 31
DIFF_HEADS = 8
DIFF_HEAD_DIM = 64
LAMBDA_INIT = 0.2
X_HEADS = 4
X_HEAD_DIM = D // X_HEADS
SB_HEADS = 8
SB_HEAD_DIM = 64
D_SB = SB_HEADS * SB_HEAD_DIM
D_RG = D - D_SB
RG_TILES = D_RG // P
RG_WIDTH = 4
PEER_HEADS = 8
PEER_KEYS = 128
PEER_TOPK = 16
PEER_SIDES = 2 * PEER_HEADS
PICKS = PEER_HEADS * PEER_TOPK
MASKED = -1.0e30
W_RING = 3
UV_RING = 6

VECTORS = [("norm_g", KT), ("mem_norm_g", KT), ("conv_dw", KT * CONV_K), ("conv_dw_b", KT),
           ("conv_ln_g", KT), ("conv_ln_b", KT), ("diff_qn_g", 1), ("diff_kn_g", 1),
           ("lambda_q1", 64), ("lambda_k1", 64), ("lambda_q2", 64), ("lambda_k2", 64),
           ("diff_subln_g", 1), ("x_qn_g", 2), ("x_kn_g", 2), ("norm_mix_2", KT),
           ("q_norm_2", 1), ("k_norm_2", 1), ("conv_w_2", RG_TILES * RG_WIDTH),
           ("conv_b_2", RG_TILES), ("rg_b_a_2", RG_TILES), ("rg_b_x_2", RG_TILES),
           ("rg_lambda_2", RG_TILES), ("out_norm_sb_2", D_SB // P), ("out_norm_rg_2", RG_TILES)]
VECTOR_AT = {}
for _name, _n in VECTORS:
    VECTOR_AT[_name] = (sum(n for _, n in VECTORS[:len(VECTOR_AT)]), _n)
VECTOR_COLS = sum(n for _, n in VECTORS)


class Counter:

    def __init__(self, sem):
        self.sem, self.value = sem, 0


class Step:

    def __init__(self, counter):
        self.counter, self.value, self.waited = counter, None, False


class Queue:

    def __init__(self, name, semaphore):
        self.name, self.semaphore, self.items, self.counter = name, semaphore, [], None

    def stage(self, name):
        self.counter = Counter(self.semaphore(f"{self.name}_{name}"))

    def do(self, instruction, *args, after=(), **named):
        step = Step(self.counter)
        return self.put(step, 1, instruction, args, named, after)

    def dma(self, instruction, *args, counter, after=(), **named):
        step = Step(counter)
        step.waited = True
        return self.put(step, 16, instruction, args, named, after)

    def put(self, step, by, instruction, args, named, after):
        for a in after:
            a.waited = True
        self.items.append((list(after), instruction, args, named, step, by))
        return step

    def number(self):
        for *_, step, by in self.items:
            if step.waited:
                step.counter.value += by
                step.value = step.counter.value

    def emit(self, engine):
        reached = {}
        for after, instruction, args, named, step, by in self.items:
            need = {}
            for a in after:
                need[id(a.counter)] = max(need.get(id(a.counter), (0, None))[0], a.value), a.counter
            for key, (value, counter) in need.items():
                if reached.get(key, 0) < value:
                    engine.wait_ge(counter.sem, value)
                    reached[key] = value
            issued = instruction(*args, **named)
            if step.waited:
                issued.then_inc(step.counter.sem, by)


class Buffer:

    def __init__(self, ap, counter=None):
        self.ap, self.counter, self.free = ap, counter, []


class Ring:
    def __init__(self, buffers):
        self.buffers, self.n = buffers, 0

    def take(self):
        self.n += 1
        return self.buffers[(self.n - 1) % len(self.buffers)]


def build(nc, x, mem, vectors, w_in, w_conv_proj, w_diff_proj, w_mem_kv, w_x_proj, w_out,
          w_in_2, rg_w_a, rg_w_x, w_out_2, norm_ffn, w_query, sub_keys_t, experts, out):
    with ExitStack() as ctx:
        def sb(name, shape, dt=F32):
            return ctx.enter_context(nc.sbuf_tensor(name, [P, *shape], dt))

        def semaphore(name):
            return ctx.enter_context(nc.semaphore(name))

        pe, act, dve, pool, sp = (Queue(n, semaphore) for n in ("pe", "act", "dve", "pool", "sp"))

        def stage(name):
            for q in (pe, act, dve, pool):
                q.stage(name)

        def load_counter(name):
            return Counter(semaphore(f"load_{name}"))

        stage("setup")

        w_space = sb("w_ring", [W_RING * KT * SLOT])
        w_ring = Ring([Buffer(w_space[:, i * KT * SLOT:(i + 1) * KT * SLOT]
                              .rearrange("p (k n) -> p k n", k=KT), load_counter(f"w{i}"))
                       for i in range(W_RING)])
        vec = sb("vec", [VECTOR_COLS])
        actT = sb("actT", [KT, T])
        conv_in = sb("conv_in", [KT, CONV_K - 1 + T])
        conv_acc = sb("conv_acc", [KT, T])
        big = [sb(f"big{i}", [KT * T]) for i in range(9)]
        merge = sb("merge", [3 * KT, T])
        work = Ring([Buffer(sb(f"work{i}", [4 * T])) for i in range(4)])
        probs = Ring([Buffer(sb(f"probs{i}", [2, 384])) for i in range(2)])
        probs_t = Ring([Buffer(sb(f"probs_t{i}", [512])) for i in range(2)])
        ident = sb("ident", [P])
        ones = sb("ones", [P])
        ones64 = sb("ones64", [P])
        later = sb("later", [P])
        before = sb("before", [P])
        dist = sb("dist", [384])
        iota16 = sb("iota16", [PEER_TOPK])
        col = sb("col", [96])

        units = Ring([Buffer(ctx.enter_context(nc.psum_tensor(f"unit{i}", [P, 1024], F32)))
                      for i in range(3)])
        banks = Ring([Buffer(ctx.enter_context(nc.psum_tensor(f"bank{i}", [P, 512], F32)))
                      for i in range(2)])

        def cm(b):
            return b[:, :].rearrange("p (k t) -> p k t", k=KT)

        def tm(b):
            return b[:, :].rearrange("p (t c) -> p t c", t=TT)

        def v(name, i=0, n=1):
            at = VECTOR_AT[name][0]
            return vec[:, at + i:at + i + n]

        EPS6, EPS5, ONE, NEG_HALF = (col[:, i:i + 1] for i in range(4))
        LAM = col[:, 8:9]
        used = [12]

        def cols(n):
            used[0] += n
            return col[:, used[0] - n:used[0]]

        def load_weights(w, column):
            slot = w_ring.take()
            src = w.rearrange("(k p) n -> p k n", p=P)[:, :, column:column + SLOT]
            dst = slot.ap
            slot.ready = sp.dma(nc.sync.dma_start, dst, src, counter=slot.counter,
                                after=slot.free)
            slot.free = []
            return slot

        x_tm, mem_tm = tm(big[8]), merge[:, 0:KT, :].rearrange("p k t -> p (k t)").rearrange(
            "p (t c) -> p t c", t=TT)
        x_in = x.rearrange("(t p) c -> p t c", p=P)
        mem_in = mem.rearrange("(t p) c -> p t c", p=P)
        c_x, c_vec, c_mem = load_counter("x"), load_counter("vec"), load_counter("mem")
        x_ready = act.dma(nc.scalar.dma_start, x_tm, x_in, counter=c_x)
        vec_ready = act.dma(nc.scalar.dma_start, vec[:, :], vectors, counter=c_vec)
        mem_ready = act.dma(nc.scalar.dma_start, mem_tm, mem_in, counter=c_mem)

        s = dve.do(nc.vector.memset, col[:, :], 0.0)
        for ap, value in ((EPS6, 1e-6), (EPS5, 1e-5), (ONE, 1.0), (NEG_HALF, -0.5)):
            const_ready = dve.do(nc.vector.memset, ap, value, after=[s])
        ones_ready = dve.do(nc.vector.memset, ones[:, :], 1.0)
        s = dve.do(nc.vector.memset, ones64[:, :], 0.0)
        dve.do(nc.vector.memset, ones64[0:64, 0:64], 1.0, after=[s])
        ones64_ready = dve.do(nc.vector.memset, ones64[64:128, 64:128], 1.0, after=[s])
        conv_pad = dve.do(nc.vector.memset, conv_in[:, :, 0:CONV_K - 1], 0.0)

        s = pool.do(nc.gpsimd.memset, ident[:, :], 0.0)
        ident_ready = pool.do(nc.gpsimd.affine_select,
            out=ident[:, :], in_=ident[:, :], compare_op=ALU.not_equal, fill=1.0, base=0,
            pattern=[[-1, P]], channel_multiplier=1, after=[s])
        s = pool.do(nc.gpsimd.memset, later[:, :], 1.0)
        pool.do(nc.gpsimd.affine_select, out=later[:, :], in_=later[:, :], compare_op=ALU.is_gt,
                                          fill=0.0, base=0, pattern=[[-1, P]],
                                          channel_multiplier=1, after=[s])
        s = pool.do(nc.gpsimd.memset, before[:, :], 1.0)
        pool.do(nc.gpsimd.affine_select, out=before[:, :], in_=before[:, :], compare_op=ALU.is_gt,
                                          fill=0.0, base=0, pattern=[[1, P]],
                                          channel_multiplier=-1, after=[s])
        s = pool.do(nc.gpsimd.iota, dist[:, 0:256], [[1, 256]], base=-P, channel_multiplier=-1,
                                     allow_small_or_imprecise_dtypes=True)
        s = pool.do(nc.gpsimd.iota, dist[:, 256:384], [[1, P]], base=0, channel_multiplier=-1,
                                     allow_small_or_imprecise_dtypes=True, after=[s])
        s = pool.do(nc.gpsimd.affine_select,
            out=dist[:, 0:256], in_=dist[:, 0:256], compare_op=ALU.is_ge, fill=MASKED, base=P,
            pattern=[[-1, 256]], channel_multiplier=1, after=[s])
        s = pool.do(nc.gpsimd.affine_select,
            out=dist[:, 256:384], in_=dist[:, 256:384], compare_op=ALU.is_ge, fill=MASKED, base=0,
            pattern=[[-1, P]], channel_multiplier=1, after=[s])
        pool_consts = pool.do(nc.gpsimd.iota, iota16[:, :], [[1, PEER_TOPK]], base=0,
                                               channel_multiplier=0,
                                               allow_small_or_imprecise_dtypes=True, after=[s])

        def project_cm(slot, rhs, rhs_ready):
            unit = units.take()
            after = [slot.ready, *unit.free, *rhs_ready]
            for j in range(SLOT // P):
                for k in range(KT):
                    s = pe.do(nc.tensor.matmul,
                        unit.ap[:, j * T:(j + 1) * T], slot.ap[:, k, j * P:(j + 1) * P],
                        rhs[:, k, :], start=k == 0, stop=k == KT - 1, after=after)
                    after = []
            slot.free, unit.ready, unit.free = [s], s, []
            return unit

        def project_tm(slot, lhs, lhs_ready):
            unit = units.take()
            after = [slot.ready, *unit.free, *lhs_ready]
            for t in range(TT):
                for k in range(KT):
                    s = pe.do(nc.tensor.matmul,
                        unit.ap[:, t * SLOT:(t + 1) * SLOT], lhs[:, k, t * P:(t + 1) * P],
                        slot.ap[:, k, :], start=k == 0, stop=k == KT - 1, after=after)
                    after = []
            slot.free, unit.ready, unit.free = [s], s, []
            return unit

        def tiles4(ap):
            return ap.rearrange("p (j t) -> p j t", j=4)

        def rsqrt_of(out_ap, in_ap, mean_over, eps, after):
            s = act.do(nc.scalar.activation, out_ap, in_ap, ACT.Ln, bias=eps,
                                              scale=1.0 / mean_over, after=[*after, const_ready])
            s2 = act.do(nc.scalar.activation, out_ap, out_ap, ACT.Exp, scale=-0.5, after=[s])
            return s, s2

        def normalise_tm(src, ready, scratch):
            ss = cols(TT)
            for t in range(TT):
                s = dve.do(nc.vector.tensor_tensor_reduce,
                    out=scratch.ap[:, 0:D], in0=src[:, t, :], in1=src[:, t, :], scale=1.0,
                    scalar=0.0, op0=ALU.mult, op1=ALU.add, accum_out=ss[:, t:t + 1],
                    after=[*ready, *scratch.free, const_ready])
                scratch.free = [s]
            return ss, rsqrt_of(ss, ss, D, EPS6, [s])[1]

        def transpose_tm(src, ready, dst, dst_free, gain=None):
            done = []
            for half in range(2):
                unit = units.take()
                after = [*ready, *unit.free, ident_ready]
                for j in range(4):
                    for t in range(TT):
                        k = 4 * half + j
                        s = pe.do(nc.tensor.transpose,
                            unit.ap[:, j * T + t * P:j * T + (t + 1) * P],
                            src[:, t, k * P:(k + 1) * P], ident[:, :], after=after)
                        after = []
                unit.free = []
                for j in range(4):
                    k = 4 * half + j
                    if gain is None:
                        d = act.do(nc.scalar.copy,
                            dst[:, k, :], unit.ap[:, j * T:(j + 1) * T], after=[s, *dst_free])
                    else:
                        d = act.do(nc.scalar.activation,
                            dst[:, k, :], unit.ap[:, j * T:(j + 1) * T], ACT.Copy,
                            scale=v(gain, k), after=[s, *dst_free, vec_ready])
                unit.free = [d]
                done.append(d)
            return done

        def sum_over_channels(sq, ready, weights, groups, width, unit):
            after = [*ready, *unit.free, ones64_ready]
            for g, members in enumerate(groups):
                for i, a in enumerate(members):
                    s = pe.do(nc.tensor.matmul,
                        unit.ap[:, g * width:(g + 1) * width], weights[:, :],
                        sq[:, a * width:(a + 1) * width], start=i == 0, stop=i == len(members) - 1,
                        after=after)
                    after = []
            unit.free = []
            return s

        def to_silu(unit, dst):
            s = act.do(nc.scalar.activation, dst, tiles4(unit.ap[:, :]), ACT.Tanh, scale=0.5,
                       after=[unit.ready])
            s = dve.do(nc.vector.scalar_tensor_tensor,
                out=dst, in0=dst, scalar=1.0, in1=tiles4(unit.ap[:, :]), op0=ALU.add,
                op1=ALU.mult, after=[s])
            unit.free = [s]
            return s

        def copy_out(unit, dst, ready, engine):
            if engine is act:
                s = act.do(nc.scalar.copy, dst, unit, after=ready)
            else:
                s = dve.do(nc.vector.tensor_copy, dst, unit, after=ready)
            return s

        stage("input")
        w = w_ring.buffers[0]
        ss, s = normalise_tm(x_tm, [x_ready], work.buffers[0])
        for t in range(TT):
            s2 = dve.do(nc.vector.tensor_scalar, x_tm[:, t, :], x_tm[:, t, :],
                                                       ss[:, t:t + 1], None, ALU.mult, after=[s])
        hT_ready = transpose_tm(x_tm, [s2], actT, [], "norm_g")
        memT = merge[:, KT:2 * KT, :]
        ssm, s = normalise_tm(mem_tm, [mem_ready], work.buffers[1])
        for t in range(TT):
            s2 = dve.do(nc.vector.tensor_scalar, mem_tm[:, t, :], mem_tm[:, t, :],
                                                       ssm[:, t:t + 1], None, ALU.mult, after=[s])
        mem_norm_ready = s2

        dots = cols(2)
        for i, (a, b) in enumerate((("lambda_q1", "lambda_k1"), ("lambda_q2", "lambda_k2"))):
            junk = work.buffers[2].ap
            s = dve.do(nc.vector.tensor_tensor_reduce,
                out=junk[:, 64 * i:64 * i + 64], in0=v(a, 0, 64), in1=v(b, 0, 64), scale=1.0,
                scalar=0.0, op0=ALU.mult, op1=ALU.add, accum_out=dots[:, i:i + 1],
                after=[vec_ready])
        work.buffers[2].free = [s]
        s = act.do(nc.scalar.activation, dots, dots, ACT.Exp, after=[s])
        lam_ready = dve.do(nc.vector.scalar_tensor_tensor,
            out=LAM, in0=dots[:, 0:1], scalar=LAMBDA_INIT, in1=dots[:, 1:2], op0=ALU.add,
            op1=ALU.subtract, after=[s, const_ready])
        qg, subln_g, xq_g, q2_g = cols(1), cols(1), cols(2), cols(1)
        half_dw = vec[:, VECTOR_AT["conv_dw"][0]:VECTOR_AT["conv_dw"][0] + KT * CONV_K]
        for dst, src, by in ((qg, v("diff_qn_g"), DIFF_HEAD_DIM ** -0.5),
                             (subln_g, v("diff_subln_g"), 0.5 * (1.0 - LAMBDA_INIT)),
                             (xq_g, v("x_qn_g", 0, 2), X_HEAD_DIM ** -0.5),
                             (q2_g, v("q_norm_2"), SB_HEAD_DIM ** -0.5),
                             (half_dw, half_dw, 0.5)):
            gains_ready = dve.do(nc.vector.tensor_scalar,
                dst, src, by, None, ALU.mult, after=[vec_ready, const_ready])

        stage("glu")
        u_ready = []
        for i in range(2):
            slot_a, slot_b = load_weights(w_in, i * SLOT), load_weights(w_in, D + i * SLOT)
            ua = project_cm(slot_a, actT, hT_ready)
            ub = project_cm(slot_b, actT, [])
            th = work.take()
            s = act.do(nc.scalar.activation, th.ap[:, :], ub.ap[:, :], ACT.Tanh,
                                                            scale=0.5, after=[ub.ready, *th.free])
            ub.free = [s]
            s = dve.do(nc.vector.scalar_tensor_tensor,
                out=conv_in[:, 4 * i:4 * i + 4, CONV_K - 1:], in0=tiles4(th.ap[:, :]), scalar=1.0,
                in1=tiles4(ua.ap[:, :]), op0=ALU.add, op1=ALU.mult,
                after=[s, ua.ready, conv_pad])
            ua.free, th.free = [s], [s]
            u_ready.append(s)

        conv_done = {}

        def convolve(tiles):
            last = {}
            for k in range(CONV_K):
                for t in tiles:
                    tap = v("conv_dw", t * CONV_K + k)
                    src = conv_in[:, t, k:k + T]
                    dst = conv_acc[:, t, :]
                    if k == 0:
                        last[t] = dve.do(nc.vector.tensor_scalar,
                            dst, src, tap, v("conv_dw_b", t), ALU.mult, ALU.add,
                            after=[u_ready[t // 4], gains_ready])
                    else:
                        last[t] = dve.do(nc.vector.scalar_tensor_tensor, out=dst, in0=src, scalar=tap,
                                                                in1=dst, op0=ALU.mult,
                                                                op1=ALU.add, after=[last[t]])
            conv_done.update(last)

        def head_norm(unit, dst, weights, mean_over, gain, per_head):
            sq = work.take()
            s2 = dve.do(nc.vector.tensor_copy, dst, tiles4(unit.ap[:, :]), after=[unit.ready])
            unit.free = [s2]
            s1 = act.do(nc.scalar.activation, tiles4(sq.ap[:, :]), dst, ACT.Square,
                        after=[s2, *sq.free])
            sums = units.take()
            if per_head == 1:
                s = sum_over_channels(sq.ap, [s1], weights, [[0], [1]], 512, sums)
                n = 4 * T
            else:
                s = sum_over_channels(sq.ap, [s1], weights, [[0, 1], [2, 3]], T, sums)
                n = 2 * T
            sq.free = [s]
            rs = work.take()
            s, s3 = rsqrt_of(rs.ap[:, 0:n], sums.ap[:, 0:n], mean_over, EPS6, [s, *rs.free])
            sums.free = [s]
            if per_head == 1:
                s = dve.do(nc.vector.scalar_tensor_tensor,
                    out=dst, in0=dst, scalar=gain, in1=tiles4(rs.ap[:, :]), op0=ALU.mult,
                    op1=ALU.mult, after=[s2, s3, gains_ready])
            else:
                for j in range(per_head):
                    part = dst[:, j:4:per_head, :]
                    s = dve.do(nc.vector.scalar_tensor_tensor,
                        out=part, in0=part, scalar=gain[:, j:j + 1],
                        in1=rs.ap[:, 0:n].rearrange("p (g t) -> p g t", t=T), op0=ALU.mult,
                        op1=ALU.mult, after=[s2, s3, gains_ready])
            rs.free = [s]
            return s

        q_cm, k_cm, v_tm, dgate = cm(big[0]), cm(big[1]), tm(big[2]), cm(big[3])
        cgate, xq_cm, xk_cm, xv_tm = cm(big[4]), cm(big[5]), cm(big[6]), tm(big[7])
        COL_CGATE, COL_Q, COL_K, COL_V = 2 * D, 3 * D, 4 * D, 5 * D
        COL_DGATE, COL_XQ, COL_XGATE, COL_MERGE = 6 * D, 7 * D, 8 * D, 9 * D

        stage("diff_qkv")
        q_ready, k_ready, v_ready = [], [], []
        for i in range(2):
            unit = project_cm(load_weights(w_in, COL_Q + i * SLOT), actT, [])
            q_ready.append(head_norm(unit, q_cm[:, 4 * i:4 * i + 4, :], ones64, DIFF_HEAD_DIM,
                                     qg, 1))
            unit = project_cm(load_weights(w_in, COL_K + i * SLOT), actT, [])
            k_ready.append(head_norm(unit, k_cm[:, 4 * i:4 * i + 4, :], ones64, DIFF_HEAD_DIM,
                                     v("diff_kn_g"), 1))
            if i == 0:
                convolve((0, 1))
            unit = project_tm(load_weights(w_in, COL_V + i * SLOT), actT, [])
            s = copy_out(unit.ap[:, :].rearrange("p (t c) -> p t c", t=TT),
                         v_tm[:, :, i * SLOT:(i + 1) * SLOT], [unit.ready], act)
            unit.free = [s]
            v_ready.append(s)

        stage("diff_attention")
        o_ready = {}
        scored = {}

        def diff_scores(h):
            slope = 2.0 ** (-8.0 * (h + 1) / DIFF_HEADS)
            unit, p = units.take(), probs.take()
            after = [q_ready[h // 4], k_ready[h // 4], *unit.free]
            for m in range(2):
                rows = slice(64 * m, 64 * m + 64)
                for qt, width, at in ((1, 2 * P, 0), (0, P, 2 * P)):
                    s = pe.do(nc.tensor.matmul,
                        unit.ap[:, 512 * m + at:512 * m + at + width],
                        q_cm[rows, h, qt * P:(qt + 1) * P], k_cm[rows, h, 0:width],
                        start=True, stop=True, after=after)
                    after = []
            scores = unit.ap[:, :].rearrange("p (m c) -> p m c", m=2)[:, :, 0:384]
            s = dve.do(nc.vector.scalar_tensor_tensor,
                out=p.ap[:, :, :], in0=dist[:, :].unsqueeze(1).to_broadcast([P, 2, 384]),
                scalar=slope, in1=scores, op0=ALU.mult, op1=ALU.add,
                after=[s, *p.free, pool_consts])
            unit.free = [s]
            small = p.small
            top, total, inv, inv_lam = (small[:, i:i + 4] for i in (0, 4, 8, 12))
            wide, narrow = p.ap[:, :, 0:256], p.ap[:, :, 256:384]
            dve.do(nc.vector.tensor_reduce, top[:, 0:2], wide, AX, ALU.max, after=[s])
            s = dve.do(nc.vector.tensor_reduce, top[:, 2:4], narrow, AX, ALU.max, after=[s])
            s = dve.do(nc.vector.tensor_scalar, top, top, -1.0, None, ALU.mult, after=[s])
            for i, part in ((0, wide), (2, narrow)):
                for m in range(2):
                    e1 = act.do(nc.scalar.activation,
                        part[:, m, :], part[:, m, :], ACT.Exp, bias=top[:, i + m:i + m + 1],
                        accum_out=total[:, i + m:i + m + 1], after=[s])
            s = dve.do(nc.vector.reciprocal, inv, total, after=[e1])
            s = dve.do(nc.vector.tensor_scalar, inv_lam, inv, LAM, None, ALU.mult,
                       after=[s, lam_ready])
            for i, part in ((0, wide), (2, narrow)):
                s2 = dve.do(nc.vector.tensor_scalar,
                    part[:, 1, :], part[:, 1, :], inv_lam[:, i + 1:i + 2], None, ALU.mult,
                    after=[s])
                s3 = dve.do(nc.vector.scalar_tensor_tensor,
                    out=part[:, 0, :], in0=part[:, 0, :], scalar=inv[:, i:i + 1],
                    in1=part[:, 1, :], op0=ALU.mult, op1=ALU.subtract, after=[s2])
            scored[h] = p, s3

        def diff_turn(h):
            p, ready = scored[h]
            bank, pt = banks.take(), probs_t.take()
            after = [ready, *bank.free, ident_ready]
            for dst, src in ((0, 256), (P, 0), (2 * P, P)):
                s = pe.do(nc.tensor.transpose,
                    bank.ap[:, dst:dst + P], p.ap[:, 0, src:src + P], ident[:, :], after=after)
                after = []
            p.free = [s]
            s = act.do(nc.scalar.copy, pt.ap[:, 0:384], bank.ap[:, 0:384], after=[s, *pt.free])
            bank.free = [s]
            scored[h] = pt, s

        def diff_values(h):
            pt, ready = scored[h]
            bank = banks.take()
            vh = v_tm[:, :, h * P:(h + 1) * P]
            pe.do(nc.tensor.matmul, bank.ap[:, 0:256], vh[:, 0, :], pt.ap[:, 0:256], start=True,
                                     stop=False, after=[ready, v_ready[h // 4], *bank.free])
            s = pe.do(nc.tensor.matmul, bank.ap[:, P:256], vh[:, 1, :], pt.ap[:, 256:384],
                                         start=False, stop=True)
            pt.free = [s]
            s = dve.do(nc.vector.tensor_copy, q_cm[:, h, :], bank.ap[:, 0:256], after=[s])
            bank.free = [s]
            o_ready[h] = s

        def diff_finish(i, gate_ready):
            o = q_cm[:, 4 * i:4 * i + 4, :]
            sq = work.take()
            ready = [o_ready[h] for h in range(4 * i, 4 * i + 4)]
            s = act.do(nc.scalar.activation, tiles4(sq.ap[:, :]), o, ACT.Square,
                       after=[*ready, *sq.free])
            sums = units.take()
            s = sum_over_channels(sq.ap, [s], ones, [[0], [1]], 512, sums)
            sq.free = [s]
            rs = work.take()
            s, s3 = rsqrt_of(rs.ap[:, :], sums.ap[:, :], P, EPS6, [s, *rs.free])
            sums.free = [s]
            s = dve.do(nc.vector.scalar_tensor_tensor,
                out=o, in0=o, scalar=subln_g, in1=tiles4(rs.ap[:, :]), op0=ALU.mult,
                op1=ALU.mult, after=[*ready, s3, gains_ready])
            rs.free = [s]
            return dve.do(nc.vector.tensor_tensor, o, o, dgate[:, 4 * i:4 * i + 4, :], ALU.mult,
                          after=[s, gate_ready])

        for i, p in enumerate(probs.buffers):
            p.small = cols(16)

        gate = {}
        dg_ready, cg_ready, xg_ready, xq_ready, xk_ready, xv_ready = [], [], [], [], [], []

        diff_scores(0)
        for i in range(2):
            unit = project_cm(load_weights(w_in, COL_DGATE + i * SLOT), actT, [])
            dg_ready.append(to_silu(unit, dgate[:, 4 * i:4 * i + 4, :]))
            diff_turn(i)
            diff_scores(i + 1)
            convolve((2 + i,))
        for i in range(2):
            unit = project_cm(load_weights(w_in, COL_CGATE + i * SLOT), actT, [])
            cg_ready.append(to_silu(unit, cgate[:, 4 * i:4 * i + 4, :]))
            diff_values(i)
            diff_turn(2 + i)
            diff_scores(3 + i)
            convolve((4 + i,))
        for i in range(2):
            unit = project_cm(load_weights(w_in, COL_XQ + i * SLOT), actT, [])
            xq_ready.append(head_norm(unit, xq_cm[:, 4 * i:4 * i + 4, :], ones, X_HEAD_DIM, xq_g,
                                      2))
            diff_values(2 + i)
            diff_turn(4 + i)
            diff_scores(5 + i)
            convolve((6 + i,))
        do0 = diff_finish(0, dg_ready[0])
        memT_ready = transpose_tm(mem_tm, [mem_norm_ready], memT, [], "mem_norm_g")
        for i in range(2):
            unit = project_cm(load_weights(w_mem_kv, i * SLOT), memT, memT_ready)
            xk_ready.append(head_norm(unit, xk_cm[:, 4 * i:4 * i + 4, :], ones, X_HEAD_DIM,
                                      v("x_kn_g", 0, 2), 2))
            diff_values(4 + i)
            diff_turn(6 + i)
            if i == 0:
                diff_scores(7)
        for i in range(2):
            unit = project_tm(load_weights(w_mem_kv, D + i * SLOT), memT, [])
            s = copy_out(unit.ap[:, :].rearrange("p (t c) -> p t c", t=TT),
                         xv_tm[:, :, i * SLOT:(i + 1) * SLOT], [unit.ready], act)
            mem_used = unit.ready
            unit.free = [s]
            xv_ready.append(s)
            diff_values(6 + i)
        do1 = diff_finish(1, dg_ready[1])
        diff_out_ready = [do0, do1]

        stage("cross_attention")
        xgate = cm(big[8])

        def cross_scores(h):
            unit, p = units.take(), probs.take()
            after = [xq_ready[h // 2], xk_ready[h // 2], *unit.free]
            for qt in range(TT):
                for j in range(2):
                    s = pe.do(nc.tensor.matmul,
                        unit.ap[:, qt * T:(qt + 1) * T], xq_cm[:, 2 * h + j, qt * P:(qt + 1) * P],
                        xk_cm[:, 2 * h + j, :], start=j == 0, stop=j == 1, after=after)
                    after = []
            small = p.small
            top, total = small[:, 0:2], small[:, 4:6]
            flat = p.ap[:, :, :].rearrange("p a b -> p (a b)")[:, 0:2 * T]
            s = dve.do(nc.vector.tensor_reduce,
                top, unit.ap[:, 0:2 * T].rearrange("p (q k) -> p q k", q=2), AX, ALU.max,
                after=[s, *p.free])
            s = dve.do(nc.vector.tensor_scalar, top, top, -1.0, None, ALU.mult, after=[s])
            for qt in range(TT):
                e1 = act.do(nc.scalar.activation,
                    flat[:, qt * T:(qt + 1) * T], unit.ap[:, qt * T:(qt + 1) * T], ACT.Exp,
                    bias=top[:, qt:qt + 1], accum_out=total[:, qt:qt + 1], after=[s])
            unit.free = [e1]
            s = dve.do(nc.vector.reciprocal, total, total, after=[e1])
            for qt in range(TT):
                s2 = dve.do(nc.vector.tensor_scalar,
                    flat[:, qt * T:(qt + 1) * T], flat[:, qt * T:(qt + 1) * T],
                    total[:, qt:qt + 1], 0.5, ALU.mult, ALU.mult, after=[s])
            scored["x", h] = p, flat, s2

        def cross_turn(h):
            p, flat, ready = scored["x", h]
            bank, pt = banks.take(), probs_t.take()
            after = [ready, *bank.free]
            for kt in range(2):
                for qt in range(TT):
                    s = pe.do(nc.tensor.transpose,
                        bank.ap[:, kt * T + qt * P:kt * T + (qt + 1) * P],
                        flat[:, qt * T + kt * P:qt * T + (kt + 1) * P], ident[:, :], after=after)
                    after = []
            p.free = [s]
            s = act.do(nc.scalar.copy, pt.ap[:, :], bank.ap[:, :], after=[s, *pt.free])
            bank.free = [s]
            scored["x", h] = pt, s

        def cross_values(h):
            pt, ready = scored["x", h]
            bank = banks.take()
            after = [ready, xv_ready[h // 2], *bank.free]
            for j in range(2):
                for kt in range(2):
                    s = pe.do(nc.tensor.matmul,
                        bank.ap[:, j * T:(j + 1) * T],
                        xv_tm[:, kt, (2 * h + j) * P:(2 * h + j + 1) * P],
                        pt.ap[:, kt * T:(kt + 1) * T], start=kt == 0, stop=kt == 1, after=after)
                    after = []
            pt.free = [s]
            dst = xgate[:, 2 * h:2 * h + 2, :]
            s = dve.do(nc.vector.tensor_tensor,
                dst, dst, bank.ap[:, :].rearrange("p (j t) -> p j t", j=2), ALU.mult,
                after=[s, xg_ready[h // 2]])
            bank.free = [s]
            return s

        cross_scores(0)
        for i in range(2):
            unit = project_cm(load_weights(w_in, COL_XGATE + i * SLOT), actT, [])
            xg_ready.append(to_silu(unit, xgate[:, 4 * i:4 * i + 4, :]))
            cross_turn(i)
            cross_scores(i + 1)

        stage("conv_norm")
        rows, rs_row = cols(1), None
        unit = units.take()
        s = None
        after = [*conv_done.values(), *unit.free, ones_ready]
        for k in range(KT):
            s = pe.do(nc.tensor.matmul,
                unit.ap[:, 0:T], ones[:, :], conv_acc[:, k, :], start=k == 0, stop=k == KT - 1,
                after=after)
            after = []
        mean = work.take()
        s = act.do(nc.scalar.activation,
            mean.ap[:, 0:T], unit.ap[:, 0:T], ACT.Copy, scale=1.0 / D, after=[s, *mean.free])
        unit.free = [s]
        centred = dve.do(nc.vector.tensor_tensor,
            conv_acc[:, :, :], conv_acc[:, :, :],
            mean.ap[:, 0:T].unsqueeze(1).to_broadcast([P, KT, T]), ALU.subtract, after=[s])
        mean.free = [centred]
        merge_free = [mem_used]
        merge_ready = {}

        def merge_slot(i):
            unit = project_cm(load_weights(w_in, COL_MERGE + i * SLOT), actT, [])
            s = act.do(nc.scalar.activation, merge[:, 4 * i:4 * i + 4, :],
                                              tiles4(unit.ap[:, :]), ACT.Tanh, scale=0.5,
                       after=[unit.ready, *merge_free])
            unit.free = [s]
            merge_ready[i] = s

        merge_slot(0)
        unit = units.take()
        after = [*unit.free]
        for half in range(2):
            sq = work.take()
            s = act.do(nc.scalar.activation,
                tiles4(sq.ap[:, :]), conv_acc[:, 4 * half:4 * half + 4, :], ACT.Square,
                after=[centred, *sq.free])
            after.append(s)
            for k in range(4):
                s = pe.do(nc.tensor.matmul,
                    unit.ap[:, 0:T], ones[:, :], sq.ap[:, k * T:(k + 1) * T],
                    start=half == 0 and k == 0, stop=half == 1 and k == 3, after=after)
                after = []
            sq.free = [s]
        rs = work.take()
        s, s3 = rsqrt_of(rs.ap[:, 0:T], unit.ap[:, 0:T], D, EPS5, [s, *rs.free])
        unit.free = [s]
        conv_out_ready = []
        for half in range(2):
            part = conv_acc[:, 4 * half:4 * half + 4, :]
            z = work.take()
            for j in range(4):
                k = 4 * half + j
                s = dve.do(nc.vector.scalar_tensor_tensor,
                    out=conv_acc[:, k, :], in0=conv_acc[:, k, :], scalar=v("conv_ln_g", k),
                    in1=rs.ap[:, 0:T], op0=ALU.mult, op1=ALU.mult, after=[s3, centred])
                s = dve.do(nc.vector.tensor_scalar,
                    conv_acc[:, k, :], conv_acc[:, k, :], v("conv_ln_b", k), 0.25, ALU.add,
                    ALU.mult, after=[s])
            s2 = act.do(nc.scalar.activation,
                tiles4(z.ap[:, :]), part, ACT.Tanh, scale=2.0, after=[s, *z.free])
            s2 = dve.do(nc.vector.scalar_tensor_tensor,
                out=part, in0=tiles4(z.ap[:, :]), scalar=1.0, in1=part, op0=ALU.add,
                op1=ALU.mult, after=[s2])
            z.free = [s2]
            gpart = cgate[:, 4 * half:4 * half + 4, :]
            conv_out_ready.append(dve.do(nc.vector.tensor_tensor,
                part, part, gpart, ALU.mult, after=[s2, cg_ready[half]]))
        rs.free = [s]

        merge_slot(1)
        cross_ready = [cross_values(0)]
        cross_turn(2)
        cross_scores(3)
        merge_slot(2)
        cross_ready.append(cross_values(1))
        cross_turn(3)
        merge_slot(3)
        cross_ready.append(cross_values(2))
        merge_slot(4)
        cross_ready.append(cross_values(3))
        merge_slot(5)

        stage("branches")
        y_cm = cm(big[1])
        x_res = tm(big[2])
        res_ready = sp.dma(nc.sync.dma_start, x_res, x_in, counter=c_x, after=[o_ready[7]])
        y_last = {}
        for branch, (w, src, ready) in enumerate(((w_conv_proj, conv_acc, conv_out_ready),
                                                  (w_diff_proj, q_cm, diff_out_ready),
                                                  (w_x_proj, xgate, cross_ready))):
            for i in range(2):
                unit = project_cm(load_weights(w, i * SLOT), src, ready)
                gates = merge[:, branch * KT + 4 * i:branch * KT + 4 * i + 4, :]
                part = y_cm[:, 4 * i:4 * i + 4, :]
                dst = work.take() if branch else None
                target = tiles4(dst.ap[:, :]) if branch else part
                s = dve.do(nc.vector.scalar_tensor_tensor, out=target, in0=gates, scalar=1.0,
                                                  in1=tiles4(unit.ap[:, :]), op0=ALU.add,
                                                  op1=ALU.mult,
                           after=[unit.ready, merge_ready[2 * branch + i], scored_all(o_ready),
                                  *(dst.free if dst else [])])
                unit.free = [s]
                if branch:
                    s = dve.do(nc.vector.tensor_tensor,
                        part, part, target, ALU.add, after=[s, y_last[i]])
                    dst.free = [s]
                y_last[i] = s

        stage("block1_out")
        for i in range(2):
            unit = project_tm(load_weights(w_out, i * SLOT), y_cm, list(y_last.values()))
            part = x_res[:, :, i * SLOT:(i + 1) * SLOT]
            s = dve.do(nc.vector.scalar_tensor_tensor,
                out=part, in0=unit.ap[:, :].rearrange("p (t c) -> p t c", t=TT), scalar=0.5,
                in1=part, op0=ALU.mult, op1=ALU.add, after=[unit.ready, res_ready])
            unit.free = [s]
        x1_ready = s

        stage("block2_input")
        xn = tm(big[3])
        junk = work.take()
        ss, s = normalise_tm(x_res, [x1_ready], junk)
        for t in range(TT):
            s2 = dve.do(nc.vector.tensor_scalar, xn[:, t, :], x_res[:, t, :],
                                                       ss[:, t:t + 1], None, ALU.mult, after=[s])
        hT_ready = transpose_tm(xn, [s2], actT, [merge_ready[5]], "norm_mix_2")

        gates_w = merge[:, 0:KT, :].rearrange("p k t -> p (k t)")
        bd = [gates_w[:, i * 512:(i + 1) * 512].rearrange("p (t j) -> p t j", t=4)
              for i in range(2)]
        keys = merge[:, KT:2 * KT, :].rearrange("p k t -> p (k t)").rearrange(
            "p (s n) -> p s n", s=PEER_SIDES)
        ffn_gain = merge[:, 2 * KT:2 * KT + 4, :].rearrange("p k t -> p (k t)")
        c_small = load_counter("block2_small")
        bd_zero = dve.do(nc.vector.memset, gates_w[:, 0:1024], 0.0, after=[y_last[1]])
        bd_ready = []
        for i, w in enumerate((rg_w_a, rg_w_x)):
            for b in range(2):
                src = w.rearrange("(t b) i j -> b i t j", b=2)[b]
                dst = bd[i][64 * b:64 * b + 64, :, 64 * b:64 * b + 64]
                bd_ready.append(act.dma(nc.scalar.dma_start, dst, src,
                                        counter=load_counter(f"rg{i}{b}"), after=[bd_zero]))
        keys_ready = act.dma(nc.scalar.dma_start, keys, sub_keys_t, counter=c_small, after=[y_last[1]])
        ffn_gain_ready = act.dma(nc.scalar.dma_start, ffn_gain, norm_ffn,
                                 counter=load_counter("ffn_gain"), after=[y_last[1]])

        stage("rg_lambda")
        lam_v = v("rg_lambda_2", 0, RG_TILES)
        u, z, z2, acc, neg4sp = (cols(RG_TILES) for _ in range(5))
        s = act.do(nc.scalar.activation, u, lam_v, ACT.Abs, after=[vec_ready])
        s = act.do(nc.scalar.activation, u, u, ACT.Exp, scale=-1.0, after=[s])
        s2 = dve.do(nc.vector.tensor_scalar, z, u, 2.0, None, ALU.add, after=[s])
        s2 = dve.do(nc.vector.reciprocal, z, z, after=[s2])
        s2 = dve.do(nc.vector.tensor_tensor, z, z, u, ALU.mult, after=[s2])
        s2 = dve.do(nc.vector.tensor_tensor, z2, z, z, ALU.mult, after=[s2])
        s2 = dve.do(nc.vector.tensor_scalar, acc, z2, 1.0 / 17, None, ALU.mult, after=[s2])
        for n in (15, 13, 11, 9, 7, 5, 3):
            s2 = dve.do(nc.vector.scalar_tensor_tensor,
                out=acc, in0=acc, scalar=1.0 / n, in1=z2, op0=ALU.add, op1=ALU.mult, after=[s2])
        s2 = dve.do(nc.vector.scalar_tensor_tensor, out=acc, in0=acc, scalar=1.0, in1=z,
                                                     op0=ALU.add, op1=ALU.mult, after=[s2])
        s3 = dve.do(nc.vector.tensor_scalar, u, lam_v, 0.0, 4.0, ALU.min, ALU.mult, after=[s2])
        sp_ready = dve.do(nc.vector.scalar_tensor_tensor,
            out=neg4sp, in0=acc, scalar=-8.0, in1=u, op0=ALU.mult, op1=ALU.add, after=[s3])
        half_ba, half_bx = cols(RG_TILES), cols(RG_TILES)
        dve.do(nc.vector.tensor_scalar, half_ba, v("rg_b_a_2", 0, RG_TILES), 0.5, None,
                                         ALU.mult, after=[vec_ready])
        rg_bias_ready = dve.do(nc.vector.tensor_scalar,
            half_bx, v("rg_b_x_2", 0, RG_TILES), 0.5, None, ALU.mult, after=[vec_ready])

        stage("rg_in")
        xr = conv_in[:, 0:RG_TILES, 0:RG_WIDTH - 1 + T]
        xc = big[4][:, 0:4 * T].rearrange("p (j t) -> p j t", j=4)
        decay = big[4][:, 4 * T:8 * T].rearrange("p (j t) -> p j t", j=4)
        drive = big[5][:, 0:4 * T].rearrange("p (j t) -> p j t", j=4)
        geluT = big[5][:, 4 * T:8 * T].rearrange("p (j t) -> p j t", j=4)
        gate_r = big[6][:, 0:4 * T].rearrange("p (j t) -> p j t", j=4)
        gate_i = big[6][:, 4 * T:8 * T].rearrange("p (j t) -> p j t", j=4)
        mixed = cm(big[7])
        unit = project_cm(load_weights(w_in_2, 3 * D_SB), actT, hT_ready)
        pad = dve.do(nc.vector.memset, xr[:, :, 0:RG_WIDTH - 1], 0.0, after=[*conv_done.values()])
        s = act.do(nc.scalar.copy, xr[:, :, RG_WIDTH - 1:], tiles4(unit.ap[:, :]),
                   after=[unit.ready])
        unit.free = [s]
        xr_ready = s
        last = {}
        for k in range(RG_WIDTH):
            for j in range(RG_TILES):
                tap = v("conv_w_2", j * RG_WIDTH + k)
                src, dst = xr[:, j, k:k + T], xc[:, j, :]
                if k == 0:
                    last[j] = dve.do(nc.vector.tensor_scalar,
                        dst, src, tap, v("conv_b_2", j), ALU.mult, ALU.add,
                        after=[xr_ready, pad])
                else:
                    last[j] = dve.do(nc.vector.scalar_tensor_tensor,
                        out=dst, in0=src, scalar=tap, in1=dst, op0=ALU.mult, op1=ALU.add,
                        after=[last[j]])
        xc_ready = list(last.values())
        q2_cm = big[0][:, 0:4 * T].rearrange("p (j t) -> p j t", j=4)
        k2_cm = big[0][:, 4 * T:8 * T].rearrange("p (j t) -> p j t", j=4)
        v2_tm = big[1][:, 0:2 * D_SB].rearrange("p (t c) -> p t c", t=TT)

        stage("sb_qkv")
        unit = project_cm(load_weights(w_in_2, 0), actT, [])
        q2_ready = head_norm(unit, q2_cm, ones64, SB_HEAD_DIM, q2_g, 1)
        unit = project_cm(load_weights(w_in_2, D_SB), actT, [])
        k2_ready = head_norm(unit, k2_cm, ones64, SB_HEAD_DIM, v("k_norm_2"), 1)

        stage("rg_gates")
        gate_units = []
        for i in range(2):
            unit = units.take()
            after = [*unit.free, *xc_ready, *bd_ready]
            for j in range(RG_TILES):
                s = pe.do(nc.tensor.matmul,
                    unit.ap[:, j * T:(j + 1) * T], bd[i][:, j, :], xc[:, j, :], start=True,
                    stop=True, after=after)
                after = []
            dst, bias = ((gate_r, half_ba), (gate_i, half_bx))[i]
            for j in range(RG_TILES):
                g = act.do(nc.scalar.activation,
                    dst[:, j, :], unit.ap[:, j * T:(j + 1) * T], ACT.Tanh, scale=0.5,
                    bias=bias[:, j:j + 1], after=[s, rg_bias_ready])
            unit.free = [g]
            gate_units.append(g)
        for j in range(RG_TILES):
            s = act.do(nc.scalar.activation,
                decay[:, j, :], gate_r[:, j, :], ACT.Exp, scale=neg4sp[:, j:j + 1],
                bias=neg4sp[:, j:j + 1], after=[gate_units[0], sp_ready])
            s = act.do(nc.scalar.activation,
                gate_r[:, j, :], gate_r[:, j, :], ACT.Tanh, scale=neg4sp[:, j:j + 1],
                bias=neg4sp[:, j:j + 1], after=[s])
        s2 = dve.do(nc.vector.tensor_tensor, drive, decay, decay, ALU.mult, after=[s])
        s2 = dve.do(nc.vector.scalar_tensor_tensor, out=gate_r, in0=drive, scalar=1.0,
                                                     in1=gate_r, op0=ALU.add, op1=ALU.mult,
                    after=[s2])
        s2 = dve.do(nc.vector.tensor_scalar, gate_r, gate_r, -1.0, 1e-19, ALU.mult, ALU.max,
                    after=[s2])
        s = act.do(nc.scalar.activation, gate_r, gate_r, ACT.Ln, after=[s2])
        s = act.do(nc.scalar.activation, gate_r, gate_r, ACT.Exp, scale=0.5, after=[s])
        s2 = dve.do(nc.vector.scalar_tensor_tensor, out=drive, in0=gate_i, scalar=1.0, in1=xc,
                                                     op0=ALU.add, op1=ALU.mult,
                    after=[s2, gate_units[1], *xc_ready])
        s2 = dve.do(nc.vector.scalar_tensor_tensor, out=drive, in0=drive, scalar=0.5,
                                                     in1=gate_r, op0=ALU.mult, op1=ALU.mult,
                    after=[s2, s])
        for j in range(RG_TILES):
            s2_ = dve.do(nc.vector.tensor_tensor_scan,
                mixed[:, 4 + j, :], decay[:, j, :], drive[:, j, :], 0.0, ALU.mult, ALU.add,
                after=[s2])
        scan_ready = s2_

        stage("sb_attention")
        pairs = SB_HEADS // 2
        unit = project_tm(load_weights(w_in_2, 2 * D_SB), actT, [])
        s = copy_out(unit.ap[:, :].rearrange("p (t c) -> p t c", t=TT), v2_tm, [unit.ready], act)
        unit.free = [s]
        v2_ready = s
        unit = project_cm(load_weights(w_in_2, 3 * D_SB + D_RG), actT, [])
        s = act.do(nc.scalar.activation, geluT, tiles4(unit.ap[:, :]),
                                                     ACT.Gelu_apprx_tanh, after=[unit.ready])
        unit.free = [s]
        rg_ready = dve.do(nc.vector.tensor_tensor, mixed[:, 4:8, :], mixed[:, 4:8, :], geluT,
                                                    ALU.mult, after=[s, scan_ready])
        sb_state = {}
        lb_space = [big[3][:, i * 1024:i * 1024 + 768].rearrange("p (a c) -> p a c", a=2)
                    for i in range(2)]
        lb_ring = Ring([Buffer(a) for a in lb_space])
        for b in lb_ring.buffers:
            b.free = hT_ready

        def sb_logits(i):
            unit, lo, lb = units.take(), probs.take(), lb_ring.take()
            after = [q2_ready, k2_ready, *unit.free]
            for m in range(2):
                rows = slice(64 * m, 64 * m + 64)
                for kt, q0, at in ((0, 0, 0), (1, P, 2 * P)):
                    s = pe.do(nc.tensor.matmul,
                        unit.ap[:, 512 * m + at:512 * m + at + T - q0],
                        k2_cm[rows, i, kt * P:(kt + 1) * P], q2_cm[rows, i, q0:T],
                        start=True, stop=True, after=after)
                    after = []
            z = unit.ap[:, :].rearrange("p (m c) -> p m c", m=2)[:, :, 0:384]
            lo_ap, lb_ap = lo.ap[:, :, :], lb.ap
            s = act.do(nc.scalar.activation, lo_ap, z, ACT.Abs, after=[s, *lo.free])
            s = act.do(nc.scalar.activation, lo_ap, lo_ap, ACT.Exp, scale=-1.0, after=[s])
            s = act.do(nc.scalar.activation, lo_ap, lo_ap, ACT.Ln, bias=ONE, after=[s])
            s = dve.do(nc.vector.scalar_tensor_tensor, out=lb_ap, in0=z, scalar=0.0, in1=lo_ap,
                                                        op0=ALU.min, op1=ALU.subtract,
                       after=[s, *lb.free])
            s = dve.do(nc.vector.tensor_tensor, lo_ap, lb_ap, z, ALU.subtract, after=[s])
            unit.free = [s]
            mask = before[:, :].unsqueeze(1).to_broadcast([P, 2, P])
            for at in (0, 2 * P):
                s2 = dve.do(nc.vector.tensor_tensor,
                    lo_ap[:, :, at:at + P], lo_ap[:, :, at:at + P], mask, ALU.mult, after=[s])
            sb_state[i] = lo, lb, s2

        def sb_weights(i):
            lo, lb, ready = sb_state[i]
            unit = units.take()
            after = [ready, *unit.free]
            for m in range(2):
                at = 512 * m
                for dst, w, src, n, start, stop in ((0, later, 0, T, True, False),
                                                    (P, ones, 2 * P, P, False, True),
                                                    (2 * P, later, 2 * P, P, True, True)):
                    s = pe.do(nc.tensor.matmul, unit.ap[:, at + dst:at + dst + n], w[:, :],
                                                  lo.ap[:, m, src:src + n], start=start,
                                                  stop=stop, after=after)
                    after = []
            lo.free = [s]
            suffix = unit.ap[:, :].rearrange("p (m c) -> p m c", m=2)[:, :, 0:384]
            lb_ap = lb.ap
            s = dve.do(nc.vector.tensor_tensor, lb_ap, lb_ap, suffix, ALU.add, after=[s])
            unit.free = [s]
            s = act.do(nc.scalar.activation, lb_ap, lb_ap, ACT.Exp, after=[s])
            mask = before[:, :].unsqueeze(1).to_broadcast([P, 2, P])
            for at in (0, 2 * P):
                s2 = dve.do(nc.vector.tensor_tensor,
                    lb_ap[:, :, at:at + P], lb_ap[:, :, at:at + P], mask, ALU.mult, after=[s])
            sb_state[i] = lb, s2

        def sb_values(i):
            lb, ready = sb_state[i]
            bank = banks.take()
            after = [ready, v2_ready, *bank.free]
            for m in range(2):
                rows = slice(64 * m, 64 * m + 64)
                h = 2 * i + m
                pe.do(nc.tensor.matmul,
                    bank.ap[rows, 0:T], v2_tm[:, 0, h * 64:(h + 1) * 64], lb.ap[:, m, 0:T],
                    start=True, stop=False, after=after)
                after = []
                s = pe.do(nc.tensor.matmul,
                    bank.ap[rows, P:T], v2_tm[:, 1, h * 64:(h + 1) * 64],
                    lb.ap[:, m, 2 * P:3 * P], start=False, stop=True)
            lb.free = [s]
            s = act.do(nc.scalar.copy, mixed[:, i, :], bank.ap[:, 0:T], after=[s])
            bank.free = [s]
            return s

        sb_logits(0)
        sb_logits(1)
        sb_weights(0)
        sb_out = []
        for i in range(pairs):
            if i + 1 < pairs:
                sb_weights(i + 1)
            sb_out.append(sb_values(i))
            if i + 2 < pairs:
                sb_logits(i + 2)

        stage("mix")
        mixed_ready = []
        for half, gain, ready in ((1, "out_norm_rg_2", [rg_ready]), (0, "out_norm_sb_2", sb_out)):
            o = mixed[:, 4 * half:4 * half + 4, :]
            sq = work.take()
            s = act.do(nc.scalar.activation, tiles4(sq.ap[:, :]), o, ACT.Square,
                       after=[*ready, *sq.free])
            unit = units.take()
            s = sum_over_channels(sq.ap, [s], ones, [[0, 1, 2, 3]], T, unit)
            sq.free = [s]
            rs = work.take()
            s, s3 = rsqrt_of(rs.ap[:, 0:T], unit.ap[:, 0:T], D_SB, EPS6, [s, *rs.free])
            unit.free = [s]
            for j in range(4):
                s = dve.do(nc.vector.scalar_tensor_tensor,
                    out=o[:, j, :], in0=o[:, j, :], scalar=v(gain, j), in1=rs.ap[:, 0:T],
                    op0=ALU.mult, op1=ALU.mult, after=[s3, *ready])
            rs.free = [s]
            mixed_ready.append(s)
        for i in range(2):
            unit = project_tm(load_weights(w_out_2, i * SLOT), mixed, mixed_ready)
            part = x_res[:, :, i * SLOT:(i + 1) * SLOT]
            s = dve.do(nc.vector.tensor_tensor,
                part, unit.ap[:, :].rearrange("p (t c) -> p t c", t=TT), part, ALU.add,
                after=[unit.ready])
            unit.free = [s]
        x2_ready = s

        stage("peer_queries")
        h3 = tm(big[3])
        junk = work.take()
        ss, s = normalise_tm(x_res, [x2_ready], junk)
        for t in range(TT):
            h3_ready = dve.do(nc.vector.scalar_tensor_tensor,
                out=h3[:, t, :], in0=x_res[:, t, :], scalar=ss[:, t:t + 1], in1=ffn_gain,
                op0=ALU.mult, op1=ALU.mult, after=[s, ffn_gain_ready, *lb_ring.buffers[0].free,
                                                    *lb_ring.buffers[1].free])
        hT_ready = transpose_tm(h3, [h3_ready], actT, [])
        pq = [cm(big[0]), cm(big[1])]
        pq_ready = []
        for i in range(4):
            unit = project_cm(load_weights(w_query, i * SLOT), actT, hT_ready)
            dst = pq[i // 2][:, 4 * (i % 2):4 * (i % 2) + 4, :]
            s = copy_out(tiles4(unit.ap[:, :]), dst, [unit.ready], act)
            unit.free = [s]
            pq_ready.append(s)
        queries_done = unit.ready

        scores = big[4][:, :].rearrange("p (s n) -> p s n", s=PEER_SIDES)
        cand = big[5][:, :]
        onehot = big[6][:, :]
        small = big[7][:, :]
        top_s = small[:, 0:256].rearrange("p (s k) -> p s k", s=PEER_SIDES)
        top_i = small[:, 256:512].bitcast(U32).rearrange("p (s k) -> p s k", s=PEER_SIDES)
        top_f = small[:, 512:768].rearrange("p (s k) -> p s k", s=PEER_SIDES)
        best = small[:, 768:896].rearrange("p (h k) -> p h k", h=PEER_HEADS)
        pos = small[:, 896:1024].bitcast(U32).rearrange("p (h k) -> p h k", h=PEER_HEADS)
        part_i = small[:, 1024:1152].bitcast(U32)
        part_f = small[:, 1152:1280]
        row_f = small[:, 1280:1408]
        col_f = small[:, 1408:1536]
        sel = big[8]
        expert = [sel[:, t * 128:(t + 1) * 128].bitcast(U32) for t in range(TT)]
        weight = [sel[:, 256 + t * 128:256 + (t + 1) * 128] for t in range(TT)]
        dot = [sel[:, 512 + t * 128:512 + (t + 1) * 128] for t in range(TT)]
        coef = [sel[:, 768 + t * 128:768 + (t + 1) * 128] for t in range(TT)]
        total = [sel[:, 1024 + t * 8:1024 + (t + 1) * 8] for t in range(TT)]

        def top16(values, out_s, out_i, after):
            s = dve.do(nc.vector.max, out_s[:, 0:8], values, after=after)
            s = dve.do(nc.vector.max_index, out_i[:, 0:8], out_s[:, 0:8], values, after=[s])
            s = dve.do(nc.vector.match_replace, values, out_s[:, 0:8], values, -3.0e38,
                       after=[s])
            s = dve.do(nc.vector.max, out_s[:, 8:16], values, after=[s])
            return dve.do(nc.vector.max_index, out_i[:, 8:16], out_s[:, 8:16], values,
                          after=[s])

        def choose(t, before_steps):
            done = []
            for half in range(2):
                unit = units.take()
                after = [*unit.free, *pq_ready, keys_ready]
                for j in range(8):
                    side = 8 * half + j
                    s = pe.do(nc.tensor.matmul,
                        unit.ap[:, j * P:(j + 1) * P],
                        pq[side // 8][:, side % 8, t * P:(t + 1) * P], keys[:, side, :],
                        start=True, stop=True, after=after)
                    after = []
                s = act.do(nc.scalar.copy,
                    scores[:, 8 * half:8 * half + 8, :],
                    unit.ap[:, :].rearrange("p (s n) -> p s n", s=8), after=[s, *before_steps])
                unit.free = [s]
                done.append(s)
            for side in range(PEER_SIDES):
                s = top16(scores[:, side, :], top_s[:, side, :], top_i[:, side, :],
                          [done[side // 8], *before_steps])
            s = dve.do(nc.vector.tensor_copy, top_f, top_i, after=[s])
            pairs4 = cand.rearrange("p (h i j) -> p h i j", h=PEER_HEADS, i=PEER_TOPK)
            first = top_s[:, 0:PEER_SIDES:2, :].unsqueeze(3).to_broadcast(
                [P, PEER_HEADS, PEER_TOPK, PEER_TOPK])
            second = top_s[:, 1:PEER_SIDES:2, :].unsqueeze(2).to_broadcast(
                [P, PEER_HEADS, PEER_TOPK, PEER_TOPK])
            s = dve.do(nc.vector.tensor_tensor, pairs4, first, second, ALU.add, after=[s])
            by_head = cand.rearrange("p (h c) -> p h c", h=PEER_HEADS)
            for h in range(PEER_HEADS):
                s1 = top16(by_head[:, h, :], best[:, h, :], pos[:, h, :], [s])
            w3 = weight[t].rearrange("p (h k) -> p h k", h=PEER_HEADS)
            s = dve.do(nc.vector.tensor_tensor,
                w3, best, best[:, :, 0:1].to_broadcast([P, PEER_HEADS, PEER_TOPK]),
                ALU.subtract, after=[s1])
            s_exp = act.do(nc.scalar.activation, w3, w3, ACT.Exp, after=[s])
            flat_pos = pos.rearrange("p h k -> p (h k)")
            hot = onehot.rearrange("p (h k c) -> p h k c", h=PEER_HEADS, k=PEER_TOPK)
            hot3 = onehot.rearrange("p (n c) -> p n c", c=PEER_TOPK)
            for side, (op, by), found in ((0, (ALU.logical_shift_right, 4), row_f),
                                          (1, (ALU.bitwise_and, PEER_TOPK - 1), col_f)):
                s = dve.do(nc.vector.tensor_scalar, part_i, flat_pos, by, None,
                                                                   op, after=[s])
                s = dve.do(nc.vector.tensor_copy, part_f, part_i, after=[s])
                s = dve.do(nc.vector.tensor_tensor,
                    hot3, iota16[:, :].unsqueeze(1).to_broadcast([P, PICKS, PEER_TOPK]),
                    part_f.unsqueeze(2).to_broadcast([P, PICKS, PEER_TOPK]), ALU.is_equal,
                    after=[s])
                table = top_f[:, side:PEER_SIDES:2, :].unsqueeze(2).to_broadcast(
                    [P, PEER_HEADS, PEER_TOPK, PEER_TOPK])
                s = dve.do(nc.vector.tensor_tensor, hot, hot, table, ALU.mult,
                           after=[s])
                s = dve.do(nc.vector.tensor_reduce, found, hot3, AX, ALU.add,
                           after=[s])
            picked = dve.do(nc.vector.scalar_tensor_tensor,
                out=expert[t], in0=row_f, scalar=float(PEER_KEYS), in1=col_f, op0=ALU.mult,
                op1=ALU.add, after=[s])
            s = dve.do(nc.vector.tensor_reduce, total[t], w3, AX, ALU.add, after=[s_exp])
            s = dve.do(nc.vector.reciprocal, total[t], total[t], after=[s])
            s = dve.do(nc.vector.tensor_tensor,
                w3, w3, total[t].unsqueeze(2).to_broadcast([P, PEER_HEADS, PEER_TOPK]),
                ALU.mult, after=[s])
            return picked, s

        uv = Ring([Buffer(w_space[:, i * 2 * D:(i + 1) * 2 * D], load_counter(f"uv{i}"))
                   for i in range(UV_RING)])
        for b in uv.buffers:
            b.free = [queries_done]
        diag = Ring([Buffer(actT[:, i // 2, (i % 2) * P:(i % 2 + 1) * P]) for i in range(8)])
        for b in diag.buffers:
            b.free = [queries_done]
        out_tm = out.rearrange("(t p) c -> p t c", p=P)
        c_out = load_counter("out")
        GROUP = 2

        def retrieve(t, picked, weights_ready):
            unit = units.take()
            pending = []

            def flush():
                n0 = pending[0][0]
                n1 = pending[-1][0] + 1
                g = act.do(nc.scalar.activation,
                    coef[t][:, n0:n1], dot[t][:, n0:n1], ACT.Gelu_apprx_tanh,
                    after=[pending[-1][2]])
                c = dve.do(nc.vector.tensor_tensor,
                    coef[t][:, n0:n1], coef[t][:, n0:n1], weight[t][:, n0:n1], ALU.mult,
                    after=[g, weights_ready])
                for n, slot, _ in pending:
                    d = diag.take()
                    s = act.do(nc.scalar.activation,
                        d.ap, ident[:, :], ACT.Copy, scale=coef[t][:, n:n + 1],
                        after=[c, *d.free])
                    after = [s, *unit.free]
                    for half in range(2):
                        m = pe.do(nc.tensor.matmul,
                            unit.ap[:, half * 512:(half + 1) * 512], d.ap,
                            slot.ap[:, D + half * 512:D + (half + 1) * 512], start=n == 0,
                            stop=n == PICKS - 1, after=after)
                        after = []
                    d.free, slot.free = [m], [m]
                    last[0] = m
                pending.clear()

            last = [None]
            held = []
            for n in range(PICKS):
                slot = uv.take()
                index = expert[t][:, n:n + 1]
                ready = pool.dma(nc.gpsimd.indirect_dma_start,
                    out=slot.ap, out_offset=None, in_=experts,
                    in_offset=bass.IndirectOffsetOnAxis(ap=index, axis=0), counter=slot.counter,
                    after=[picked, *slot.free])
                junk = work.buffers[n % 2]
                s = dve.do(nc.vector.tensor_tensor_reduce,
                    out=junk.ap[:, 0:D], in0=h3[:, t, :], in1=slot.ap[:, 0:D], scale=1.0,
                    scalar=0.0, op0=ALU.mult, op1=ALU.add, accum_out=dot[t][:, n:n + 1],
                    after=[ready, h3_ready, *junk.free])
                junk.free = [s]
                held.append((n, slot, s))
                if len(held) == 2 * GROUP:
                    pending.extend(held[:GROUP])
                    del held[:GROUP]
                    flush()
            while held:
                pending.extend(held[:GROUP])
                del held[:GROUP]
                flush()
            y = x_res[:, t, :]
            s = dve.do(nc.vector.tensor_tensor, y, unit.ap[:, :], y, ALU.add, after=[last[0]])
            unit.free = [s]
            sp.dma(nc.sync.dma_start, out_tm[:, t, :], y, counter=c_out, after=[s])

        stage("choose0")
        picked0, weights0 = choose(0, [sp_ready])
        stage("choose1")
        picked1, weights1 = choose(1, [picked0])
        stage("retrieve0")
        retrieve(0, picked0, weights0)
        stage("retrieve1")
        retrieve(1, picked1, weights1)

        queues = (pe, act, dve, pool, sp)
        for q in queues:
            q.number()
        with nc.Block() as block:
            @block.tensor
            def _(e):
                pe.emit(e)

            @block.scalar
            def _(e):
                act.emit(e)

            @block.vector
            def _(e):
                dve.emit(e)

            @block.gpsimd
            def _(e):
                pool.emit(e)

            @block.sync
            def _(e):
                sp.emit(e)
                e.wait_ge(c_out.sem, c_out.value)


def scored_all(o_ready):
    return o_ready[max(o_ready)]


def kernel(**inputs):
    import numpy as np
    import concourse.bacc as bacc
    from concourse.bass_utils import run_bass_kernel_spmd

    a = {n: np.asarray(x) for n, x in inputs.items()}

    def per_channel(name):
        return a[name].reshape(-1, P).T

    def halves(name):
        return np.concatenate([a[name].reshape(64, 1)] * 2, axis=0)

    def on_all(name):
        return np.broadcast_to(a[name].reshape(1, -1), (P, 64))

    def taps(name):
        k, c = a[name].shape[-2:]
        return a[name].reshape(k, c // P, P).transpose(2, 1, 0).reshape(P, -1)

    pack = {}
    for name, n in VECTORS:
        if name in ("conv_dw", "conv_w_2"):
            pack[name] = taps(name)
        elif name.startswith("lambda_"):
            pack[name] = on_all(name)
        elif a[name].size == 64:
            pack[name] = halves(name)
        else:
            pack[name] = per_channel(name)
        assert pack[name].shape == (P, n), name
    arrays = {
        "x": a["x"][0], "mem": a["mem"][0],
        "vectors": np.concatenate([pack[n] for n, _ in VECTORS], axis=1),
        "w_in": a["w_in"][0], "w_conv_proj": a["w_conv_proj"][0],
        "w_diff_proj": a["w_diff_proj"][0], "w_mem_kv": a["w_mem_kv"][0],
        "w_x_proj": a["w_x_proj"][0], "w_out": a["w_out"][0], "w_in_2": a["w_in_2"][0],
        "rg_w_a": a["rg_w_a_2"][0], "rg_w_x": a["rg_w_x_2"][0], "w_out_2": a["w_out_2"][0],
        "norm_ffn": np.broadcast_to(a["norm_ffn_2"][0].reshape(1, D), (P, D)),
        "w_query": a["peer_w_query_2"][0].reshape(D, PEER_SIDES * P),
        "sub_keys_t": a["peer_sub_keys_2"][0].reshape(PEER_SIDES, PEER_KEYS, P).transpose(2, 0, 1),
        "experts": np.concatenate([a["peer_u_2"][0], a["peer_v_2"][0]], axis=1),
    }
    arrays = {f"in_{n}": np.ascontiguousarray(x) for n, x in arrays.items()}
    nc = bacc.Bacc("TRN2", target_bir_lowering=False, num_devices=1)
    aps = [nc.dram_tensor(n, x.shape, mybir.dt.from_np(x.dtype), kind="ExternalInput").ap()
           for n, x in arrays.items()]
    out = nc.dram_tensor("out_x", [T, D], F32, kind="ExternalOutput").ap()
    build(nc, *aps, out)
    r = run_bass_kernel_spmd(nc, [arrays], core_ids=[0])
    return r.results[0]["out_x"].reshape(1, T, D)
```

```python
from contextlib import ExitStack

import concourse.bass as bass
from concourse import mybir

P = 128
F32 = mybir.dt.float32
U32 = mybir.dt.uint32
ALU = mybir.AluOpType
ACT = mybir.ActivationFunctionType
AX = mybir.AxisListType.X

T = 256
TT = T // P
D = 1024
KT = D // P
SLOT = 512
CONV_K = 31
DIFF_HEADS = 8
DIFF_HEAD_DIM = 64
LAMBDA_INIT = 0.2
X_HEADS = 4
X_HEAD_DIM = D // X_HEADS
SB_HEADS = 8
SB_HEAD_DIM = 64
D_SB = SB_HEADS * SB_HEAD_DIM
D_RG = D - D_SB
RG_TILES = D_RG // P
RG_WIDTH = 4
PEER_HEADS = 8
PEER_KEYS = 128
PEER_TOPK = 16
PEER_SIDES = 2 * PEER_HEADS
PICKS = PEER_HEADS * PEER_TOPK
MASKED = -1.0e30
W_RING = 3

VECTORS = [("norm_g", KT), ("mem_norm_g", KT), ("conv_dw", KT * CONV_K), ("conv_dw_b", KT),
           ("conv_ln_g", KT), ("conv_ln_b", KT), ("diff_qn_g", 1), ("diff_kn_g", 1),
           ("lambda_q1", 64), ("lambda_k1", 64), ("lambda_q2", 64), ("lambda_k2", 64),
           ("diff_subln_g", 1), ("x_qn_g", 2), ("x_kn_g", 2), ("norm_mix_2", KT),
           ("q_norm_2", 1), ("k_norm_2", 1), ("conv_w_2", RG_TILES * RG_WIDTH),
           ("conv_b_2", RG_TILES), ("rg_b_a_2", RG_TILES), ("rg_b_x_2", RG_TILES),
           ("rg_lambda_2", RG_TILES), ("out_norm_sb_2", D_SB // P), ("out_norm_rg_2", RG_TILES)]
VECTOR_AT = {}
for _name, _n in VECTORS:
    VECTOR_AT[_name] = (sum(n for _, n in VECTORS[:len(VECTOR_AT)]), _n)
VECTOR_COLS = sum(n for _, n in VECTORS)


class Counter:

    def __init__(self, sem):
        self.sem, self.value = sem, 0


class Step:

    def __init__(self, counter):
        self.counter, self.value, self.waited = counter, None, False


class Queue:

    def __init__(self, name, semaphore):
        self.name, self.semaphore, self.items, self.counter = name, semaphore, [], None

    def stage(self, name):
        self.counter = Counter(self.semaphore(f"{self.name}_{name}"))

    def do(self, instruction, *args, after=(), **named):
        step = Step(self.counter)
        return self.put(step, 1, instruction, args, named, after)

    def dma(self, instruction, *args, counter, after=(), **named):
        step = Step(counter)
        step.waited = True
        return self.put(step, 16, instruction, args, named, after)

    def put(self, step, by, instruction, args, named, after):
        for a in after:
            a.waited = True
        self.items.append((list(after), instruction, args, named, step, by))
        return step

    def number(self):
        for *_, step, by in self.items:
            if step.waited:
                step.counter.value += by
                step.value = step.counter.value

    def emit(self, engine):
        reached = {}
        for after, instruction, args, named, step, by in self.items:
            need = {}
            for a in after:
                need[id(a.counter)] = max(need.get(id(a.counter), (0, None))[0], a.value), a.counter
            for key, (value, counter) in need.items():
                if reached.get(key, 0) < value:
                    engine.wait_ge(counter.sem, value)
                    reached[key] = value
            issued = instruction(*args, **named)
            if step.waited:
                issued.then_inc(step.counter.sem, by)


class Buffer:

    def __init__(self, ap, counter=None):
        self.ap, self.counter, self.free = ap, counter, []


class Ring:
    def __init__(self, buffers):
        self.buffers, self.n = buffers, 0

    def take(self):
        self.n += 1
        return self.buffers[(self.n - 1) % len(self.buffers)]


def build(nc, x, mem, vectors, w_in, w_conv_proj, w_diff_proj, w_mem_kv, w_x_proj, w_out,
          w_in_2, rg_w_a, rg_w_x, w_out_2, norm_ffn, w_query, sub_keys_t, experts, out):
    with ExitStack() as ctx:
        def sb(name, shape, dt=F32):
            return ctx.enter_context(nc.sbuf_tensor(name, [P, *shape], dt))

        def semaphore(name):
            return ctx.enter_context(nc.semaphore(name))

        pe, act, dve, pool, sp = (Queue(n, semaphore) for n in ("pe", "act", "dve", "pool", "sp"))

        def stage(name):
            for q in (pe, act, dve, pool):
                q.stage(name)

        def load_counter(name):
            return Counter(semaphore(f"load_{name}"))

        stage("setup")

        w_space = sb("w_ring", [W_RING * KT * SLOT])
        w_ring = Ring([Buffer(w_space[:, i * KT * SLOT:(i + 1) * KT * SLOT]
                              .rearrange("p (k n) -> p k n", k=KT), load_counter(f"w{i}"))
                       for i in range(W_RING)])
        vec = sb("vec", [VECTOR_COLS])
        actT = sb("actT", [KT, T])
        conv_in = sb("conv_in", [KT, CONV_K - 1 + T])
        conv_acc = sb("conv_acc", [KT, T])
        big = [sb(f"big{i}", [KT * T]) for i in range(9)]
        merge = sb("merge", [3 * KT, T])
        work = Ring([Buffer(sb(f"work{i}", [4 * T])) for i in range(4)])
        probs = Ring([Buffer(sb(f"probs{i}", [2, 384])) for i in range(2)])
        probs_t = Ring([Buffer(sb(f"probs_t{i}", [512])) for i in range(2)])
        ident = sb("ident", [P])
        ones = sb("ones", [P])
        ones64 = sb("ones64", [P])
        later = sb("later", [P])
        before = sb("before", [P])
        dist = sb("dist", [384])
        iota16 = sb("iota16", [PEER_TOPK])
        col = sb("col", [96])

        units = Ring([Buffer(ctx.enter_context(nc.psum_tensor(f"unit{i}", [P, 1024], F32)))
                      for i in range(3)])
        banks = Ring([Buffer(ctx.enter_context(nc.psum_tensor(f"bank{i}", [P, 512], F32)))
                      for i in range(2)])

        def cm(b):
            return b[:, :].rearrange("p (k t) -> p k t", k=KT)

        def tm(b):
            return b[:, :].rearrange("p (t c) -> p t c", t=TT)

        def v(name, i=0, n=1):
            at = VECTOR_AT[name][0]
            return vec[:, at + i:at + i + n]

        EPS6, EPS5, ONE, NEG_HALF = (col[:, i:i + 1] for i in range(4))
        LAM = col[:, 8:9]
        used = [12]

        def cols(n):
            used[0] += n
            return col[:, used[0] - n:used[0]]

        def load_weights(w, column):
            slot = w_ring.take()
            src = w.rearrange("(k p) n -> p k n", p=P)[:, :, column:column + SLOT]
            dst = slot.ap
            slot.ready = sp.dma(nc.sync.dma_start, dst, src, counter=slot.counter,
                                after=slot.free)
            slot.free = []
            return slot

        x_tm, mem_tm = tm(big[8]), merge[:, 0:KT, :].rearrange("p k t -> p (k t)").rearrange(
            "p (t c) -> p t c", t=TT)
        x_in = x.rearrange("(t p) c -> p t c", p=P)
        mem_in = mem.rearrange("(t p) c -> p t c", p=P)
        c_x, c_vec, c_mem = load_counter("x"), load_counter("vec"), load_counter("mem")
        x_ready = act.dma(nc.scalar.dma_start, x_tm, x_in, counter=c_x)
        vec_ready = act.dma(nc.scalar.dma_start, vec[:, :], vectors, counter=c_vec)
        mem_ready = act.dma(nc.scalar.dma_start, mem_tm, mem_in, counter=c_mem)

        s = dve.do(nc.vector.memset, col[:, :], 0.0)
        for ap, value in ((EPS6, 1e-6), (EPS5, 1e-5), (ONE, 1.0), (NEG_HALF, -0.5)):
            const_ready = dve.do(nc.vector.memset, ap, value, after=[s])
        ones_ready = dve.do(nc.vector.memset, ones[:, :], 1.0)
        s = dve.do(nc.vector.memset, ones64[:, :], 0.0)
        dve.do(nc.vector.memset, ones64[0:64, 0:64], 1.0, after=[s])
        ones64_ready = dve.do(nc.vector.memset, ones64[64:128, 64:128], 1.0, after=[s])
        conv_pad = dve.do(nc.vector.memset, conv_in[:, :, 0:CONV_K - 1], 0.0)

        s = pool.do(nc.gpsimd.memset, ident[:, :], 0.0)
        ident_ready = pool.do(nc.gpsimd.affine_select,
            out=ident[:, :], in_=ident[:, :], compare_op=ALU.not_equal, fill=1.0, base=0,
            pattern=[[-1, P]], channel_multiplier=1, after=[s])
        s = pool.do(nc.gpsimd.memset, later[:, :], 1.0)
        pool.do(nc.gpsimd.affine_select, out=later[:, :], in_=later[:, :], compare_op=ALU.is_gt,
                                          fill=0.0, base=0, pattern=[[-1, P]],
                                          channel_multiplier=1, after=[s])
        s = pool.do(nc.gpsimd.memset, before[:, :], 1.0)
        pool.do(nc.gpsimd.affine_select, out=before[:, :], in_=before[:, :], compare_op=ALU.is_gt,
                                          fill=0.0, base=0, pattern=[[1, P]],
                                          channel_multiplier=-1, after=[s])
        s = pool.do(nc.gpsimd.iota, dist[:, 0:256], [[1, 256]], base=-P, channel_multiplier=-1,
                                     allow_small_or_imprecise_dtypes=True)
        s = pool.do(nc.gpsimd.iota, dist[:, 256:384], [[1, P]], base=0, channel_multiplier=-1,
                                     allow_small_or_imprecise_dtypes=True, after=[s])
        s = pool.do(nc.gpsimd.affine_select,
            out=dist[:, 0:256], in_=dist[:, 0:256], compare_op=ALU.is_ge, fill=MASKED, base=P,
            pattern=[[-1, 256]], channel_multiplier=1, after=[s])
        s = pool.do(nc.gpsimd.affine_select,
            out=dist[:, 256:384], in_=dist[:, 256:384], compare_op=ALU.is_ge, fill=MASKED, base=0,
            pattern=[[-1, P]], channel_multiplier=1, after=[s])
        pool_consts = pool.do(nc.gpsimd.iota, iota16[:, :], [[1, PEER_TOPK]], base=0,
                                               channel_multiplier=0,
                                               allow_small_or_imprecise_dtypes=True, after=[s])

        def project_cm(slot, rhs, rhs_ready):
            unit = units.take()
            after = [slot.ready, *unit.free, *rhs_ready]
            for j in range(SLOT // P):
                for k in range(KT):
                    s = pe.do(nc.tensor.matmul,
                        unit.ap[:, j * T:(j + 1) * T], slot.ap[:, k, j * P:(j + 1) * P],
                        rhs[:, k, :], start=k == 0, stop=k == KT - 1, after=after)
                    after = []
            slot.free, unit.ready, unit.free = [s], s, []
            return unit

        def project_tm(slot, lhs, lhs_ready):
            unit = units.take()
            after = [slot.ready, *unit.free, *lhs_ready]
            for t in range(TT):
                for k in range(KT):
                    s = pe.do(nc.tensor.matmul,
                        unit.ap[:, t * SLOT:(t + 1) * SLOT], lhs[:, k, t * P:(t + 1) * P],
                        slot.ap[:, k, :], start=k == 0, stop=k == KT - 1, after=after)
                    after = []
            slot.free, unit.ready, unit.free = [s], s, []
            return unit

        def tiles4(ap):
            return ap.rearrange("p (j t) -> p j t", j=4)

        def rsqrt_of(out_ap, in_ap, mean_over, eps, after):
            s = act.do(nc.scalar.activation, out_ap, in_ap, ACT.Ln, bias=eps,
                                              scale=1.0 / mean_over, after=[*after, const_ready])
            s2 = act.do(nc.scalar.activation, out_ap, out_ap, ACT.Exp, scale=-0.5, after=[s])
            return s, s2

        def normalise_tm(src, ready, scratch):
            ss = cols(TT)
            for t in range(TT):
                s = dve.do(nc.vector.tensor_tensor_reduce,
                    out=scratch.ap[:, 0:D], in0=src[:, t, :], in1=src[:, t, :], scale=1.0,
                    scalar=0.0, op0=ALU.mult, op1=ALU.add, accum_out=ss[:, t:t + 1],
                    after=[*ready, *scratch.free, const_ready])
                scratch.free = [s]
            return ss, rsqrt_of(ss, ss, D, EPS6, [s])[1]

        def transpose_tm(src, ready, dst, dst_free, gain=None):
            done = []
            for half in range(2):
                unit = units.take()
                after = [*ready, *unit.free, ident_ready]
                for j in range(4):
                    for t in range(TT):
                        k = 4 * half + j
                        s = pe.do(nc.tensor.transpose,
                            unit.ap[:, j * T + t * P:j * T + (t + 1) * P],
                            src[:, t, k * P:(k + 1) * P], ident[:, :], after=after)
                        after = []
                unit.free = []
                for j in range(4):
                    k = 4 * half + j
                    if gain is None:
                        d = act.do(nc.scalar.copy,
                            dst[:, k, :], unit.ap[:, j * T:(j + 1) * T], after=[s, *dst_free])
                    else:
                        d = act.do(nc.scalar.activation,
                            dst[:, k, :], unit.ap[:, j * T:(j + 1) * T], ACT.Copy,
                            scale=v(gain, k), after=[s, *dst_free, vec_ready])
                unit.free = [d]
                done.append(d)
            return done

        def sum_over_channels(sq, ready, weights, groups, width, unit):
            after = [*ready, *unit.free, ones64_ready]
            for g, members in enumerate(groups):
                for i, a in enumerate(members):
                    s = pe.do(nc.tensor.matmul,
                        unit.ap[:, g * width:(g + 1) * width], weights[:, :],
                        sq[:, a * width:(a + 1) * width], start=i == 0, stop=i == len(members) - 1,
                        after=after)
                    after = []
            unit.free = []
            return s

        def to_silu(unit, dst):
            s = act.do(nc.scalar.activation, dst, tiles4(unit.ap[:, :]), ACT.Tanh, scale=0.5,
                       after=[unit.ready])
            s = dve.do(nc.vector.scalar_tensor_tensor,
                out=dst, in0=dst, scalar=1.0, in1=tiles4(unit.ap[:, :]), op0=ALU.add,
                op1=ALU.mult, after=[s])
            unit.free = [s]
            return s

        def copy_out(unit, dst, ready, engine):
            if engine is act:
                s = act.do(nc.scalar.copy, dst, unit, after=ready)
            else:
                s = dve.do(nc.vector.tensor_copy, dst, unit, after=ready)
            return s

        stage("input")
        w = w_ring.buffers[0]
        ss, s = normalise_tm(x_tm, [x_ready], work.buffers[0])
        for t in range(TT):
            s2 = dve.do(nc.vector.tensor_scalar, x_tm[:, t, :], x_tm[:, t, :],
                                                       ss[:, t:t + 1], None, ALU.mult, after=[s])
        hT_ready = transpose_tm(x_tm, [s2], actT, [], "norm_g")
        memT = merge[:, KT:2 * KT, :]
        ssm, s = normalise_tm(mem_tm, [mem_ready], work.buffers[1])
        for t in range(TT):
            s2 = dve.do(nc.vector.tensor_scalar, mem_tm[:, t, :], mem_tm[:, t, :],
                                                       ssm[:, t:t + 1], None, ALU.mult, after=[s])
        mem_norm_ready = s2

        dots = cols(2)
        for i, (a, b) in enumerate((("lambda_q1", "lambda_k1"), ("lambda_q2", "lambda_k2"))):
            junk = work.buffers[2].ap
            s = dve.do(nc.vector.tensor_tensor_reduce,
                out=junk[:, 64 * i:64 * i + 64], in0=v(a, 0, 64), in1=v(b, 0, 64), scale=1.0,
                scalar=0.0, op0=ALU.mult, op1=ALU.add, accum_out=dots[:, i:i + 1],
                after=[vec_ready])
        work.buffers[2].free = [s]
        s = act.do(nc.scalar.activation, dots, dots, ACT.Exp, after=[s])
        lam_ready = dve.do(nc.vector.scalar_tensor_tensor,
            out=LAM, in0=dots[:, 0:1], scalar=LAMBDA_INIT, in1=dots[:, 1:2], op0=ALU.add,
            op1=ALU.subtract, after=[s, const_ready])
        qg, subln_g, xq_g, q2_g = cols(1), cols(1), cols(2), cols(1)
        half_dw = vec[:, VECTOR_AT["conv_dw"][0]:VECTOR_AT["conv_dw"][0] + KT * CONV_K]
        for dst, src, by in ((qg, v("diff_qn_g"), DIFF_HEAD_DIM ** -0.5),
                             (subln_g, v("diff_subln_g"), 0.5 * (1.0 - LAMBDA_INIT)),
                             (xq_g, v("x_qn_g", 0, 2), X_HEAD_DIM ** -0.5),
                             (q2_g, v("q_norm_2"), SB_HEAD_DIM ** -0.5),
                             (half_dw, half_dw, 0.5)):
            gains_ready = dve.do(nc.vector.tensor_scalar,
                dst, src, by, None, ALU.mult, after=[vec_ready, const_ready])

        stage("glu")
        u_ready = []
        for i in range(2):
            slot_a, slot_b = load_weights(w_in, i * SLOT), load_weights(w_in, D + i * SLOT)
            ua = project_cm(slot_a, actT, hT_ready)
            ub = project_cm(slot_b, actT, [])
            th = work.take()
            s = act.do(nc.scalar.activation, th.ap[:, :], ub.ap[:, :], ACT.Tanh,
                                                            scale=0.5, after=[ub.ready, *th.free])
            ub.free = [s]
            s = dve.do(nc.vector.scalar_tensor_tensor,
                out=conv_in[:, 4 * i:4 * i + 4, CONV_K - 1:], in0=tiles4(th.ap[:, :]), scalar=1.0,
                in1=tiles4(ua.ap[:, :]), op0=ALU.add, op1=ALU.mult,
                after=[s, ua.ready, conv_pad])
            ua.free, th.free = [s], [s]
            u_ready.append(s)

        conv_done = {}

        def convolve(tiles):
            last = {}
            for k in range(CONV_K):
                for t in tiles:
                    tap = v("conv_dw", t * CONV_K + k)
                    src = conv_in[:, t, k:k + T]
                    dst = conv_acc[:, t, :]
                    if k == 0:
                        last[t] = dve.do(nc.vector.tensor_scalar,
                            dst, src, tap, v("conv_dw_b", t), ALU.mult, ALU.add,
                            after=[u_ready[t // 4], gains_ready])
                    else:
                        last[t] = dve.do(nc.vector.scalar_tensor_tensor, out=dst, in0=src, scalar=tap,
                                                                in1=dst, op0=ALU.mult,
                                                                op1=ALU.add, after=[last[t]])
            conv_done.update(last)

        def head_norm(unit, dst, weights, mean_over, gain, per_head):
            sq = work.take()
            s2 = dve.do(nc.vector.tensor_copy, dst, tiles4(unit.ap[:, :]), after=[unit.ready])
            unit.free = [s2]
            s1 = act.do(nc.scalar.activation, tiles4(sq.ap[:, :]), dst, ACT.Square,
                        after=[s2, *sq.free])
            sums = units.take()
            if per_head == 1:
                s = sum_over_channels(sq.ap, [s1], weights, [[0], [1]], 512, sums)
                n = 4 * T
            else:
                s = sum_over_channels(sq.ap, [s1], weights, [[0, 1], [2, 3]], T, sums)
                n = 2 * T
            sq.free = [s]
            rs = work.take()
            s, s3 = rsqrt_of(rs.ap[:, 0:n], sums.ap[:, 0:n], mean_over, EPS6, [s, *rs.free])
            sums.free = [s]
            if per_head == 1:
                s = dve.do(nc.vector.scalar_tensor_tensor,
                    out=dst, in0=dst, scalar=gain, in1=tiles4(rs.ap[:, :]), op0=ALU.mult,
                    op1=ALU.mult, after=[s2, s3, gains_ready])
            else:
                for j in range(per_head):
                    part = dst[:, j:4:per_head, :]
                    s = dve.do(nc.vector.scalar_tensor_tensor,
                        out=part, in0=part, scalar=gain[:, j:j + 1],
                        in1=rs.ap[:, 0:n].rearrange("p (g t) -> p g t", t=T), op0=ALU.mult,
                        op1=ALU.mult, after=[s2, s3, gains_ready])
            rs.free = [s]
            return s

        q_cm, k_cm, v_tm, dgate = cm(big[0]), cm(big[1]), tm(big[2]), cm(big[3])
        cgate, xq_cm, xk_cm, xv_tm = cm(big[4]), cm(big[5]), cm(big[6]), tm(big[7])
        COL_CGATE, COL_Q, COL_K, COL_V = 2 * D, 3 * D, 4 * D, 5 * D
        COL_DGATE, COL_XQ, COL_XGATE, COL_MERGE = 6 * D, 7 * D, 8 * D, 9 * D

        stage("diff_qkv")
        q_ready, k_ready, v_ready = [], [], []
        for i in range(2):
            unit = project_cm(load_weights(w_in, COL_Q + i * SLOT), actT, [])
            q_ready.append(head_norm(unit, q_cm[:, 4 * i:4 * i + 4, :], ones64, DIFF_HEAD_DIM,
                                     qg, 1))
            unit = project_cm(load_weights(w_in, COL_K + i * SLOT), actT, [])
            k_ready.append(head_norm(unit, k_cm[:, 4 * i:4 * i + 4, :], ones64, DIFF_HEAD_DIM,
                                     v("diff_kn_g"), 1))
            if i == 0:
                convolve((0, 1))
            unit = project_tm(load_weights(w_in, COL_V + i * SLOT), actT, [])
            s = copy_out(unit.ap[:, :].rearrange("p (t c) -> p t c", t=TT),
                         v_tm[:, :, i * SLOT:(i + 1) * SLOT], [unit.ready], act)
            unit.free = [s]
            v_ready.append(s)

        stage("diff_attention")
        o_ready = {}
        scored = {}

        def diff_scores(h):
            slope = 2.0 ** (-8.0 * (h + 1) / DIFF_HEADS)
            unit, p = units.take(), probs.take()
            after = [q_ready[h // 4], k_ready[h // 4], *unit.free]
            for m in range(2):
                rows = slice(64 * m, 64 * m + 64)
                for qt, width, at in ((1, 2 * P, 0), (0, P, 2 * P)):
                    s = pe.do(nc.tensor.matmul,
                        unit.ap[:, 512 * m + at:512 * m + at + width],
                        q_cm[rows, h, qt * P:(qt + 1) * P], k_cm[rows, h, 0:width],
                        start=True, stop=True, after=after)
                    after = []
            scores = unit.ap[:, :].rearrange("p (m c) -> p m c", m=2)[:, :, 0:384]
            s = dve.do(nc.vector.scalar_tensor_tensor,
                out=p.ap[:, :, :], in0=dist[:, :].unsqueeze(1).to_broadcast([P, 2, 384]),
                scalar=slope, in1=scores, op0=ALU.mult, op1=ALU.add,
                after=[s, *p.free, pool_consts])
            unit.free = [s]
            small = p.small
            top, total, inv, inv_lam = (small[:, i:i + 4] for i in (0, 4, 8, 12))
            wide, narrow = p.ap[:, :, 0:256], p.ap[:, :, 256:384]
            dve.do(nc.vector.tensor_reduce, top[:, 0:2], wide, AX, ALU.max, after=[s])
            s = dve.do(nc.vector.tensor_reduce, top[:, 2:4], narrow, AX, ALU.max, after=[s])
            s = dve.do(nc.vector.tensor_scalar, top, top, -1.0, None, ALU.mult, after=[s])
            for i, part in ((0, wide), (2, narrow)):
                for m in range(2):
                    e1 = act.do(nc.scalar.activation,
                        part[:, m, :], part[:, m, :], ACT.Exp, bias=top[:, i + m:i + m + 1],
                        accum_out=total[:, i + m:i + m + 1], after=[s])
            s = dve.do(nc.vector.reciprocal, inv, total, after=[e1])
            s = dve.do(nc.vector.tensor_scalar, inv_lam, inv, LAM, None, ALU.mult,
                       after=[s, lam_ready])
            for i, part in ((0, wide), (2, narrow)):
                s2 = dve.do(nc.vector.tensor_scalar,
                    part[:, 1, :], part[:, 1, :], inv_lam[:, i + 1:i + 2], None, ALU.mult,
                    after=[s])
                s3 = dve.do(nc.vector.scalar_tensor_tensor,
                    out=part[:, 0, :], in0=part[:, 0, :], scalar=inv[:, i:i + 1],
                    in1=part[:, 1, :], op0=ALU.mult, op1=ALU.subtract, after=[s2])
            scored[h] = p, s3

        def diff_turn(h):
            p, ready = scored[h]
            bank, pt = banks.take(), probs_t.take()
            after = [ready, *bank.free, ident_ready]
            for dst, src in ((0, 256), (P, 0), (2 * P, P)):
                s = pe.do(nc.tensor.transpose,
                    bank.ap[:, dst:dst + P], p.ap[:, 0, src:src + P], ident[:, :], after=after)
                after = []
            p.free = [s]
            s = act.do(nc.scalar.copy, pt.ap[:, 0:384], bank.ap[:, 0:384], after=[s, *pt.free])
            bank.free = [s]
            scored[h] = pt, s

        def diff_values(h):
            pt, ready = scored[h]
            bank = banks.take()
            vh = v_tm[:, :, h * P:(h + 1) * P]
            pe.do(nc.tensor.matmul, bank.ap[:, 0:256], vh[:, 0, :], pt.ap[:, 0:256], start=True,
                                     stop=False, after=[ready, v_ready[h // 4], *bank.free])
            s = pe.do(nc.tensor.matmul, bank.ap[:, P:256], vh[:, 1, :], pt.ap[:, 256:384],
                                         start=False, stop=True)
            pt.free = [s]
            s = dve.do(nc.vector.tensor_copy, q_cm[:, h, :], bank.ap[:, 0:256], after=[s])
            bank.free = [s]
            o_ready[h] = s

        def diff_finish(i, gate_ready):
            o = q_cm[:, 4 * i:4 * i + 4, :]
            sq = work.take()
            ready = [o_ready[h] for h in range(4 * i, 4 * i + 4)]
            s = act.do(nc.scalar.activation, tiles4(sq.ap[:, :]), o, ACT.Square,
                       after=[*ready, *sq.free])
            sums = units.take()
            s = sum_over_channels(sq.ap, [s], ones, [[0], [1]], 512, sums)
            sq.free = [s]
            rs = work.take()
            s, s3 = rsqrt_of(rs.ap[:, :], sums.ap[:, :], P, EPS6, [s, *rs.free])
            sums.free = [s]
            s = dve.do(nc.vector.scalar_tensor_tensor,
                out=o, in0=o, scalar=subln_g, in1=tiles4(rs.ap[:, :]), op0=ALU.mult,
                op1=ALU.mult, after=[*ready, s3, gains_ready])
            rs.free = [s]
            return dve.do(nc.vector.tensor_tensor, o, o, dgate[:, 4 * i:4 * i + 4, :], ALU.mult,
                          after=[s, gate_ready])

        for i, p in enumerate(probs.buffers):
            p.small = cols(16)

        gate = {}
        dg_ready, cg_ready, xg_ready, xq_ready, xk_ready, xv_ready = [], [], [], [], [], []

        diff_scores(0)
        for i in range(2):
            unit = project_cm(load_weights(w_in, COL_DGATE + i * SLOT), actT, [])
            dg_ready.append(to_silu(unit, dgate[:, 4 * i:4 * i + 4, :]))
            diff_turn(i)
            diff_scores(i + 1)
            convolve((2 + i,))
        for i in range(2):
            unit = project_cm(load_weights(w_in, COL_CGATE + i * SLOT), actT, [])
            cg_ready.append(to_silu(unit, cgate[:, 4 * i:4 * i + 4, :]))
            diff_values(i)
            diff_turn(2 + i)
            diff_scores(3 + i)
            convolve((4 + i,))
        for i in range(2):
            unit = project_cm(load_weights(w_in, COL_XQ + i * SLOT), actT, [])
            xq_ready.append(head_norm(unit, xq_cm[:, 4 * i:4 * i + 4, :], ones, X_HEAD_DIM, xq_g,
                                      2))
            diff_values(2 + i)
            diff_turn(4 + i)
            diff_scores(5 + i)
            convolve((6 + i,))
        do0 = diff_finish(0, dg_ready[0])
        memT_ready = transpose_tm(mem_tm, [mem_norm_ready], memT, [], "mem_norm_g")
        for i in range(2):
            unit = project_cm(load_weights(w_mem_kv, i * SLOT), memT, memT_ready)
            xk_ready.append(head_norm(unit, xk_cm[:, 4 * i:4 * i + 4, :], ones, X_HEAD_DIM,
                                      v("x_kn_g", 0, 2), 2))
            diff_values(4 + i)
            diff_turn(6 + i)
            if i == 0:
                diff_scores(7)
        for i in range(2):
            unit = project_tm(load_weights(w_mem_kv, D + i * SLOT), memT, [])
            s = copy_out(unit.ap[:, :].rearrange("p (t c) -> p t c", t=TT),
                         xv_tm[:, :, i * SLOT:(i + 1) * SLOT], [unit.ready], act)
            mem_used = unit.ready
            unit.free = [s]
            xv_ready.append(s)
            diff_values(6 + i)
        do1 = diff_finish(1, dg_ready[1])
        diff_out_ready = [do0, do1]

        stage("cross_attention")
        xgate = cm(big[8])

        def cross_scores(h):
            unit, p = units.take(), probs.take()
            after = [xq_ready[h // 2], xk_ready[h // 2], *unit.free]
            for qt in range(TT):
                for j in range(2):
                    s = pe.do(nc.tensor.matmul,
                        unit.ap[:, qt * T:(qt + 1) * T], xq_cm[:, 2 * h + j, qt * P:(qt + 1) * P],
                        xk_cm[:, 2 * h + j, :], start=j == 0, stop=j == 1, after=after)
                    after = []
            small = p.small
            top, total = small[:, 0:2], small[:, 4:6]
            flat = p.ap[:, :, :].rearrange("p a b -> p (a b)")[:, 0:2 * T]
            s = dve.do(nc.vector.tensor_reduce,
                top, unit.ap[:, 0:2 * T].rearrange("p (q k) -> p q k", q=2), AX, ALU.max,
                after=[s, *p.free])
            s = dve.do(nc.vector.tensor_scalar, top, top, -1.0, None, ALU.mult, after=[s])
            for qt in range(TT):
                e1 = act.do(nc.scalar.activation,
                    flat[:, qt * T:(qt + 1) * T], unit.ap[:, qt * T:(qt + 1) * T], ACT.Exp,
                    bias=top[:, qt:qt + 1], accum_out=total[:, qt:qt + 1], after=[s])
            unit.free = [e1]
            s = dve.do(nc.vector.reciprocal, total, total, after=[e1])
            for qt in range(TT):
                s2 = dve.do(nc.vector.tensor_scalar,
                    flat[:, qt * T:(qt + 1) * T], flat[:, qt * T:(qt + 1) * T],
                    total[:, qt:qt + 1], 0.5, ALU.mult, ALU.mult, after=[s])
            scored["x", h] = p, flat, s2

        def cross_turn(h):
            p, flat, ready = scored["x", h]
            bank, pt = banks.take(), probs_t.take()
            after = [ready, *bank.free]
            for kt in range(2):
                for qt in range(TT):
                    s = pe.do(nc.tensor.transpose,
                        bank.ap[:, kt * T + qt * P:kt * T + (qt + 1) * P],
                        flat[:, qt * T + kt * P:qt * T + (kt + 1) * P], ident[:, :], after=after)
                    after = []
            p.free = [s]
            s = act.do(nc.scalar.copy, pt.ap[:, :], bank.ap[:, :], after=[s, *pt.free])
            bank.free = [s]
            scored["x", h] = pt, s

        def cross_values(h):
            pt, ready = scored["x", h]
            bank = banks.take()
            after = [ready, xv_ready[h // 2], *bank.free]
            for j in range(2):
                for kt in range(2):
                    s = pe.do(nc.tensor.matmul,
                        bank.ap[:, j * T:(j + 1) * T],
                        xv_tm[:, kt, (2 * h + j) * P:(2 * h + j + 1) * P],
                        pt.ap[:, kt * T:(kt + 1) * T], start=kt == 0, stop=kt == 1, after=after)
                    after = []
            pt.free = [s]
            dst = xgate[:, 2 * h:2 * h + 2, :]
            s = dve.do(nc.vector.tensor_tensor,
                dst, dst, bank.ap[:, :].rearrange("p (j t) -> p j t", j=2), ALU.mult,
                after=[s, xg_ready[h // 2]])
            bank.free = [s]
            return s

        cross_scores(0)
        for i in range(2):
            unit = project_cm(load_weights(w_in, COL_XGATE + i * SLOT), actT, [])
            xg_ready.append(to_silu(unit, xgate[:, 4 * i:4 * i + 4, :]))
            cross_turn(i)
            cross_scores(i + 1)

        stage("conv_norm")
        rows, rs_row = cols(1), None
        unit = units.take()
        s = None
        after = [*conv_done.values(), *unit.free, ones_ready]
        for k in range(KT):
            s = pe.do(nc.tensor.matmul,
                unit.ap[:, 0:T], ones[:, :], conv_acc[:, k, :], start=k == 0, stop=k == KT - 1,
                after=after)
            after = []
        mean = work.take()
        s = act.do(nc.scalar.activation,
            mean.ap[:, 0:T], unit.ap[:, 0:T], ACT.Copy, scale=1.0 / D, after=[s, *mean.free])
        unit.free = [s]
        centred = dve.do(nc.vector.tensor_tensor,
            conv_acc[:, :, :], conv_acc[:, :, :],
            mean.ap[:, 0:T].unsqueeze(1).to_broadcast([P, KT, T]), ALU.subtract, after=[s])
        mean.free = [centred]
        merge_free = [mem_used]
        merge_ready = {}

        def merge_slot(i):
            unit = project_cm(load_weights(w_in, COL_MERGE + i * SLOT), actT, [])
            s = act.do(nc.scalar.activation, merge[:, 4 * i:4 * i + 4, :],
                                              tiles4(unit.ap[:, :]), ACT.Tanh, scale=0.5,
                       after=[unit.ready, *merge_free])
            unit.free = [s]
            merge_ready[i] = s

        merge_slot(0)
        unit = units.take()
        after = [*unit.free]
        for half in range(2):
            sq = work.take()
            s = act.do(nc.scalar.activation,
                tiles4(sq.ap[:, :]), conv_acc[:, 4 * half:4 * half + 4, :], ACT.Square,
                after=[centred, *sq.free])
            after.append(s)
            for k in range(4):
                s = pe.do(nc.tensor.matmul,
                    unit.ap[:, 0:T], ones[:, :], sq.ap[:, k * T:(k + 1) * T],
                    start=half == 0 and k == 0, stop=half == 1 and k == 3, after=after)
                after = []
            sq.free = [s]
        rs = work.take()
        s, s3 = rsqrt_of(rs.ap[:, 0:T], unit.ap[:, 0:T], D, EPS5, [s, *rs.free])
        unit.free = [s]
        conv_out_ready = []
        for half in range(2):
            part = conv_acc[:, 4 * half:4 * half + 4, :]
            z = work.take()
            for j in range(4):
                k = 4 * half + j
                s = dve.do(nc.vector.scalar_tensor_tensor,
                    out=conv_acc[:, k, :], in0=conv_acc[:, k, :], scalar=v("conv_ln_g", k),
                    in1=rs.ap[:, 0:T], op0=ALU.mult, op1=ALU.mult, after=[s3, centred])
                s = dve.do(nc.vector.tensor_scalar,
                    conv_acc[:, k, :], conv_acc[:, k, :], v("conv_ln_b", k), 0.25, ALU.add,
                    ALU.mult, after=[s])
            s2 = act.do(nc.scalar.activation,
                tiles4(z.ap[:, :]), part, ACT.Tanh, scale=2.0, after=[s, *z.free])
            s2 = dve.do(nc.vector.scalar_tensor_tensor,
                out=part, in0=tiles4(z.ap[:, :]), scalar=1.0, in1=part, op0=ALU.add,
                op1=ALU.mult, after=[s2])
            z.free = [s2]
            gpart = cgate[:, 4 * half:4 * half + 4, :]
            conv_out_ready.append(dve.do(nc.vector.tensor_tensor,
                part, part, gpart, ALU.mult, after=[s2, cg_ready[half]]))
        rs.free = [s]

        merge_slot(1)
        cross_ready = [cross_values(0)]
        cross_turn(2)
        cross_scores(3)
        merge_slot(2)
        cross_ready.append(cross_values(1))
        cross_turn(3)
        merge_slot(3)
        cross_ready.append(cross_values(2))
        merge_slot(4)
        cross_ready.append(cross_values(3))
        merge_slot(5)

        stage("branches")
        y_cm = cm(big[1])
        x_res = tm(big[2])
        res_ready = sp.dma(nc.sync.dma_start, x_res, x_in, counter=c_x, after=[o_ready[7]])
        y_last = {}
        for branch, (w, src, ready) in enumerate(((w_conv_proj, conv_acc, conv_out_ready),
                                                  (w_diff_proj, q_cm, diff_out_ready),
                                                  (w_x_proj, xgate, cross_ready))):
            for i in range(2):
                unit = project_cm(load_weights(w, i * SLOT), src, ready)
                gates = merge[:, branch * KT + 4 * i:branch * KT + 4 * i + 4, :]
                part = y_cm[:, 4 * i:4 * i + 4, :]
                dst = work.take() if branch else None
                target = tiles4(dst.ap[:, :]) if branch else part
                s = dve.do(nc.vector.scalar_tensor_tensor, out=target, in0=gates, scalar=1.0,
                                                  in1=tiles4(unit.ap[:, :]), op0=ALU.add,
                                                  op1=ALU.mult,
                           after=[unit.ready, merge_ready[2 * branch + i], scored_all(o_ready),
                                  *(dst.free if dst else [])])
                unit.free = [s]
                if branch:
                    s = dve.do(nc.vector.tensor_tensor,
                        part, part, target, ALU.add, after=[s, y_last[i]])
                    dst.free = [s]
                y_last[i] = s

        stage("block1_out")
        for i in range(2):
            unit = project_tm(load_weights(w_out, i * SLOT), y_cm, list(y_last.values()))
            part = x_res[:, :, i * SLOT:(i + 1) * SLOT]
            s = dve.do(nc.vector.scalar_tensor_tensor,
                out=part, in0=unit.ap[:, :].rearrange("p (t c) -> p t c", t=TT), scalar=0.5,
                in1=part, op0=ALU.mult, op1=ALU.add, after=[unit.ready, res_ready])
            unit.free = [s]
        x1_ready = s

        stage("block2_input")
        xn = tm(big[3])
        junk = work.take()
        ss, s = normalise_tm(x_res, [x1_ready], junk)
        for t in range(TT):
            s2 = dve.do(nc.vector.tensor_scalar, xn[:, t, :], x_res[:, t, :],
                                                       ss[:, t:t + 1], None, ALU.mult, after=[s])
        hT_ready = transpose_tm(xn, [s2], actT, [merge_ready[5]], "norm_mix_2")

        gates_w = merge[:, 0:KT, :].rearrange("p k t -> p (k t)")
        bd = [gates_w[:, i * 512:(i + 1) * 512].rearrange("p (t j) -> p t j", t=4)
              for i in range(2)]
        keys = merge[:, KT:2 * KT, :].rearrange("p k t -> p (k t)").rearrange(
            "p (s n) -> p s n", s=PEER_SIDES)
        ffn_gain = merge[:, 2 * KT:2 * KT + 4, :].rearrange("p k t -> p (k t)")
        c_small = load_counter("block2_small")
        bd_zero = dve.do(nc.vector.memset, gates_w[:, 0:1024], 0.0, after=[y_last[1]])
        bd_ready = []
        for i, w in enumerate((rg_w_a, rg_w_x)):
            for b in range(2):
                src = w.rearrange("(t b) i j -> b i t j", b=2)[b]
                dst = bd[i][64 * b:64 * b + 64, :, 64 * b:64 * b + 64]
                bd_ready.append(act.dma(nc.scalar.dma_start, dst, src,
                                        counter=load_counter(f"rg{i}{b}"), after=[bd_zero]))
        keys_ready = act.dma(nc.scalar.dma_start, keys, sub_keys_t, counter=c_small, after=[y_last[1]])
        ffn_gain_ready = act.dma(nc.scalar.dma_start, ffn_gain, norm_ffn,
                                 counter=load_counter("ffn_gain"), after=[y_last[1]])

        stage("rg_lambda")
        lam_v = v("rg_lambda_2", 0, RG_TILES)
        u, z, z2, acc, neg4sp = (cols(RG_TILES) for _ in range(5))
        s = act.do(nc.scalar.activation, u, lam_v, ACT.Abs, after=[vec_ready])
        s = act.do(nc.scalar.activation, u, u, ACT.Exp, scale=-1.0, after=[s])
        s2 = dve.do(nc.vector.tensor_scalar, z, u, 2.0, None, ALU.add, after=[s])
        s2 = dve.do(nc.vector.reciprocal, z, z, after=[s2])
        s2 = dve.do(nc.vector.tensor_tensor, z, z, u, ALU.mult, after=[s2])
        s2 = dve.do(nc.vector.tensor_tensor, z2, z, z, ALU.mult, after=[s2])
        s2 = dve.do(nc.vector.tensor_scalar, acc, z2, 1.0 / 17, None, ALU.mult, after=[s2])
        for n in (15, 13, 11, 9, 7, 5, 3):
            s2 = dve.do(nc.vector.scalar_tensor_tensor,
                out=acc, in0=acc, scalar=1.0 / n, in1=z2, op0=ALU.add, op1=ALU.mult, after=[s2])
        s2 = dve.do(nc.vector.scalar_tensor_tensor, out=acc, in0=acc, scalar=1.0, in1=z,
                                                     op0=ALU.add, op1=ALU.mult, after=[s2])
        s3 = dve.do(nc.vector.tensor_scalar, u, lam_v, 0.0, 4.0, ALU.min, ALU.mult, after=[s2])
        sp_ready = dve.do(nc.vector.scalar_tensor_tensor,
            out=neg4sp, in0=acc, scalar=-8.0, in1=u, op0=ALU.mult, op1=ALU.add, after=[s3])
        half_ba, half_bx = cols(RG_TILES), cols(RG_TILES)
        dve.do(nc.vector.tensor_scalar, half_ba, v("rg_b_a_2", 0, RG_TILES), 0.5, None,
                                         ALU.mult, after=[vec_ready])
        rg_bias_ready = dve.do(nc.vector.tensor_scalar,
            half_bx, v("rg_b_x_2", 0, RG_TILES), 0.5, None, ALU.mult, after=[vec_ready])

        stage("rg_in")
        xr = conv_in[:, 0:RG_TILES, 0:RG_WIDTH - 1 + T]
        xc = big[4][:, 0:4 * T].rearrange("p (j t) -> p j t", j=4)
        decay = big[4][:, 4 * T:8 * T].rearrange("p (j t) -> p j t", j=4)
        drive = big[5][:, 0:4 * T].rearrange("p (j t) -> p j t", j=4)
        geluT = big[5][:, 4 * T:8 * T].rearrange("p (j t) -> p j t", j=4)
        gate_r = big[6][:, 0:4 * T].rearrange("p (j t) -> p j t", j=4)
        gate_i = big[6][:, 4 * T:8 * T].rearrange("p (j t) -> p j t", j=4)
        mixed = cm(big[7])
        unit = project_cm(load_weights(w_in_2, 3 * D_SB), actT, hT_ready)
        pad = dve.do(nc.vector.memset, xr[:, :, 0:RG_WIDTH - 1], 0.0, after=[*conv_done.values()])
        s = act.do(nc.scalar.copy, xr[:, :, RG_WIDTH - 1:], tiles4(unit.ap[:, :]),
                   after=[unit.ready])
        unit.free = [s]
        xr_ready = s
        last = {}
        for k in range(RG_WIDTH):
            for j in range(RG_TILES):
                tap = v("conv_w_2", j * RG_WIDTH + k)
                src, dst = xr[:, j, k:k + T], xc[:, j, :]
                if k == 0:
                    last[j] = dve.do(nc.vector.tensor_scalar,
                        dst, src, tap, v("conv_b_2", j), ALU.mult, ALU.add,
                        after=[xr_ready, pad])
                else:
                    last[j] = dve.do(nc.vector.scalar_tensor_tensor,
                        out=dst, in0=src, scalar=tap, in1=dst, op0=ALU.mult, op1=ALU.add,
                        after=[last[j]])
        xc_ready = list(last.values())
        q2_cm = big[0][:, 0:4 * T].rearrange("p (j t) -> p j t", j=4)
        k2_cm = big[0][:, 4 * T:8 * T].rearrange("p (j t) -> p j t", j=4)
        v2_tm = big[1][:, 0:2 * D_SB].rearrange("p (t c) -> p t c", t=TT)

        stage("sb_qkv")
        unit = project_cm(load_weights(w_in_2, 0), actT, [])
        q2_ready = head_norm(unit, q2_cm, ones64, SB_HEAD_DIM, q2_g, 1)
        unit = project_cm(load_weights(w_in_2, D_SB), actT, [])
        k2_ready = head_norm(unit, k2_cm, ones64, SB_HEAD_DIM, v("k_norm_2"), 1)

        stage("rg_gates")
        gate_units = []
        for i in range(2):
            unit = units.take()
            after = [*unit.free, *xc_ready, *bd_ready]
            for j in range(RG_TILES):
                s = pe.do(nc.tensor.matmul,
                    unit.ap[:, j * T:(j + 1) * T], bd[i][:, j, :], xc[:, j, :], start=True,
                    stop=True, after=after)
                after = []
            dst, bias = ((gate_r, half_ba), (gate_i, half_bx))[i]
            for j in range(RG_TILES):
                g = act.do(nc.scalar.activation,
                    dst[:, j, :], unit.ap[:, j * T:(j + 1) * T], ACT.Tanh, scale=0.5,
                    bias=bias[:, j:j + 1], after=[s, rg_bias_ready])
            unit.free = [g]
            gate_units.append(g)
        for j in range(RG_TILES):
            s = act.do(nc.scalar.activation,
                decay[:, j, :], gate_r[:, j, :], ACT.Exp, scale=neg4sp[:, j:j + 1],
                bias=neg4sp[:, j:j + 1], after=[gate_units[0], sp_ready])
            s = act.do(nc.scalar.activation,
                gate_r[:, j, :], gate_r[:, j, :], ACT.Tanh, scale=neg4sp[:, j:j + 1],
                bias=neg4sp[:, j:j + 1], after=[s])
        s2 = dve.do(nc.vector.tensor_tensor, drive, decay, decay, ALU.mult, after=[s])
        s2 = dve.do(nc.vector.scalar_tensor_tensor, out=gate_r, in0=drive, scalar=1.0,
                                                     in1=gate_r, op0=ALU.add, op1=ALU.mult,
                    after=[s2])
        s2 = dve.do(nc.vector.tensor_scalar, gate_r, gate_r, -1.0, 1e-19, ALU.mult, ALU.max,
                    after=[s2])
        s = act.do(nc.scalar.activation, gate_r, gate_r, ACT.Ln, after=[s2])
        s = act.do(nc.scalar.activation, gate_r, gate_r, ACT.Exp, scale=0.5, after=[s])
        s2 = dve.do(nc.vector.scalar_tensor_tensor, out=drive, in0=gate_i, scalar=1.0, in1=xc,
                                                     op0=ALU.add, op1=ALU.mult,
                    after=[s2, gate_units[1], *xc_ready])
        s2 = dve.do(nc.vector.scalar_tensor_tensor, out=drive, in0=drive, scalar=0.5,
                                                     in1=gate_r, op0=ALU.mult, op1=ALU.mult,
                    after=[s2, s])
        for j in range(RG_TILES):
            s2_ = dve.do(nc.vector.tensor_tensor_scan,
                mixed[:, 4 + j, :], decay[:, j, :], drive[:, j, :], 0.0, ALU.mult, ALU.add,
                after=[s2])
        scan_ready = s2_

        stage("sb_attention")
        pairs = SB_HEADS // 2
        unit = project_tm(load_weights(w_in_2, 2 * D_SB), actT, [])
        s = copy_out(unit.ap[:, :].rearrange("p (t c) -> p t c", t=TT), v2_tm, [unit.ready], act)
        unit.free = [s]
        v2_ready = s
        unit = project_cm(load_weights(w_in_2, 3 * D_SB + D_RG), actT, [])
        s = act.do(nc.scalar.activation, geluT, tiles4(unit.ap[:, :]),
                                                     ACT.Gelu_apprx_tanh, after=[unit.ready])
        unit.free = [s]
        rg_ready = dve.do(nc.vector.tensor_tensor, mixed[:, 4:8, :], mixed[:, 4:8, :], geluT,
                                                    ALU.mult, after=[s, scan_ready])
        sb_state = {}
        lb_space = [big[3][:, i * 1024:i * 1024 + 768].rearrange("p (a c) -> p a c", a=2)
                    for i in range(2)]
        lb_ring = Ring([Buffer(a) for a in lb_space])
        for b in lb_ring.buffers:
            b.free = hT_ready

        def sb_logits(i):
            unit, lo, lb = units.take(), probs.take(), lb_ring.take()
            after = [q2_ready, k2_ready, *unit.free]
            for m in range(2):
                rows = slice(64 * m, 64 * m + 64)
                for kt, q0, at in ((0, 0, 0), (1, P, 2 * P)):
                    s = pe.do(nc.tensor.matmul,
                        unit.ap[:, 512 * m + at:512 * m + at + T - q0],
                        k2_cm[rows, i, kt * P:(kt + 1) * P], q2_cm[rows, i, q0:T],
                        start=True, stop=True, after=after)
                    after = []
            z = unit.ap[:, :].rearrange("p (m c) -> p m c", m=2)[:, :, 0:384]
            lo_ap, lb_ap = lo.ap[:, :, :], lb.ap
            s = act.do(nc.scalar.activation, lo_ap, z, ACT.Abs, after=[s, *lo.free])
            s = act.do(nc.scalar.activation, lo_ap, lo_ap, ACT.Exp, scale=-1.0, after=[s])
            s = act.do(nc.scalar.activation, lo_ap, lo_ap, ACT.Ln, bias=ONE, after=[s])
            s = dve.do(nc.vector.scalar_tensor_tensor, out=lb_ap, in0=z, scalar=0.0, in1=lo_ap,
                                                        op0=ALU.min, op1=ALU.subtract,
                       after=[s, *lb.free])
            s = dve.do(nc.vector.tensor_tensor, lo_ap, lb_ap, z, ALU.subtract, after=[s])
            unit.free = [s]
            mask = before[:, :].unsqueeze(1).to_broadcast([P, 2, P])
            for at in (0, 2 * P):
                s2 = dve.do(nc.vector.tensor_tensor,
                    lo_ap[:, :, at:at + P], lo_ap[:, :, at:at + P], mask, ALU.mult, after=[s])
            sb_state[i] = lo, lb, s2

        def sb_weights(i):
            lo, lb, ready = sb_state[i]
            unit = units.take()
            after = [ready, *unit.free]
            for m in range(2):
                at = 512 * m
                for dst, w, src, n, start, stop in ((0, later, 0, T, True, False),
                                                    (P, ones, 2 * P, P, False, True),
                                                    (2 * P, later, 2 * P, P, True, True)):
                    s = pe.do(nc.tensor.matmul, unit.ap[:, at + dst:at + dst + n], w[:, :],
                                                  lo.ap[:, m, src:src + n], start=start,
                                                  stop=stop, after=after)
                    after = []
            lo.free = [s]
            suffix = unit.ap[:, :].rearrange("p (m c) -> p m c", m=2)[:, :, 0:384]
            lb_ap = lb.ap
            s = dve.do(nc.vector.tensor_tensor, lb_ap, lb_ap, suffix, ALU.add, after=[s])
            unit.free = [s]
            s = act.do(nc.scalar.activation, lb_ap, lb_ap, ACT.Exp, after=[s])
            mask = before[:, :].unsqueeze(1).to_broadcast([P, 2, P])
            for at in (0, 2 * P):
                s2 = dve.do(nc.vector.tensor_tensor,
                    lb_ap[:, :, at:at + P], lb_ap[:, :, at:at + P], mask, ALU.mult, after=[s])
            sb_state[i] = lb, s2

        def sb_values(i):
            lb, ready = sb_state[i]
            bank = banks.take()
            after = [ready, v2_ready, *bank.free]
            for m in range(2):
                rows = slice(64 * m, 64 * m + 64)
                h = 2 * i + m
                pe.do(nc.tensor.matmul,
                    bank.ap[rows, 0:T], v2_tm[:, 0, h * 64:(h + 1) * 64], lb.ap[:, m, 0:T],
                    start=True, stop=False, after=after)
                after = []
                s = pe.do(nc.tensor.matmul,
                    bank.ap[rows, P:T], v2_tm[:, 1, h * 64:(h + 1) * 64],
                    lb.ap[:, m, 2 * P:3 * P], start=False, stop=True)
            lb.free = [s]
            s = act.do(nc.scalar.copy, mixed[:, i, :], bank.ap[:, 0:T], after=[s])
            bank.free = [s]
            return s

        sb_logits(0)
        sb_logits(1)
        sb_weights(0)
        sb_out = []
        for i in range(pairs):
            if i + 1 < pairs:
                sb_weights(i + 1)
            sb_out.append(sb_values(i))
            if i + 2 < pairs:
                sb_logits(i + 2)

        stage("mix")
        mixed_ready = []
        for half, gain, ready in ((1, "out_norm_rg_2", [rg_ready]), (0, "out_norm_sb_2", sb_out)):
            o = mixed[:, 4 * half:4 * half + 4, :]
            sq = work.take()
            s = act.do(nc.scalar.activation, tiles4(sq.ap[:, :]), o, ACT.Square,
                       after=[*ready, *sq.free])
            unit = units.take()
            s = sum_over_channels(sq.ap, [s], ones, [[0, 1, 2, 3]], T, unit)
            sq.free = [s]
            rs = work.take()
            s, s3 = rsqrt_of(rs.ap[:, 0:T], unit.ap[:, 0:T], D_SB, EPS6, [s, *rs.free])
            unit.free = [s]
            for j in range(4):
                s = dve.do(nc.vector.scalar_tensor_tensor,
                    out=o[:, j, :], in0=o[:, j, :], scalar=v(gain, j), in1=rs.ap[:, 0:T],
                    op0=ALU.mult, op1=ALU.mult, after=[s3, *ready])
            rs.free = [s]
            mixed_ready.append(s)
        for i in range(2):
            unit = project_tm(load_weights(w_out_2, i * SLOT), mixed, mixed_ready)
            part = x_res[:, :, i * SLOT:(i + 1) * SLOT]
            s = dve.do(nc.vector.tensor_tensor,
                part, unit.ap[:, :].rearrange("p (t c) -> p t c", t=TT), part, ALU.add,
                after=[unit.ready])
            unit.free = [s]
        x2_ready = s

        stage("peer_queries")
        h3 = tm(big[3])
        junk = work.take()
        ss, s = normalise_tm(x_res, [x2_ready], junk)
        for t in range(TT):
            h3_ready = dve.do(nc.vector.scalar_tensor_tensor,
                out=h3[:, t, :], in0=x_res[:, t, :], scalar=ss[:, t:t + 1], in1=ffn_gain,
                op0=ALU.mult, op1=ALU.mult, after=[s, ffn_gain_ready, *lb_ring.buffers[0].free,
                                                    *lb_ring.buffers[1].free])
        hT_ready = transpose_tm(h3, [h3_ready], actT, [])
        pq = [cm(big[0]), cm(big[1])]
        scores = [big[4 + t][:, :].rearrange("p (s n) -> p s n", s=PEER_SIDES) for t in range(TT)]
        scored_sides = {}
        for i in range(4):
            slot = load_weights(w_query, i * SLOT)
            unit = project_cm(slot, actT, hT_ready)
            sides = slice(4 * (i % 2), 4 * (i % 2) + 4)
            copied = act.do(nc.scalar.copy, pq[i // 2][:, sides, :], tiles4(unit.ap[:, :]),
                            after=[unit.ready])
            unit.free = [copied]
            for t in range(TT):
                bank = banks.take()
                after = [*bank.free, copied, keys_ready]
                for j in range(4):
                    s = pe.do(nc.tensor.matmul, bank.ap[:, j * P:(j + 1) * P],
                              pq[i // 2][:, 4 * (i % 2) + j, t * P:(t + 1) * P],
                              keys[:, 4 * i + j, :], start=True, stop=True, after=after)
                    after = []
                d = act.do(nc.scalar.copy, scores[t][:, 4 * i:4 * i + 4, :],
                           bank.ap[:, :].rearrange("p (s n) -> p s n", s=4), after=[s])
                bank.free = [d]
                scored_sides[t, i] = d
        queries_done = unit.ready
        pq_done = s

        small = big[7][:, :]
        top_s = small[:, 0:32].rearrange("p (s k) -> p s k", s=2)
        top_i = small[:, 32:64].bitcast(U32).rearrange("p (s k) -> p s k", s=2)
        top_f = small[:, 64:96].rearrange("p (s k) -> p s k", s=2)
        best, pos = small[:, 96:112], small[:, 112:128].bitcast(U32)
        part_i = [small[:, 128 + 16 * i:144 + 16 * i].bitcast(U32) for i in range(2)]
        part_f = small[:, 160:192].rearrange("p (s k) -> p s k", s=2)
        place_f = [small[:, 192 + 16 * i:208 + 16 * i] for i in range(2)]
        cand = small[:, 256:512]
        onehot = small[:, 512:1024].rearrange("p (s k c) -> p s k c", s=2, k=PEER_TOPK)
        sel = big[8]
        expert = [sel[:, t * 128:(t + 1) * 128].bitcast(U32) for t in range(TT)]
        weight = [sel[:, 256 + t * 128:256 + (t + 1) * 128] for t in range(TT)]
        dot = [sel[:, 512 + t * 128:512 + (t + 1) * 128] for t in range(TT)]
        coef = [sel[:, 768 + t * 128:768 + (t + 1) * 128] for t in range(TT)]
        total = [sel[:, 1024 + t * 8:1032 + t * 8] for t in range(TT)]
        lowest = [sel[:, 1040 + t * 8:1048 + t * 8] for t in range(TT)]

        def top16(values, out_s, out_i, after):
            s = dve.do(nc.vector.max, out_s[:, 0:8], values, after=after)
            s = dve.do(nc.vector.max_index, out_i[:, 0:8], out_s[:, 0:8], values, after=[s])
            s = dve.do(nc.vector.match_replace, values, out_s[:, 0:8], values, -3.0e38,
                       after=[s])
            s = dve.do(nc.vector.max, out_s[:, 8:16], values, after=[s])
            return dve.do(nc.vector.max_index, out_i[:, 8:16], out_s[:, 8:16], values,
                          after=[s])

        chosen = {}
        previous = [x2_ready]

        def choose(t, h):
            s = previous[0]
            for side in range(2):
                s = top16(scores[t][:, 2 * h + side, :], top_s[:, side, :], top_i[:, side, :],
                          [s, scored_sides[t, h // 2]])
            s = dve.do(nc.vector.tensor_copy, top_f, top_i, after=[s])
            grid = [P, PEER_TOPK, PEER_TOPK]
            s = dve.do(nc.vector.tensor_tensor, cand.rearrange("p (i j) -> p i j", i=PEER_TOPK),
                       top_s[:, 0, :].unsqueeze(2).to_broadcast(grid),
                       top_s[:, 1, :].unsqueeze(1).to_broadcast(grid), ALU.add, after=[s])
            s = top16(cand, best, pos, [s])
            low, w = lowest[t][:, h:h + 1], weight[t][:, h * PEER_TOPK:(h + 1) * PEER_TOPK]
            s = dve.do(nc.vector.tensor_scalar, low, best[:, 0:1], -1.0, None, ALU.mult,
                       after=[s])
            exped = act.do(nc.scalar.activation, w, best, ACT.Exp, bias=low,
                           accum_out=total[t][:, h:h + 1], after=[s])
            for side, (op, by) in enumerate(((ALU.logical_shift_right, 4),
                                             (ALU.bitwise_and, PEER_TOPK - 1))):
                s1 = dve.do(nc.vector.tensor_scalar, part_i[side], pos, by, None, op, after=[s])
                s2 = dve.do(nc.vector.tensor_copy, part_f[:, side, :], part_i[side], after=[s1])
            for side in range(2):
                s = dve.do(nc.vector.tensor_tensor, onehot[:, side],
                           iota16[:, :].unsqueeze(1).to_broadcast(grid),
                           part_f[:, side, :].unsqueeze(2).to_broadcast(grid), ALU.is_equal,
                           after=[s2])
            for side in range(2):
                s1 = dve.do(nc.vector.tensor_tensor, onehot[:, side], onehot[:, side],
                            top_f[:, side, :].unsqueeze(1).to_broadcast(grid), ALU.mult,
                            after=[s])
            for side in range(2):
                s = dve.do(nc.vector.tensor_reduce, place_f[side], onehot[:, side], AX, ALU.add,
                           after=[s1])
            picked = dve.do(nc.vector.scalar_tensor_tensor,
                            out=expert[t][:, h * PEER_TOPK:(h + 1) * PEER_TOPK], in0=place_f[0],
                            scalar=float(PEER_KEYS), in1=place_f[1], op0=ALU.mult, op1=ALU.add,
                            after=[s])
            s = dve.do(nc.vector.reciprocal, total[t][:, h:h + 1], total[t][:, h:h + 1],
                       after=[exped, picked])
            previous[0] = s
            chosen[t, h] = picked, s

        flat = lambda ap: ap.rearrange("p k t -> p (k t)")
        rows = [(big[6][:, :], [x2_ready]), (flat(conv_acc[:, :, :]), [x2_ready]),
                (flat(conv_in[:, :, :])[:, 0:2 * D], [x2_ready]), (gates_w, [x2_ready])]
        rows += [(w_space[:, i * 2 * D:(i + 1) * 2 * D], [queries_done]) for i in range(6)]
        rows += [(big[i][:, :], [pq_done]) for i in range(2)]
        uv = Ring([Buffer(ap, load_counter(f"uv{i}")) for i, (ap, _) in enumerate(rows)])
        for b, (_, free) in zip(uv.buffers, rows):
            b.free = free
        diag = Ring([Buffer(actT[:, i // 2, (i % 2) * P:(i % 2 + 1) * P]) for i in range(8)])
        for b in diag.buffers:
            b.free = [queries_done]
        out_tm = out.rearrange("(t p) c -> p t c", p=P)
        c_out = load_counter("out")
        GROUP = 2
        heads = [(t, h) for t in range(TT) for h in range(PEER_HEADS)]
        y_unit = {}

        def dot_products(t, n):
            slot = uv.take()
            index = expert[t][:, n:n + 1]
            ready = pool.dma(nc.gpsimd.indirect_dma_start, out=slot.ap, out_offset=None,
                             in_=experts,
                             in_offset=bass.IndirectOffsetOnAxis(ap=index, axis=0),
                             counter=slot.counter,
                             after=[chosen[t, n // PEER_TOPK][0], *slot.free])
            junk = work.buffers[n % 2]
            s = dve.do(nc.vector.tensor_tensor_reduce, out=junk.ap[:, 0:D], in0=h3[:, t, :],
                       in1=slot.ap[:, 0:D], scale=1.0, scalar=0.0, op0=ALU.mult, op1=ALU.add,
                       accum_out=dot[t][:, n:n + 1], after=[ready, h3_ready, *junk.free])
            junk.free = [s]
            return t, n, slot, s

        def add_values(group):
            t, n0, _, _ = group[0]
            n1, h = n0 + len(group), n0 // PEER_TOPK
            g = act.do(nc.scalar.activation, coef[t][:, n0:n1], dot[t][:, n0:n1],
                       ACT.Gelu_apprx_tanh, after=[group[-1][3]])
            c = dve.do(nc.vector.scalar_tensor_tensor, out=coef[t][:, n0:n1],
                       in0=coef[t][:, n0:n1], scalar=total[t][:, h:h + 1],
                       in1=weight[t][:, n0:n1], op0=ALU.mult, op1=ALU.mult,
                       after=[g, chosen[t, h][1]])
            if t not in y_unit:
                y_unit[t] = units.take()
            unit = y_unit[t]
            for _, n, slot, _ in group:
                d = diag.take()
                s = act.do(nc.scalar.activation, d.ap, ident[:, :], ACT.Copy,
                           scale=coef[t][:, n:n + 1], after=[c, *d.free])
                after = [s, *unit.free]
                for half in range(2):
                    m = pe.do(nc.tensor.matmul, unit.ap[:, half * 512:(half + 1) * 512], d.ap,
                              slot.ap[:, D + half * 512:D + (half + 1) * 512], start=n == 0,
                              stop=n == PICKS - 1, after=after)
                    after = []
                d.free, slot.free = [m], [m]
            if n1 == PICKS:
                y = x_res[:, t, :]
                s = dve.do(nc.vector.tensor_tensor, y, unit.ap[:, :], y, ALU.add, after=[m])
                sp.dma(nc.sync.dma_start, out_tm[:, t, :], y, counter=c_out, after=[s])

        stage("choose_first")
        choose(*heads[0])
        choose(*heads[1])
        held = []
        for i, (t, h) in enumerate(heads):
            if h % 4 == 0:
                stage(f"retrieve_t{t}h{h}")
            for k in range(PEER_TOPK):
                held.append(dot_products(t, h * PEER_TOPK + k))
                if len(held) == 2 * GROUP:
                    add_values(held[:GROUP])
                    del held[:GROUP]
                if k == PEER_TOPK // 2 and i + 2 < len(heads):
                    choose(*heads[i + 2])
        while held:
            add_values(held[:GROUP])
            del held[:GROUP]

        queues = (pe, act, dve, pool, sp)
        for q in queues:
            q.number()
        with nc.Block() as block:
            @block.tensor
            def _(e):
                pe.emit(e)

            @block.scalar
            def _(e):
                act.emit(e)

            @block.vector
            def _(e):
                dve.emit(e)

            @block.gpsimd
            def _(e):
                pool.emit(e)

            @block.sync
            def _(e):
                sp.emit(e)
                e.wait_ge(c_out.sem, c_out.value)


def scored_all(o_ready):
    return o_ready[max(o_ready)]


def kernel(**inputs):
    import numpy as np
    import concourse.bacc as bacc
    from concourse.bass_utils import run_bass_kernel_spmd

    a = {n: np.asarray(x) for n, x in inputs.items()}

    def per_channel(name):
        return a[name].reshape(-1, P).T

    def halves(name):
        return np.concatenate([a[name].reshape(64, 1)] * 2, axis=0)

    def on_all(name):
        return np.broadcast_to(a[name].reshape(1, -1), (P, 64))

    def taps(name):
        k, c = a[name].shape[-2:]
        return a[name].reshape(k, c // P, P).transpose(2, 1, 0).reshape(P, -1)

    pack = {}
    for name, n in VECTORS:
        if name in ("conv_dw", "conv_w_2"):
            pack[name] = taps(name)
        elif name.startswith("lambda_"):
            pack[name] = on_all(name)
        elif a[name].size == 64:
            pack[name] = halves(name)
        else:
            pack[name] = per_channel(name)
        assert pack[name].shape == (P, n), name
    arrays = {
        "x": a["x"][0], "mem": a["mem"][0],
        "vectors": np.concatenate([pack[n] for n, _ in VECTORS], axis=1),
        "w_in": a["w_in"][0], "w_conv_proj": a["w_conv_proj"][0],
        "w_diff_proj": a["w_diff_proj"][0], "w_mem_kv": a["w_mem_kv"][0],
        "w_x_proj": a["w_x_proj"][0], "w_out": a["w_out"][0], "w_in_2": a["w_in_2"][0],
        "rg_w_a": a["rg_w_a_2"][0], "rg_w_x": a["rg_w_x_2"][0], "w_out_2": a["w_out_2"][0],
        "norm_ffn": np.broadcast_to(a["norm_ffn_2"][0].reshape(1, D), (P, D)),
        "w_query": a["peer_w_query_2"][0].reshape(D, PEER_SIDES * P),
        "sub_keys_t": a["peer_sub_keys_2"][0].reshape(PEER_SIDES, PEER_KEYS, P).transpose(2, 0, 1),
        "experts": np.concatenate([a["peer_u_2"][0], a["peer_v_2"][0]], axis=1),
    }
    arrays = {f"in_{n}": np.ascontiguousarray(x) for n, x in arrays.items()}
    nc = bacc.Bacc("TRN2", target_bir_lowering=False, num_devices=1)
    aps = [nc.dram_tensor(n, x.shape, mybir.dt.from_np(x.dtype), kind="ExternalInput").ap()
           for n, x in arrays.items()]
    out = nc.dram_tensor("out_x", [T, D], F32, kind="ExternalOutput").ap()
    build(nc, *aps, out)
    r = run_bass_kernel_spmd(nc, [arrays], core_ids=[0])
    return r.results[0]["out_x"].reshape(1, T, D)
```

```python
from contextlib import ExitStack

import concourse.bass as bass
from concourse import mybir

P = 128
F32 = mybir.dt.float32
F32R = mybir.dt.float32r
U32 = mybir.dt.uint32
ALU = mybir.AluOpType
ACT = mybir.ActivationFunctionType
AX = mybir.AxisListType.X

T = 256
TT = T // P
D = 1024
KT = D // P
SLOT = 512
PIECE = 256
PIECES = SLOT // PIECE
CONV_K = 31
DIFF_HEADS = 8
DIFF_HEAD_DIM = 64
LAMBDA_INIT = 0.2
X_HEADS = 4
X_HEAD_DIM = D // X_HEADS
SB_HEADS = 8
SB_HEAD_DIM = 64
D_SB = SB_HEADS * SB_HEAD_DIM
D_RG = D - D_SB
RG_TILES = D_RG // P
RG_WIDTH = 4
PEER_HEADS = 8
PEER_KEYS = 128
PEER_TOPK = 16
PEER_SIDES = 2 * PEER_HEADS
PICKS = PEER_HEADS * PEER_TOPK
MASKED = -1.0e30

VECTORS = [("norm_g", KT), ("mem_norm_g", KT), ("conv_dw", KT * CONV_K), ("conv_dw_b", KT),
           ("conv_ln_g", KT), ("conv_ln_b", KT), ("diff_qn_g", 1), ("diff_kn_g", 1),
           ("lambda_q1", 64), ("lambda_k1", 64), ("lambda_q2", 64), ("lambda_k2", 64),
           ("diff_subln_g", 1), ("x_qn_g", 2), ("x_kn_g", 2), ("norm_mix_2", KT),
           ("q_norm_2", 1), ("k_norm_2", 1), ("conv_w_2", RG_TILES * RG_WIDTH),
           ("conv_b_2", RG_TILES), ("rg_b_a_2", RG_TILES), ("rg_b_x_2", RG_TILES),
           ("rg_lambda_2", RG_TILES), ("out_norm_sb_2", D_SB // P), ("out_norm_rg_2", RG_TILES)]
VECTOR_AT = {}
for _name, _n in VECTORS:
    VECTOR_AT[_name] = (sum(n for _, n in VECTORS[:len(VECTOR_AT)]), _n)
VECTOR_COLS = sum(n for _, n in VECTORS)


class Counter:

    def __init__(self, sem):
        self.sem, self.value = sem, 0


class Step:

    def __init__(self, counter):
        self.counter, self.value, self.waited = counter, None, False


class Queue:

    def __init__(self, name, semaphore):
        self.name, self.semaphore, self.items, self.counter = name, semaphore, [], None

    def stage(self, name):
        self.counter = Counter(self.semaphore(f"{self.name}_{name}"))

    def do(self, instruction, *args, after=(), **named):
        step = Step(self.counter)
        return self.put(step, 1, instruction, args, named, after)

    def dma(self, instruction, *args, counter, after=(), **named):
        step = Step(counter)
        step.waited = True
        return self.put(step, 16, instruction, args, named, after)

    def put(self, step, by, instruction, args, named, after):
        for a in after:
            a.waited = True
        self.items.append((list(after), instruction, args, named, step, by))
        return step

    def number(self):
        for *_, step, by in self.items:
            if step.waited:
                step.counter.value += by
                step.value = step.counter.value

    def emit(self, engine):
        reached = {}
        for after, instruction, args, named, step, by in self.items:
            need = {}
            for a in after:
                need[id(a.counter)] = max(need.get(id(a.counter), (0, None))[0], a.value), a.counter
            for key, (value, counter) in need.items():
                if reached.get(key, 0) < value:
                    engine.wait_ge(counter.sem, value)
                    reached[key] = value
            issued = instruction(*args, **named)
            if step.waited:
                issued.then_inc(step.counter.sem, by)


class Buffer:

    def __init__(self, ap, counter=None):
        self.ap, self.counter, self.free = ap, counter, []


class Ring:

    def __init__(self, buffers):
        self.buffers = buffers

    def take(self):
        taken = self.buffers.pop(0)
        self.buffers.append(taken)
        return taken


def build(nc, x, mem, vectors, w_in, w_conv_proj, w_diff_proj, w_mem_kv, w_x_proj, w_out,
          w_in_2, rg_w_a, rg_w_x, w_out_2, norm_ffn, w_query, sub_keys_t, experts, out):
    with ExitStack() as ctx:
        def sb(name, shape, dt=F32):
            return ctx.enter_context(nc.sbuf_tensor(name, [P, *shape], dt))

        def semaphore(name):
            return ctx.enter_context(nc.semaphore(name))

        pe, act, dve, pool, sp = (Queue(n, semaphore) for n in ("pe", "act", "dve", "pool", "sp"))

        def stage(name):
            for q in (pe, act, dve, pool):
                q.stage(name)

        def load_counter(name):
            return Counter(semaphore(f"load_{name}"))

        stage("setup")

        w_raw = Ring([Buffer(sb(f"w_raw{i}", [KT, PIECE]), load_counter(f"w{i}"))
                      for i in range(2)])
        vec = sb("vec", [VECTOR_COLS])
        conv_in = sb("conv_in", [KT, CONV_K - 1 + T])
        conv_acc = sb("conv_acc", [KT, T])
        big = [sb(f"big{i}", [KT * T]) for i in range(8)]
        work = Ring([Buffer(sb(f"work{i}", [4 * T])) for i in range(3)])
        probs = Ring([Buffer(sb(f"probs{i}", [2, 384])) for i in range(2)])
        probs_t = Ring([Buffer(sb(f"probs_t{i}", [512])) for i in range(2)])
        ident = sb("ident", [P])
        ones = sb("ones", [P])
        ones64 = sb("ones64", [P])
        later = sb("later", [P])
        before = sb("before", [P])
        dist = sb("dist", [384])
        iota16 = sb("iota16", [PEER_TOPK])
        col = sb("col", [128])
        def split_pair(space, name, columns):
            return Buffer(tuple(space.enter_context(
                nc.sbuf_tensor(f"{name}_{part}", [P, KT, columns], F32R)) for part in ("hi", "lo")))

        w_split = Ring([split_pair(ctx, f"w{i}", PIECE) for i in range(3)])
        pair1 = split_pair(ctx, "in1", T)
        pair0_space = ctx.enter_context(ExitStack())
        pair0 = split_pair(pair0_space, "in0", T)
        pairs = Ring([pair0, pair1])
        for pair in (pair0, pair1):
            pair.order = list(range(KT))

        units = Ring([Buffer(ctx.enter_context(nc.psum_tensor(f"unit{i}", [P, 1024], F32)))
                      for i in range(3)])
        banks = Ring([Buffer(ctx.enter_context(nc.psum_tensor(f"bank{i}", [P, 512], F32)))
                      for i in range(2)])

        def cm(b):
            return b[:, :].rearrange("p (k t) -> p k t", k=KT)

        def tm(b):
            return b[:, :].rearrange("p (t c) -> p t c", t=TT)

        def v(name, i=0, n=1):
            at = VECTOR_AT[name][0]
            return vec[:, at + i:at + i + n]

        EPS6, EPS5, ONE = (col[:, i:i + 1] for i in range(3))
        LAM = col[:, 8:9]
        used = [12]

        def cols(n):
            used[0] += n
            return col[:, used[0] - n:used[0]]

        weight_order = []
        for w, first, slots in (
                *[(w_in, c + i * SLOT, 1) for i in range(2) for c in (0, D)],
                *[(w_in, 3 * D + c + i * SLOT, 1) for i in range(2) for c in (0, D, 2 * D)],
                (w_in, 7 * D, 2), (w_mem_kv, 0, 4), (w_in, 9 * D, 6), (w_in, 6 * D, 2),
                (w_in, 8 * D, 2), (w_in, 2 * D, 2), (w_diff_proj, 0, 2), (w_x_proj, 0, 2),
                (w_conv_proj, 0, 2), (w_out, 0, 2), (w_in_2, 0, 2), (w_in_2, 3 * D_SB, 1),
                (w_in_2, 2 * D_SB, 1), (w_in_2, 3 * D_SB + D_RG, 1), (w_out_2, 0, 2), (w_query, 0, 4)):
            weight_order += [(w, first + i * PIECE) for i in range(slots * PIECES)]
        prepared = []
        taken = [0]
        beside, BESIDE_STEPS = [], 6

        def prepare_weights():
            w, column = weight_order[taken[0]]
            taken[0] += 1
            raw, split = w_raw.take(), w_split.take()
            hi, lo = split.ap
            loaded = sp.dma(nc.sync.dma_start, raw.ap[:, :, :],
                            w.rearrange("(k p) n -> p k n", p=P)[:, :, column:column + PIECE],
                            counter=raw.counter, after=raw.free)
            s = act.do(nc.scalar.copy, hi[:, :, :], raw.ap[:, :, :], after=[loaded, *split.free])
            s = dve.do(nc.vector.tensor_tensor, lo[:, :, :], raw.ap[:, :, :],
                       hi[:, :, :].bitcast(F32), ALU.subtract, after=[s, loaded])
            raw.free, split.free, split.ready = [s], [], s
            split.source = w, column
            prepared.append(split)

        def next_piece(w, column):
            while len(prepared) < 3 and taken[0] < len(weight_order):
                prepare_weights()
            piece = prepared.pop(0)
            assert piece.source[0] is w and piece.source[1] == column
            convolve_some(3)
            for _ in range(BESIDE_STEPS):
                if beside:
                    if next(beside[0], "done") == "done":
                        beside.pop(0)
            return piece

        def split_input(src, ready):
            pair = pairs.take()
            hi, lo = pair.ap
            pair.ready = []
            for i in range(4):
                k = slice(2 * i, 2 * i + 2)
                s = act.do(nc.scalar.copy, hi[:, k, :], src[:, k, :],
                           after=[ready[i // 2], *pair.free])
                s = dve.do(nc.vector.tensor_tensor, lo[:, k, :], src[:, k, :],
                           hi[:, k, :].bitcast(F32), ALU.subtract, after=[s, ready[i // 2]])
                pair.ready += [s, s]
            pair.free = []
            return pair

        x_tm, mem_tm = tm(big[3]), tm(big[7])
        x_in = x.rearrange("(t p) c -> p t c", p=P)
        mem_in = mem.rearrange("(t p) c -> p t c", p=P)
        c_x, c_vec, c_mem = load_counter("x"), load_counter("vec"), load_counter("mem")
        x_ready = act.dma(nc.scalar.dma_start, x_tm, x_in, counter=c_x)
        vec_ready = act.dma(nc.scalar.dma_start, vec[:, :], vectors, counter=c_vec)

        s = dve.do(nc.vector.memset, col[:, :], 0.0)
        for ap, value in ((EPS6, 1e-6), (EPS5, 1e-5), (ONE, 1.0)):
            const_ready = dve.do(nc.vector.memset, ap, value, after=[s])
        ones_ready = dve.do(nc.vector.memset, ones[:, :], 1.0)
        s = dve.do(nc.vector.memset, ones64[:, :], 0.0)
        dve.do(nc.vector.memset, ones64[0:64, 0:64], 1.0, after=[s])
        ones64_ready = dve.do(nc.vector.memset, ones64[64:128, 64:128], 1.0, after=[s])
        conv_pad = dve.do(nc.vector.memset, conv_in[:, :, 0:CONV_K - 1], 0.0)

        s = pool.do(nc.gpsimd.memset, ident[:, :], 0.0)
        ident_ready = pool.do(nc.gpsimd.affine_select,
            out=ident[:, :], in_=ident[:, :], compare_op=ALU.not_equal, fill=1.0, base=0,
            pattern=[[-1, P]], channel_multiplier=1, after=[s])
        s = pool.do(nc.gpsimd.memset, later[:, :], 1.0)
        pool.do(nc.gpsimd.affine_select, out=later[:, :], in_=later[:, :], compare_op=ALU.is_gt,
                                          fill=0.0, base=0, pattern=[[-1, P]],
                                          channel_multiplier=1, after=[s])
        s = pool.do(nc.gpsimd.memset, before[:, :], 1.0)
        pool.do(nc.gpsimd.affine_select, out=before[:, :], in_=before[:, :], compare_op=ALU.is_gt,
                                          fill=0.0, base=0, pattern=[[1, P]],
                                          channel_multiplier=-1, after=[s])
        s = pool.do(nc.gpsimd.iota, dist[:, 0:256], [[1, 256]], base=-P, channel_multiplier=-1,
                                     allow_small_or_imprecise_dtypes=True)
        s = pool.do(nc.gpsimd.iota, dist[:, 256:384], [[1, P]], base=0, channel_multiplier=-1,
                                     allow_small_or_imprecise_dtypes=True, after=[s])
        s = pool.do(nc.gpsimd.affine_select,
            out=dist[:, 0:256], in_=dist[:, 0:256], compare_op=ALU.is_ge, fill=MASKED, base=P,
            pattern=[[-1, 256]], channel_multiplier=1, after=[s])
        s = pool.do(nc.gpsimd.affine_select,
            out=dist[:, 256:384], in_=dist[:, 256:384], compare_op=ALU.is_ge, fill=MASKED, base=0,
            pattern=[[-1, P]], channel_multiplier=1, after=[s])
        pool_consts = pool.do(nc.gpsimd.iota, iota16[:, :], [[1, PEER_TOPK]], base=0,
                                               channel_multiplier=0,
                                               allow_small_or_imprecise_dtypes=True, after=[s])

        conv_done, taps_left, POOL_TILES = {}, [], (3, 4, 5, 6, 7)

        def convolve_some(n):
            for _ in range(min(n, len(taps_left))):
                k, t = taps_left.pop(0)
                dst, src = conv_acc[:, t, :], conv_in[:, t, k:k + T]
                tap = v("conv_dw", t * CONV_K + k)
                if k == 0:
                    conv_done[t] = dve.do(nc.vector.tensor_scalar, dst, src, tap,
                                          v("conv_dw_b", t), ALU.mult, ALU.add,
                                          after=[u_ready[t // 4], gains_ready])
                else:
                    conv_done[t] = dve.do(nc.vector.scalar_tensor_tensor, out=dst, in0=src,
                                          scalar=tap, in1=dst, op0=ALU.mult, op1=ALU.add,
                                          after=[conv_done[t]])

        def convolve_on_pool(tiles, spaces):
            for k in range(CONV_K):
                for t, product in zip(tiles, spaces):
                    dst, src = conv_acc[:, t, :], conv_in[:, t, k:k + T]
                    tap = v("conv_dw", t * CONV_K + k)
                    if k == 0:
                        conv_done[t] = pool.do(nc.gpsimd.tensor_scalar, dst, src, tap,
                                               v("conv_dw_b", t), ALU.mult, ALU.add,
                                               after=[u_ready[t // 4], gains_ready, *xT.ready])
                        continue
                    s = pool.do(nc.gpsimd.tensor_scalar, product, src, tap, 1.0, ALU.mult,
                                ALU.mult, after=[conv_done[t]])
                    conv_done[t] = pool.do(nc.gpsimd.tensor_tensor, dst, dst, product, ALU.add,
                                           after=[s])

        def project(w, column, pair, token_major=False, between=()):
            unit = units.take()
            in_hi, in_lo = pair.ap
            for piece_no in range(PIECES):
                piece = next_piece(w, column + piece_no * PIECE)
                w_hi, w_lo = piece.ap
                order = [(j, k) for j in range(2) for k in pair.order]
                if token_major:
                    order = [(j, k) for k in pair.order for j in range(2)]
                for j, k in order:
                    rows = slice(j * P, (j + 1) * P)
                    at = j * SLOT + piece_no * PIECE if token_major else (2 * piece_no + j) * T
                    for n, (w_part, in_part) in enumerate(((w_hi, in_hi), (w_hi, in_lo),
                                                           (w_lo, in_hi))):
                        if token_major:
                            fixed, moving = in_part[:, k, rows], w_part[:, k, :]
                        else:
                            fixed, moving = w_part[:, k, rows], in_part[:, k, :]
                        s = pe.do(nc.tensor.matmul, unit.ap[:, at:at + 256], fixed, moving,
                                  start=k == pair.order[0] and n == 0,
                                  stop=k == pair.order[-1] and n == 2,
                                  after=[*unit.free, piece.ready, pair.ready[k]])
                piece.free = [s]
                if piece_no == 0:
                    for f in between:
                        f()
            pair.free, unit.ready, unit.free = [s], s, []
            return unit

        def tiles4(ap):
            return ap.rearrange("p (j t) -> p j t", j=4)

        def rsqrt_of(out_ap, in_ap, mean_over, eps, after, wide=False):
            s = act.do(nc.scalar.activation, out_ap, in_ap, ACT.Ln if wide else ACT.Sqrt,
                       bias=eps, scale=1.0 / mean_over, after=[*after, const_ready])
            if wide:
                return s, act.do(nc.scalar.activation, out_ap, out_ap, ACT.Exp, scale=-0.5,
                                 after=[s])
            return s, dve.do(nc.vector.reciprocal, out_ap, out_ap, after=[s])

        def inverse_rms(src, ready):
            halves, ss = cols(2 * TT).rearrange("p (h t) -> p h t", h=2), cols(TT)
            junk = [work.take(), work.take()]
            for half in range(2):
                c = slice(half * SLOT, (half + 1) * SLOT)
                s = dve.do(nc.vector.tensor_tensor_reduce,
                    out=junk[0].ap[:, c], in0=src[:, 0, c], in1=src[:, 0, c], scale=1.0,
                    scalar=0.0, op0=ALU.mult, op1=ALU.add, accum_out=halves[:, half, 0:1],
                    after=[*ready[half], *junk[0].free, const_ready])
                s2 = act.do(nc.scalar.activation, junk[1].ap[:, c], src[:, 1, c], ACT.Square,
                            accum_out=halves[:, half, 1:2],
                            after=[*ready[half], *junk[1].free, const_ready])
            junk[0].free, junk[1].free = [s], [s2]
            s = dve.do(nc.vector.tensor_tensor, ss, halves[:, 0, :], halves[:, 1, :], ALU.add,
                       after=[s, s2])
            return ss, rsqrt_of(ss, ss, D, EPS6, [s])[1]

        def scale_tokens(dst, src, ss, ready):
            done = []
            for half in range(2):
                c = slice(half * SLOT, (half + 1) * SLOT)
                done.append([
                    dve.do(nc.vector.tensor_scalar, dst[:, 0, c], src[:, 0, c], ss[:, 0:1], None,
                           ALU.mult, after=ready),
                    act.do(nc.scalar.activation, dst[:, 1, c], src[:, 1, c], ACT.Copy,
                           scale=ss[:, 1:2], after=ready)])
            return done

        def turn_input(src, ready, gain=None):
            pair = pairs.take()
            hi, lo = pair.ap
            pair.ready = []
            for half in range(2):
                unit = units.take()
                for bank in range(2):
                    after = [*ready[half], *unit.free, ident_ready]
                    k0 = 4 * half + 2 * bank
                    for j in range(2):
                        for t in range(TT):
                            at = (2 * bank + j) * T + t * P
                            s = pe.do(nc.tensor.transpose, unit.ap[:, at:at + P],
                                      src[:, t, (k0 + j) * P:(k0 + j + 1) * P], ident[:, :],
                                      after=after)
                            after = []
                    turned = [unit.ap[:, (2 * bank + j) * T:(2 * bank + j + 1) * T]
                              for j in range(2)]
                    if gain is None:
                        both = unit.ap[:, bank * 512:(bank + 1) * 512]
                        both = both.rearrange("p (j t) -> p j t", j=2)
                        k = slice(k0, k0 + 2)
                        s = act.do(nc.scalar.copy, hi[:, k, :], both, after=[s, *pair.free])
                        s = dve.do(nc.vector.tensor_tensor, lo[:, k, :], both,
                                   hi[:, k, :].bitcast(F32), ALU.subtract, after=[s])
                    else:
                        for j in range(2):
                            d = act.do(nc.scalar.activation, hi[:, k0 + j, :], turned[j],
                                       ACT.Copy, scale=v(gain, k0 + j),
                                       after=[s, vec_ready, *pair.free])
                        for j in range(2):
                            s = dve.do(nc.vector.scalar_tensor_tensor, out=lo[:, k0 + j, :],
                                       in0=turned[j], scalar=v(gain, k0 + j),
                                       in1=hi[:, k0 + j, :].bitcast(F32), op0=ALU.mult,
                                       op1=ALU.subtract, after=[d])
                    pair.ready += [s, s]
                unit.free = [s]
            pair.free = []
            return pair

        def sum_over_channels(sq, ready, weights, groups, width, unit):
            after = [*ready, *unit.free, ones64_ready]
            for g, members in enumerate(groups):
                for i, a in enumerate(members):
                    s = pe.do(nc.tensor.matmul,
                        unit.ap[:, g * width:(g + 1) * width], weights[:, :],
                        sq[:, a * width:(a + 1) * width], start=i == 0, stop=i == len(members) - 1,
                        after=after)
                    after = []
            unit.free = []
            return s

        stage("input")
        prepare_weights()
        ss, s = inverse_rms(x_tm, [[x_ready]] * 2)
        xT = turn_input(x_tm, scale_tokens(x_tm, x_tm, ss, [s]), "norm_g")
        prepare_weights()
        mem_ready = act.dma(nc.scalar.dma_start, mem_tm, mem_in, counter=c_mem)

        dots = cols(2)
        for i, (a, b) in enumerate((("lambda_q1", "lambda_k1"), ("lambda_q2", "lambda_k2"))):
            junk = work.buffers[0].ap
            s = dve.do(nc.vector.tensor_tensor_reduce,
                out=junk[:, 64 * i:64 * i + 64], in0=v(a, 0, 64), in1=v(b, 0, 64), scale=1.0,
                scalar=0.0, op0=ALU.mult, op1=ALU.add, accum_out=dots[:, i:i + 1],
                after=[vec_ready, *work.buffers[0].free])
        work.buffers[0].free = [s]
        s = act.do(nc.scalar.activation, dots, dots, ACT.Exp, after=[s])
        lam_ready = dve.do(nc.vector.scalar_tensor_tensor,
            out=LAM, in0=dots[:, 0:1], scalar=LAMBDA_INIT, in1=dots[:, 1:2], op0=ALU.add,
            op1=ALU.subtract, after=[s, const_ready])
        qg, subln_g, xq_g, q2_g = cols(1), cols(1), cols(2), cols(1)
        half_dw = vec[:, VECTOR_AT["conv_dw"][0]:VECTOR_AT["conv_dw"][0] + KT * CONV_K]
        for dst, src, by in ((qg, v("diff_qn_g"), DIFF_HEAD_DIM ** -0.5),
                             (subln_g, v("diff_subln_g"), 0.5 * (1.0 - LAMBDA_INIT)),
                             (xq_g, v("x_qn_g", 0, 2), X_HEAD_DIM ** -0.5),
                             (q2_g, v("q_norm_2"), SB_HEAD_DIM ** -0.5),
                             (half_dw, half_dw, 0.5)):
            gains_ready = dve.do(nc.vector.tensor_scalar,
                dst, src, by, None, ALU.mult, after=[vec_ready, const_ready])

        stage("glu")
        u_ready = []
        for i in range(2):
            ua, ub = project(w_in, i * SLOT, xT), project(w_in, D + i * SLOT, xT)
            th = work.take()
            s = act.do(nc.scalar.activation, th.ap[:, :], ub.ap[:, :], ACT.Tanh,
                                                            scale=0.5, after=[ub.ready, *th.free])
            ub.free = [s]
            s = dve.do(nc.vector.scalar_tensor_tensor,
                out=conv_in[:, 4 * i:4 * i + 4, CONV_K - 1:], in0=tiles4(th.ap[:, :]), scalar=1.0,
                in1=tiles4(ua.ap[:, :]), op0=ALU.add, op1=ALU.mult,
                after=[s, ua.ready, conv_pad])
            ua.free, th.free = [s], [s]
            u_ready.append(s)

        def head_norm(unit, dst, weights, mean_over, gain, per_head):
            sq = work.take()
            copied = act.do(nc.scalar.copy, dst, tiles4(unit.ap[:, :]), after=[unit.ready])
            unit.free = [copied]
            squared = act.do(nc.scalar.activation, tiles4(sq.ap[:, :]), dst, ACT.Square,
                             after=[copied, *sq.free])

            def finish():
                sums = units.take()
                if per_head == 1:
                    s = sum_over_channels(sq.ap, [squared], weights, [[0], [1]], 512, sums)
                    n = 4 * T
                else:
                    s = sum_over_channels(sq.ap, [squared], weights, [[0, 1], [2, 3]], T, sums)
                    n = 2 * T
                s, root = rsqrt_of(sq.ap[:, 0:n], sums.ap[:, 0:n], mean_over, EPS6, [s],
                                   wide=True)
                sums.free = [s]
                for j in range(per_head):
                    part = dst[:, j:4:per_head, :]
                    s = dve.do(nc.vector.scalar_tensor_tensor, out=part, in0=part,
                               scalar=gain[:, j:j + 1],
                               in1=sq.ap[:, 0:n].rearrange("p (g t) -> p g t", t=T),
                               op0=ALU.mult, op1=ALU.mult, after=[copied, root, gains_ready])
                sq.free = [s]
                return s
            return finish

        q_cm, k_cm, v_tm = cm(big[0]), cm(big[1]), tm(big[2])
        xq_cm, xk_cm, xv_tm = cm(big[4]), cm(big[5]), tm(big[6])
        COL_CGATE, COL_Q, COL_K, COL_V = 2 * D, 3 * D, 4 * D, 5 * D
        COL_DGATE, COL_XQ, COL_XGATE, COL_MERGE = 6 * D, 7 * D, 8 * D, 9 * D

        def values_slot(unit, dst):
            s = act.do(nc.scalar.copy, dst, unit.ap[:, :].rearrange("p (t c) -> p t c", t=TT),
                       after=[unit.ready])
            unit.free = [s]
            return s

        taps_left += [(k, t) for k in range(CONV_K) for t in range(KT) if t not in POOL_TILES]
        places = [big[3][:, i * T:(i + 1) * T] for i in range(2)]
        convolve_on_pool(POOL_TILES[0:2], places)
        convolve_on_pool(POOL_TILES[2:4], places)
        convolve_on_pool(POOL_TILES[4:], places)

        stage("diff_attention")
        o_ready = {}
        scored = {}

        def diff_scores(h):
            slope = 2.0 ** (-8.0 * (h + 1) / DIFF_HEADS)
            unit, p = units.take(), probs.take()
            after = [q_ready[h // 4], k_ready[h // 4], *unit.free]
            for m in range(2):
                rows = slice(64 * m, 64 * m + 64)
                for qt, width, at in ((1, 2 * P, 0), (0, P, 2 * P)):
                    s = pe.do(nc.tensor.matmul,
                        unit.ap[:, 512 * m + at:512 * m + at + width],
                        q_cm[rows, h, qt * P:(qt + 1) * P], k_cm[rows, h, 0:width],
                        start=True, stop=True, after=after)
                    after = []
            scores = unit.ap[:, :].rearrange("p (m c) -> p m c", m=2)[:, :, 0:384]
            s = dve.do(nc.vector.scalar_tensor_tensor,
                out=p.ap[:, :, :], in0=dist[:, :].unsqueeze(1).to_broadcast([P, 2, 384]),
                scalar=slope, in1=scores, op0=ALU.mult, op1=ALU.add,
                after=[s, *p.free, pool_consts])
            unit.free = [s]
            small = p.small
            top, total, inv, inv_lam = (small[:, i:i + 4] for i in (0, 4, 8, 12))
            wide, narrow = p.ap[:, :, 0:256], p.ap[:, :, 256:384]
            dve.do(nc.vector.tensor_reduce, top[:, 0:2], wide, AX, ALU.max, after=[s])
            s = dve.do(nc.vector.tensor_reduce, top[:, 2:4], narrow, AX, ALU.max, after=[s])
            s = dve.do(nc.vector.tensor_scalar, top, top, -1.0, None, ALU.mult, after=[s])
            for i, part in ((0, wide), (2, narrow)):
                for m in range(2):
                    e1 = act.do(nc.scalar.activation,
                        part[:, m, :], part[:, m, :], ACT.Exp, bias=top[:, i + m:i + m + 1],
                        accum_out=total[:, i + m:i + m + 1], after=[s])
            s = dve.do(nc.vector.reciprocal, inv, total, after=[e1])
            s = dve.do(nc.vector.tensor_scalar, inv_lam, inv, LAM, None, ALU.mult,
                       after=[s, lam_ready])
            for i, part in ((0, wide), (2, narrow)):
                s2 = dve.do(nc.vector.tensor_scalar,
                    part[:, 1, :], part[:, 1, :], inv_lam[:, i + 1:i + 2], None, ALU.mult,
                    after=[s])
                s3 = dve.do(nc.vector.scalar_tensor_tensor,
                    out=part[:, 0, :], in0=part[:, 0, :], scalar=inv[:, i:i + 1],
                    in1=part[:, 1, :], op0=ALU.mult, op1=ALU.subtract, after=[s2])
            scored[h] = p, s3

        def diff_turn(h):
            p, ready = scored[h]
            bank, pt = banks.take(), probs_t.take()
            after = [ready, *bank.free, ident_ready]
            for dst, src in ((0, 256), (P, 0), (2 * P, P)):
                s = pe.do(nc.tensor.transpose,
                    bank.ap[:, dst:dst + P], p.ap[:, 0, src:src + P], ident[:, :], after=after)
                after = []
            p.free = [s]
            s = act.do(nc.scalar.copy, pt.ap[:, 0:384], bank.ap[:, 0:384], after=[s, *pt.free])
            bank.free = [s]
            scored[h] = pt, s

        def diff_values(h):
            pt, ready = scored[h]
            bank = banks.take()
            vh = v_tm[:, :, h * P:(h + 1) * P]
            pe.do(nc.tensor.matmul, bank.ap[:, 0:256], vh[:, 0, :], pt.ap[:, 0:256], start=True,
                                     stop=False, after=[ready, v_ready[h // 4], *bank.free])
            s = pe.do(nc.tensor.matmul, bank.ap[:, P:256], vh[:, 1, :], pt.ap[:, 256:384],
                                         start=False, stop=True)
            pt.free = [s]
            s = act.do(nc.scalar.copy, q_cm[:, h, :], bank.ap[:, 0:256], after=[s])
            bank.free = [s]
            o_ready[h] = s

        def diff_norm(i):
            o = q_cm[:, 4 * i:4 * i + 4, :]
            sq = work.take()
            ready = [o_ready[h] for h in range(4 * i, 4 * i + 4)]
            squared = act.do(nc.scalar.activation, tiles4(sq.ap[:, :]), o, ACT.Square,
                             after=[*ready, *sq.free])

            def finish():
                sums = units.take()
                s = sum_over_channels(sq.ap, [squared], ones, [[0], [1]], 512, sums)
                s, root = rsqrt_of(sq.ap[:, :], sums.ap[:, :], P, EPS6, [s], wide=True)
                sums.free = [s]
                s = dve.do(nc.vector.scalar_tensor_tensor, out=o, in0=o, scalar=subln_g,
                           in1=tiles4(sq.ap[:, :]), op0=ALU.mult, op1=ALU.mult,
                           after=[*ready, root, gains_ready])
                sq.free = [s]
                return s
            return finish

        for i, p in enumerate(probs.buffers):
            p.small = cols(16)

        xq_ready, xk_ready, xv_ready, diff_normed = [None] * 2, [None] * 2, [], [None] * 2

        def cross_scores(h):
            unit, p = units.take(), probs.take()
            after = [xq_ready[h // 2], xk_ready[h // 2], *unit.free]
            for qt in range(TT):
                for j in range(2):
                    s = pe.do(nc.tensor.matmul,
                        unit.ap[:, qt * T:(qt + 1) * T], xq_cm[:, 2 * h + j, qt * P:(qt + 1) * P],
                        xk_cm[:, 2 * h + j, :], start=j == 0, stop=j == 1, after=after)
                    after = []
            small = p.small
            top, total = small[:, 0:2], small[:, 4:6]
            flat = p.ap[:, :, :].rearrange("p a b -> p (a b)")[:, 0:2 * T]
            s = dve.do(nc.vector.tensor_reduce,
                top, unit.ap[:, 0:2 * T].rearrange("p (q k) -> p q k", q=2), AX, ALU.max,
                after=[s, *p.free])
            s = dve.do(nc.vector.tensor_scalar, top, top, -1.0, None, ALU.mult, after=[s])
            for qt in range(TT):
                e1 = act.do(nc.scalar.activation,
                    flat[:, qt * T:(qt + 1) * T], unit.ap[:, qt * T:(qt + 1) * T], ACT.Exp,
                    bias=top[:, qt:qt + 1], accum_out=total[:, qt:qt + 1], after=[s])
            unit.free = [e1]
            s = dve.do(nc.vector.reciprocal, total, total, after=[e1])
            for qt in range(TT):
                s2 = dve.do(nc.vector.tensor_scalar,
                    flat[:, qt * T:(qt + 1) * T], flat[:, qt * T:(qt + 1) * T],
                    total[:, qt:qt + 1], 0.5, ALU.mult, ALU.mult, after=[s])
            scored["x", h] = p, flat, s2

        def cross_turn(h):
            p, flat, ready = scored["x", h]
            bank, pt = banks.take(), probs_t.take()
            after = [ready, *bank.free]
            for kt in range(2):
                for qt in range(TT):
                    s = pe.do(nc.tensor.transpose,
                        bank.ap[:, kt * T + qt * P:kt * T + (qt + 1) * P],
                        flat[:, qt * T + kt * P:qt * T + (kt + 1) * P], ident[:, :], after=after)
                    after = []
            p.free = [s]
            s = act.do(nc.scalar.copy, pt.ap[:, :], bank.ap[:, :], after=[s, *pt.free])
            bank.free = [s]
            scored["x", h] = pt, s

        def cross_values(h):
            pt, ready = scored["x", h]
            bank = banks.take()
            after = [ready, xv_ready[h // 2], *bank.free]
            for j in range(2):
                for kt in range(2):
                    s = pe.do(nc.tensor.matmul,
                        bank.ap[:, j * T:(j + 1) * T],
                        xv_tm[:, kt, (2 * h + j) * P:(2 * h + j + 1) * P],
                        pt.ap[:, kt * T:(kt + 1) * T], start=kt == 0, stop=kt == 1, after=after)
                    after = []
            pt.free = [s]
            s = act.do(nc.scalar.copy, xq_cm[:, 2 * h:2 * h + 2, :],
                       bank.ap[:, :].rearrange("p (j t) -> p j t", j=2), after=[s])
            bank.free = [s]
            return s

        merge = [cm(big[1]), cm(big[2]), cm(big[7])]
        merge_ready = {}

        def merge_slot(i, unit):
            s = act.do(nc.scalar.activation, merge[i // 2][:, 4 * (i % 2):4 * (i % 2) + 4, :],
                       tiles4(unit.ap[:, :]), ACT.Tanh, scale=0.5,
                       after=[unit.ready, o_ready[7]])
            unit.free = [s]
            merge_ready[i] = s

        q_ready, k_ready, v_ready = [None] * 2, [None] * 2, []
        finish = None
        cross_ready = {}
        order = [(kind, i, w_in, column + i * SLOT) for i in range(2)
                 for kind, column in (("q", COL_Q), ("k", COL_K), ("v", COL_V))]
        order += [("xq", i, w_in, COL_XQ + i * SLOT) for i in range(2)]
        order += [("xk", i, w_mem_kv, i * SLOT) for i in range(2)]
        order += [("xv", i, w_mem_kv, D + i * SLOT) for i in range(2)]
        order += [("m", i, w_in, COL_MERGE + i * SLOT) for i in range(2 * 3)]
        for n, (kind, i, w, column) in enumerate(order):
            half = slice(4 * i, 4 * i + 4)
            if kind == "v" and i == 0:
                memT = turn_input(mem_tm, mem_scaled, "mem_norm_g")
            unit = project(w, column, memT if w is w_mem_kv else xT,
                           token_major=kind in ("v", "xv"))
            pending, finish = finish, None
            if n == 0:
                ss, s = inverse_rms(mem_tm, [[mem_ready]] * 2)
                mem_scaled = scale_tokens(mem_tm, mem_tm, ss, [s])
            if kind == "q":
                finish = q_ready, i, head_norm(unit, q_cm[:, half, :], ones64, DIFF_HEAD_DIM,
                                               qg, 1)
            if kind == "k":
                finish = k_ready, i, head_norm(unit, k_cm[:, half, :], ones64, DIFF_HEAD_DIM,
                                               v("diff_kn_g"), 1)
            if kind == "v":
                v_ready.append(values_slot(unit, v_tm[:, :, i * SLOT:(i + 1) * SLOT]))
            if kind == "xq":
                finish = xq_ready, i, head_norm(unit, xq_cm[:, half, :], ones, X_HEAD_DIM, xq_g, 2)
            if kind == "xk":
                finish = xk_ready, i, head_norm(unit, xk_cm[:, half, :], ones, X_HEAD_DIM,
                                                v("x_kn_g", 0, 2), 2)
            if kind == "xv":
                xv_ready.append(values_slot(unit, xv_tm[:, :, i * SLOT:(i + 1) * SLOT]))
            if kind == "m":
                if i == 0:
                    diff_values(7)
                    finish = diff_normed, 1, diff_norm(1)
                merge_slot(i, unit)
            if pending:
                where, at, steps = pending
                where[at] = steps()
            h = n - 3
            if 0 <= h - 2 < DIFF_HEADS - 1:
                diff_values(h - 2)
            if 0 <= h - 1 < DIFF_HEADS:
                diff_turn(h - 1)
            if 0 <= h < DIFF_HEADS:
                diff_scores(h)
            if h == 7:
                finish = diff_normed, 0, diff_norm(0)
            h = n - 11
            if 0 <= h - 2 < X_HEADS:
                cross_ready[h - 2] = cross_values(h - 2)
            if 0 <= h - 1 < X_HEADS:
                cross_turn(h - 1)
            if 0 <= h < X_HEADS:
                cross_scores(h)
        cross_out = list(cross_ready.values())

        stage("conv_norm")
        convolve_some(len(taps_left))
        normed = {}

        def gate_slot(column, o, ready):
            unit = project(w_in, column, xT)
            g = work.take()
            s = act.do(nc.scalar.activation, g.ap[:, :], unit.ap[:, :], ACT.Tanh, scale=0.5,
                       after=[unit.ready, *g.free])
            s = dve.do(nc.vector.scalar_tensor_tensor, out=g.ap[:, :], in0=g.ap[:, :],
                       scalar=1.0, in1=unit.ap[:, :], op0=ALU.add, op1=ALU.mult, after=[s])
            unit.free = [s]
            s = dve.do(nc.vector.tensor_tensor, o, o, tiles4(g.ap[:, :]), ALU.mult,
                       after=[s, *ready])
            g.free = [s]
            return s

        diff_out = [gate_slot(COL_DGATE + i * SLOT, q_cm[:, 4 * i:4 * i + 4, :],
                              [diff_normed[i]]) for i in range(2)]
        unit = units.take()
        after = [*conv_done.values(), *unit.free, ones_ready]
        for k in range(KT):
            s = pe.do(nc.tensor.matmul, unit.ap[:, 0:T], ones[:, :], conv_acc[:, k, :],
                      start=k == 0, stop=k == KT - 1, after=after)
            after = []
        mean = work.take()
        s = act.do(nc.scalar.activation, mean.ap[:, 0:T], unit.ap[:, 0:T], ACT.Copy,
                   scale=1.0 / D, after=[s, *mean.free])
        unit.free = [s]
        centred = dve.do(nc.vector.tensor_tensor, conv_acc[:, :, :], conv_acc[:, :, :],
                         mean.ap[:, 0:T].unsqueeze(1).to_broadcast([P, KT, T]), ALU.subtract,
                         after=[s])
        mean.free = [centred]
        x_gated = [gate_slot(COL_XGATE, xq_cm[:, 0:4, :], cross_out)]
        unit = units.take()
        after = [*unit.free]
        for half in range(2):
            sq = work.take()
            s = act.do(nc.scalar.activation, tiles4(sq.ap[:, :]),
                       conv_acc[:, 4 * half:4 * half + 4, :], ACT.Square,
                       after=[centred, *sq.free])
            after.append(s)
            for k in range(4):
                s = pe.do(nc.tensor.matmul, unit.ap[:, 0:T], ones[:, :],
                          sq.ap[:, k * T:(k + 1) * T], start=half == 0 and k == 0,
                          stop=half == 1 and k == 3, after=after)
                after = []
            sq.free = [s]
        rs = work.take()
        s, root = rsqrt_of(rs.ap[:, 0:T], unit.ap[:, 0:T], D, EPS5, [s, *rs.free])
        unit.free = [s]
        for k in range(KT):
            s = dve.do(nc.vector.scalar_tensor_tensor, out=conv_acc[:, k, :],
                       in0=conv_acc[:, k, :], scalar=v("conv_ln_g", k), in1=rs.ap[:, 0:T],
                       op0=ALU.mult, op1=ALU.mult, after=[root, centred])
            normed[k] = dve.do(nc.vector.tensor_scalar, conv_acc[:, k, :], conv_acc[:, k, :],
                               v("conv_ln_b", k), 0.25, ALU.add, ALU.mult, after=[s])
        rs.free = [s]
        x_gated.append(gate_slot(COL_XGATE + SLOT, xq_cm[:, 4:8, :], cross_out))
        conv_out = []
        for half in range(2):
            part = conv_acc[:, 4 * half:4 * half + 4, :]
            z = work.take()
            s = act.do(nc.scalar.activation, tiles4(z.ap[:, :]), part, ACT.Tanh, scale=2.0,
                       after=[normed[4 * half + 3], *z.free])
            s = dve.do(nc.vector.scalar_tensor_tensor, out=part, in0=tiles4(z.ap[:, :]),
                       scalar=1.0, in1=part, op0=ALU.add, op1=ALU.mult, after=[s])
            z.free = [s]
            conv_out.append(gate_slot(COL_CGATE + half * SLOT, part, [s]))
            if half == 0:
                pairs.take()
                diff_pair = split_input(q_cm, diff_out)

        stage("branches")
        y_cm = cm(big[3])
        x_res = tm(big[5])
        res_ready = act.dma(nc.scalar.dma_start, x_res, x_in, counter=c_x, after=cross_out)
        y_last = {}
        pair = diff_pair
        for branch, w in ((1, w_diff_proj), (2, w_x_proj), (0, w_conv_proj)):
            for i in range(2):
                unit = project(w, i * SLOT, pair)
                if i == 0 and branch == 1:
                    next_pair = split_input(xq_cm, x_gated)
                if i == 0 and branch == 2:
                    next_pair = split_input(conv_acc, conv_out)
                gates = merge[branch][:, 4 * i:4 * i + 4, :]
                part = y_cm[:, 4 * i:4 * i + 4, :]
                dst = work.take() if branch != 1 else None
                target = tiles4(dst.ap[:, :]) if dst else part
                s = dve.do(nc.vector.scalar_tensor_tensor, out=target, in0=gates, scalar=1.0,
                           in1=tiles4(unit.ap[:, :]), op0=ALU.add, op1=ALU.mult,
                           after=[unit.ready, merge_ready[2 * branch + i], *conv_done.values(),
                                  *(dst.free if dst else [])])
                unit.free = [s]
                if dst:
                    s = dve.do(nc.vector.tensor_tensor, part, part, target, ALU.add,
                               after=[s, y_last[i]])
                    dst.free = [s]
                y_last[i] = s
            pair = next_pair

        stage("block1_out")
        y_pair = split_input(y_cm, y_last)
        x1_ready = []
        for i in range(2):
            unit = project(w_out, i * SLOT, y_pair, token_major=True)
            part = x_res[:, :, i * SLOT:(i + 1) * SLOT]
            for t in range(TT):
                s = dve.do(nc.vector.scalar_tensor_tensor, out=part[:, t, :],
                           in0=unit.ap[:, t * SLOT:(t + 1) * SLOT], scalar=0.5,
                           in1=part[:, t, :], op0=ALU.mult, op1=ALU.add,
                           after=[unit.ready, res_ready])
            unit.free = [s]
            x1_ready.append([s])

        stage("block2_input")
        ss, s = inverse_rms(x_res, x1_ready)
        xn = tm(big[3])
        xT = turn_input(xn, scale_tokens(xn, x_res, ss, [s]), "norm_mix_2")

        gates_w = big[1][:, 1024:2048]
        bd = [gates_w[:, i * 512:(i + 1) * 512].rearrange("p (t j) -> p t j", t=4)
              for i in range(2)]
        keys = big[7][:, :].rearrange("p (s n) -> p s n", s=PEER_SIDES)
        ffn_gain = conv_in[:, :, :].rearrange("p k t -> p (k t)")[:, 1264:2288]
        c_small = load_counter("block2_small")
        bd_zero = dve.do(nc.vector.memset, gates_w, 0.0, after=[y_last[1]])
        bd_ready = []
        for i, w in enumerate((rg_w_a, rg_w_x)):
            for b in range(2):
                src = w.rearrange("(t b) i j -> b i t j", b=2)[b]
                dst = bd[i][64 * b:64 * b + 64, :, 64 * b:64 * b + 64]
                bd_ready.append(act.dma(nc.scalar.dma_start, dst, src,
                                        counter=load_counter(f"rg{i}{b}"), after=[bd_zero]))
        keys_ready = act.dma(nc.scalar.dma_start, keys, sub_keys_t, counter=c_small, after=[y_last[1]])
        ffn_gain_ready = act.dma(nc.scalar.dma_start, ffn_gain, norm_ffn,
                                 counter=load_counter("ffn_gain"), after=[y_last[1]])

        stage("rg_lambda")
        lam_v = v("rg_lambda_2", 0, RG_TILES)
        u, z, z2, acc, neg4sp = (cols(RG_TILES) for _ in range(5))
        s = act.do(nc.scalar.activation, u, lam_v, ACT.Abs, after=[vec_ready])
        s = act.do(nc.scalar.activation, u, u, ACT.Exp, scale=-1.0, after=[s])
        s2 = dve.do(nc.vector.tensor_scalar, z, u, 2.0, None, ALU.add, after=[s])
        s2 = dve.do(nc.vector.reciprocal, z, z, after=[s2])
        s2 = dve.do(nc.vector.tensor_tensor, z, z, u, ALU.mult, after=[s2])
        s2 = dve.do(nc.vector.tensor_tensor, z2, z, z, ALU.mult, after=[s2])
        s2 = dve.do(nc.vector.tensor_scalar, acc, z2, 1.0 / 17, None, ALU.mult, after=[s2])
        for n in (15, 13, 11, 9, 7, 5, 3):
            s2 = dve.do(nc.vector.scalar_tensor_tensor,
                out=acc, in0=acc, scalar=1.0 / n, in1=z2, op0=ALU.add, op1=ALU.mult, after=[s2])
        s2 = dve.do(nc.vector.scalar_tensor_tensor, out=acc, in0=acc, scalar=1.0, in1=z,
                                                     op0=ALU.add, op1=ALU.mult, after=[s2])
        s3 = dve.do(nc.vector.tensor_scalar, u, lam_v, 0.0, 4.0, ALU.min, ALU.mult, after=[s2])
        sp_ready = dve.do(nc.vector.scalar_tensor_tensor,
            out=neg4sp, in0=acc, scalar=-8.0, in1=u, op0=ALU.mult, op1=ALU.add, after=[s3])
        half_ba, half_bx = cols(RG_TILES), cols(RG_TILES)
        dve.do(nc.vector.tensor_scalar, half_ba, v("rg_b_a_2", 0, RG_TILES), 0.5, None,
                                         ALU.mult, after=[vec_ready])
        rg_bias_ready = dve.do(nc.vector.tensor_scalar,
            half_bx, v("rg_b_x_2", 0, RG_TILES), 0.5, None, ALU.mult, after=[vec_ready])

        xr = conv_in[:, 0:RG_TILES, 0:RG_WIDTH - 1 + T]
        xc = conv_acc[:, 0:4, :]
        decay = conv_acc[:, 4:8, :]
        drive = big[4][:, 0:4 * T].rearrange("p (j t) -> p j t", j=4)
        geluT = big[4][:, 4 * T:8 * T].rearrange("p (j t) -> p j t", j=4)
        gate_r = big[2][:, 0:4 * T].rearrange("p (j t) -> p j t", j=4)
        gate_i = big[2][:, 4 * T:8 * T].rearrange("p (j t) -> p j t", j=4)
        mixed = cm(big[6])
        q2_cm = big[0][:, 0:4 * T].rearrange("p (j t) -> p j t", j=4)
        k2_cm = big[0][:, 4 * T:8 * T].rearrange("p (j t) -> p j t", j=4)
        v2_tm = big[1][:, 0:2 * D_SB].rearrange("p (t c) -> p t c", t=TT)


        sb_state = {}
        sb_out = []

        def sb_logits(i):
            unit, lo, lb = units.take(), probs.take(), work.take()
            after = [q2_ready, *k2_ready, *unit.free]
            for m in range(2):
                rows = slice(64 * m, 64 * m + 64)
                for kt, q0, at in ((0, 0, 0), (1, P, 2 * P)):
                    s = pe.do(nc.tensor.matmul,
                        unit.ap[:, 512 * m + at:512 * m + at + T - q0],
                        k2_cm[rows, i, kt * P:(kt + 1) * P], q2_cm[rows, i, q0:T],
                        start=True, stop=True, after=after)
                    after = []
            z = unit.ap[:, :].rearrange("p (m c) -> p m c", m=2)[:, :, 0:384]
            lo_ap = lo.ap[:, :, :]
            lb_ap = lb.ap[:, 0:768].rearrange("p (a c) -> p a c", a=2)
            s = act.do(nc.scalar.activation, lo_ap, z, ACT.Abs, after=[s, *lo.free])
            s = act.do(nc.scalar.activation, lo_ap, lo_ap, ACT.Exp, scale=-1.0, after=[s])
            s = act.do(nc.scalar.activation, lo_ap, lo_ap, ACT.Ln, bias=ONE, after=[s])
            s = dve.do(nc.vector.scalar_tensor_tensor, out=lb_ap, in0=z, scalar=0.0, in1=lo_ap,
                                                        op0=ALU.min, op1=ALU.subtract,
                       after=[s, *lb.free])
            s = dve.do(nc.vector.tensor_tensor, lo_ap, lb_ap, z, ALU.subtract, after=[s])
            unit.free = [s]
            mask = before[:, :].unsqueeze(1).to_broadcast([P, 2, P])
            for at in (0, 2 * P):
                s2 = dve.do(nc.vector.tensor_tensor,
                    lo_ap[:, :, at:at + P], lo_ap[:, :, at:at + P], mask, ALU.mult, after=[s])
            sb_state[i] = lo, lb, lb_ap, s2

        def sb_weights(i):
            lo, lb, lb_ap, ready = sb_state[i]
            unit = units.take()
            after = [ready, *unit.free]
            for m in range(2):
                at = 512 * m
                for dst, w, src, n, start, stop in ((0, later, 0, T, True, False),
                                                    (P, ones, 2 * P, P, False, True),
                                                    (2 * P, later, 2 * P, P, True, True)):
                    s = pe.do(nc.tensor.matmul, unit.ap[:, at + dst:at + dst + n], w[:, :],
                                                  lo.ap[:, m, src:src + n], start=start,
                                                  stop=stop, after=after)
                    after = []
            lo.free = [s]
            suffix = unit.ap[:, :].rearrange("p (m c) -> p m c", m=2)[:, :, 0:384]
            s = dve.do(nc.vector.tensor_tensor, lb_ap, lb_ap, suffix, ALU.add, after=[s])
            unit.free = [s]
            s = act.do(nc.scalar.activation, lb_ap, lb_ap, ACT.Exp, after=[s])
            mask = before[:, :].unsqueeze(1).to_broadcast([P, 2, P])
            for at in (0, 2 * P):
                s2 = dve.do(nc.vector.tensor_tensor,
                    lb_ap[:, :, at:at + P], lb_ap[:, :, at:at + P], mask, ALU.mult, after=[s])
            sb_state[i] = lb, lb_ap, s2

        def sb_values(i):
            lb, lb_ap, ready = sb_state[i]
            bank = banks.take()
            after = [ready, v2_ready, *bank.free]
            for m in range(2):
                rows = slice(64 * m, 64 * m + 64)
                h = 2 * i + m
                pe.do(nc.tensor.matmul,
                    bank.ap[rows, 0:T], v2_tm[:, 0, h * 64:(h + 1) * 64], lb_ap[:, m, 0:T],
                    start=True, stop=False, after=after)
                after = []
                s = pe.do(nc.tensor.matmul,
                    bank.ap[rows, P:T], v2_tm[:, 1, h * 64:(h + 1) * 64],
                    lb_ap[:, m, 2 * P:3 * P], start=False, stop=True)
            lb.free = [s]
            s = act.do(nc.scalar.copy, mixed[:, i, :], bank.ap[:, 0:T], after=[s])
            bank.free = [s]
            sb_out.append(s)

        stage("sb_qk")
        unit = project(w_in_2, 0, xT)
        q2_finish = head_norm(unit, q2_cm, ones64, SB_HEAD_DIM, q2_g, 1)
        unit = project(w_in_2, D_SB, xT)
        q2_ready = q2_finish()
        k2_finish = head_norm(unit, k2_cm, ones64, SB_HEAD_DIM, v("k_norm_2"), 1)

        stage("rg_in")
        k2_ready = []
        unit = project(w_in_2, 3 * D_SB, xT, between=[lambda: k2_ready.append(k2_finish())])
        pad = dve.do(nc.vector.memset, xr[:, :, 0:RG_WIDTH - 1], 0.0, after=[*conv_done.values()])
        s = act.do(nc.scalar.copy, xr[:, :, RG_WIDTH - 1:], tiles4(unit.ap[:, :]),
                   after=[unit.ready])
        unit.free = [s]
        xr_ready = s
        last = {}
        for k in range(RG_WIDTH):
            for j in range(RG_TILES):
                tap = v("conv_w_2", j * RG_WIDTH + k)
                src, dst = xr[:, j, k:k + T], xc[:, j, :]
                if k == 0:
                    last[j] = dve.do(nc.vector.tensor_scalar,
                        dst, src, tap, v("conv_b_2", j), ALU.mult, ALU.add,
                        after=[xr_ready, pad])
                else:
                    last[j] = dve.do(nc.vector.scalar_tensor_tensor,
                        out=dst, in0=src, scalar=tap, in1=dst, op0=ALU.mult, op1=ALU.add,
                        after=[last[j]])
        xc_ready = list(last.values())
        sb_logits(0)

        stage("sb_attention")
        unit = project(w_in_2, 2 * D_SB, xT, token_major=True, between=[lambda: sb_logits(1)])
        s = act.do(nc.scalar.copy, v2_tm, unit.ap[:, :].rearrange("p (t c) -> p t c", t=TT),
                   after=[unit.ready])
        unit.free = [s]
        v2_ready = s
        sb_weights(0)
        sb_logits(2)

        stage("rg_gates")
        gate_units = []
        for i in range(2):
            unit = units.take()
            after = [*unit.free, *xc_ready, *bd_ready]
            for j in range(RG_TILES):
                s = pe.do(nc.tensor.matmul,
                    unit.ap[:, j * T:(j + 1) * T], bd[i][:, j, :], xc[:, j, :], start=True,
                    stop=True, after=after)
                after = []
            dst, bias = ((gate_r, half_ba), (gate_i, half_bx))[i]
            for j in range(RG_TILES):
                g = act.do(nc.scalar.activation,
                    dst[:, j, :], unit.ap[:, j * T:(j + 1) * T], ACT.Tanh, scale=0.5,
                    bias=bias[:, j:j + 1], after=[s, rg_bias_ready])
            unit.free = [g]
            gate_units.append(g)
        for j in range(RG_TILES):
            s = act.do(nc.scalar.activation,
                decay[:, j, :], gate_r[:, j, :], ACT.Exp, scale=neg4sp[:, j:j + 1],
                bias=neg4sp[:, j:j + 1], after=[gate_units[0], sp_ready])
            s = act.do(nc.scalar.activation,
                gate_r[:, j, :], gate_r[:, j, :], ACT.Tanh, scale=neg4sp[:, j:j + 1],
                bias=neg4sp[:, j:j + 1], after=[s])
        s2 = dve.do(nc.vector.tensor_tensor, drive, decay, decay, ALU.mult, after=[s])
        s2 = dve.do(nc.vector.scalar_tensor_tensor, out=gate_r, in0=drive, scalar=1.0,
                                                     in1=gate_r, op0=ALU.add, op1=ALU.mult,
                    after=[s2])
        s2 = dve.do(nc.vector.tensor_scalar, gate_r, gate_r, -1.0, 0.0, ALU.mult, ALU.max,
                    after=[s2])
        unit = project(w_in_2, 3 * D_SB + D_RG, xT,
                       between=[lambda: sb_values(0), lambda: sb_weights(1),
                                lambda: sb_logits(3)])
        s = act.do(nc.scalar.activation, gate_r, gate_r, ACT.Sqrt, after=[s2])
        s2 = dve.do(nc.vector.scalar_tensor_tensor, out=drive, in0=gate_i, scalar=1.0, in1=xc,
                                                     op0=ALU.add, op1=ALU.mult,
                    after=[s2, gate_units[1], *xc_ready])
        s2 = dve.do(nc.vector.scalar_tensor_tensor, out=drive, in0=drive, scalar=0.5,
                                                     in1=gate_r, op0=ALU.mult, op1=ALU.mult,
                    after=[s2, s])
        for j in range(RG_TILES):
            s2_ = dve.do(nc.vector.tensor_tensor_scan,
                mixed[:, 4 + j, :], decay[:, j, :], drive[:, j, :], 0.0, ALU.mult, ALU.add,
                after=[s2])
        scan_ready = s2_

        s = act.do(nc.scalar.activation, geluT, tiles4(unit.ap[:, :]),
                                                     ACT.Gelu_apprx_tanh, after=[unit.ready])
        unit.free = [s]
        rg_ready = dve.do(nc.vector.tensor_tensor, mixed[:, 4:8, :], mixed[:, 4:8, :], geluT,
                                                    ALU.mult, after=[s, scan_ready])

        stage("mix")
        mixed_pair = pairs.take()
        mixed_pair.ready = [None] * KT
        mixed_pair.order = [4, 5, 6, 7, 0, 1, 2, 3]

        def mix_sums(half, ready):
            o, sq = mixed[:, 4 * half:4 * half + 4, :], work.take()
            s = act.do(nc.scalar.activation, tiles4(sq.ap[:, :]), o, ACT.Square,
                       after=[*ready, *sq.free])
            unit = units.take()
            s = sum_over_channels(sq.ap, [s], ones, [[0, 1, 2, 3]], T, unit)
            s, root = rsqrt_of(sq.ap[:, 0:T], unit.ap[:, 0:T], D_SB, EPS6, [s])
            unit.free = [s]
            return sq, root

        def mix_split(half, gain, ready, sq, root):
            hi, lo = mixed_pair.ap
            for j in range(4):
                k = 4 * half + j
                s = dve.do(nc.vector.scalar_tensor_tensor,
                    out=mixed[:, k, :], in0=mixed[:, k, :], scalar=v(gain, j),
                    in1=sq.ap[:, 0:T], op0=ALU.mult, op1=ALU.mult, after=[root, *ready])
                if j == 3:
                    sq.free = [s]
                s2 = act.do(nc.scalar.copy, hi[:, k, :], mixed[:, k, :],
                            after=[s, *mixed_pair.free])
                mixed_pair.ready[k] = s2
            for j in range(4):
                k = 4 * half + j
                mixed_pair.ready[k] = dve.do(
                    nc.vector.tensor_tensor, lo[:, k, :], mixed[:, k, :],
                    hi[:, k, :].bitcast(F32), ALU.subtract, after=[mixed_pair.ready[k]])

        sb_values(1)
        sb_weights(2)
        sb_weights(3)
        sb_values(2)
        sq, root = mix_sums(1, [rg_ready])
        mix_split(1, "out_norm_rg_2", [rg_ready], sq, root)
        sb_values(3)
        sq, root = mix_sums(0, sb_out)
        mix_split(0, "out_norm_sb_2", sb_out, sq, root)
        x2_ready = []
        for i in range(2):
            unit = project(w_out_2, i * SLOT, mixed_pair, token_major=True)
            part = x_res[:, :, i * SLOT:(i + 1) * SLOT]
            for t in range(TT):
                s = dve.do(nc.vector.tensor_tensor, part[:, t, :],
                           unit.ap[:, t * SLOT:(t + 1) * SLOT], part[:, t, :], ALU.add,
                           after=[unit.ready])
            unit.free = [s]
            x2_ready.append([s])

        stage("peer_queries")
        h3 = tm(big[3])
        ss, s = inverse_rms(x_res, x2_ready)
        h3_ready = []
        for half in range(2):
            c = slice(half * SLOT, (half + 1) * SLOT)
            for t in range(TT):
                s2 = dve.do(nc.vector.scalar_tensor_tensor,
                    out=h3[:, t, c], in0=x_res[:, t, c], scalar=ss[:, t:t + 1],
                    in1=ffn_gain[:, c], op0=ALU.mult, op1=ALU.mult,
                    after=[s, ffn_gain_ready])
            h3_ready.append([s2])
        xT = turn_input(h3, h3_ready)
        h3_ready, x2_ready = h3_ready[1][0], x2_ready[1][0]
        pq = [cm(big[0]), cm(big[1])]
        scores = [ap.rearrange("p (s n) -> p s n", s=PEER_SIDES)
                  for ap in (big[4][:, :], conv_acc[:, :, :].rearrange("p k t -> p (k t)"))]
        scored_sides = {}

        small = big[6][:, :]
        top_s = small[:, 0:32].rearrange("p (s k) -> p s k", s=2)
        top_i = small[:, 32:64].bitcast(U32).rearrange("p (s k) -> p s k", s=2)
        top_f = small[:, 64:96].rearrange("p (s k) -> p s k", s=2)
        best, pos = small[:, 96:112], small[:, 112:128].bitcast(U32)
        part_i = [small[:, 128 + 16 * i:144 + 16 * i].bitcast(U32) for i in range(2)]
        part_f = small[:, 160:192].rearrange("p (s k) -> p s k", s=2)
        place_f = [small[:, 192 + 16 * i:208 + 16 * i] for i in range(2)]
        cand = small[:, 256:512]
        onehot = small[:, 512:1024].rearrange("p (s k c) -> p s k c", s=2, k=PEER_TOPK)
        sel = big[6][:, 1024:2048]
        expert = [sel[:, t * 128:(t + 1) * 128].bitcast(U32) for t in range(TT)]
        weight = [sel[:, 256 + t * 128:256 + (t + 1) * 128] for t in range(TT)]
        dot = [sel[:, 512 + t * 128:512 + (t + 1) * 128] for t in range(TT)]
        coef = dot
        total = [sel[:, 768 + t * 8:776 + t * 8] for t in range(TT)]
        lowest = [sel[:, 784 + t * 8:792 + t * 8] for t in range(TT)]

        def top16(values, out_s, out_i, after):
            s = dve.do(nc.vector.max, out_s[:, 0:8], values, after=after)
            s = dve.do(nc.vector.max_index, out_i[:, 0:8], out_s[:, 0:8], values, after=[s])
            s = dve.do(nc.vector.match_replace, values, out_s[:, 0:8], values, -3.0e38,
                       after=[s])
            s = dve.do(nc.vector.max, out_s[:, 8:16], values, after=[s])
            return dve.do(nc.vector.max_index, out_i[:, 8:16], out_s[:, 8:16], values,
                          after=[s])

        chosen = {}
        previous = [x2_ready]

        def choose(t, h):
            s = previous[0]
            for side in range(2):
                s = top16(scores[t][:, 2 * h + side, :], top_s[:, side, :], top_i[:, side, :],
                          [s, scored_sides[t, h // 2]])
                yield
            s = dve.do(nc.vector.tensor_copy, top_f, top_i, after=[s])
            grid = [P, PEER_TOPK, PEER_TOPK]
            s = dve.do(nc.vector.tensor_tensor, cand.rearrange("p (i j) -> p i j", i=PEER_TOPK),
                       top_s[:, 0, :].unsqueeze(2).to_broadcast(grid),
                       top_s[:, 1, :].unsqueeze(1).to_broadcast(grid), ALU.add, after=[s])
            yield
            s = top16(cand, best, pos, [s])
            yield
            low, w = lowest[t][:, h:h + 1], weight[t][:, h * PEER_TOPK:(h + 1) * PEER_TOPK]
            s = dve.do(nc.vector.tensor_scalar, low, best[:, 0:1], -1.0, None, ALU.mult,
                       after=[s])
            low_ready = s
            for side, (op, by) in enumerate(((ALU.logical_shift_right, 4),
                                             (ALU.bitwise_and, PEER_TOPK - 1))):
                s1 = dve.do(nc.vector.tensor_scalar, part_i[side], pos, by, None, op, after=[s])
                s2 = dve.do(nc.vector.tensor_copy, part_f[:, side, :], part_i[side], after=[s1])
            yield
            for side in range(2):
                s = dve.do(nc.vector.tensor_tensor, onehot[:, side],
                           iota16[:, :].unsqueeze(1).to_broadcast(grid),
                           part_f[:, side, :].unsqueeze(2).to_broadcast(grid), ALU.is_equal,
                           after=[s2])
                yield
            for side in range(2):
                s1 = dve.do(nc.vector.tensor_tensor, onehot[:, side], onehot[:, side],
                            top_f[:, side, :].unsqueeze(1).to_broadcast(grid), ALU.mult,
                            after=[s])
                yield
            exped = act.do(nc.scalar.activation, w, best, ACT.Exp, bias=low,
                           accum_out=total[t][:, h:h + 1], after=[low_ready])
            for side in range(2):
                s = dve.do(nc.vector.tensor_reduce, place_f[side], onehot[:, side], AX, ALU.add,
                           after=[s1])
                yield
            picked = dve.do(nc.vector.scalar_tensor_tensor,
                            out=expert[t][:, h * PEER_TOPK:(h + 1) * PEER_TOPK], in0=place_f[0],
                            scalar=float(PEER_KEYS), in1=place_f[1], op0=ALU.mult, op1=ALU.add,
                            after=[s])
            s = dve.do(nc.vector.reciprocal, total[t][:, h:h + 1], total[t][:, h:h + 1],
                       after=[exped, picked])
            previous[0] = s
            chosen[t, h] = picked, s

        pair0_free = pair0.free
        pair0_space.close()
        flat = lambda ap: ap.rearrange("p k t -> p (k t)")

        def row(name, ap, free):
            buffer = Buffer(ap, load_counter(name))
            buffer.free = free
            return buffer

        uv = Ring([row(f"uv{i}", sb(f"row{i}", [2 * D])[:, :], pair0_free) for i in range(2)]
                  + [row("uv2", big[2][:, :], [x2_ready]),
                     row("uv3", flat(conv_in[:, :, :])[:, 0:2 * D], [h3_ready])])
        diag = Ring([Buffer(probs.buffers[i % 2].ap[:, i // 2 % 2, i // 4 * P:(i // 4 + 1) * P])
                     for i in range(12)])
        for i, b in enumerate(diag.buffers):
            b.free = probs.buffers[i % 2].free
        out_tm = out.rearrange("(t p) c -> p t c", p=P)
        c_out = load_counter("out")
        heads = [(t, h) for t in range(TT) for h in range(PEER_HEADS)]
        picks = [(t, n) for t in range(TT) for n in range(PICKS)]
        LAG = 1
        y_unit = {}
        asked, held = [], []

        def gather(t, n):
            slot = uv.take()
            index = expert[t][:, n:n + 1]
            ready = pool.dma(nc.gpsimd.indirect_dma_start, out=slot.ap, out_offset=None,
                             in_=experts,
                             in_offset=bass.IndirectOffsetOnAxis(ap=index, axis=0),
                             counter=slot.counter,
                             after=[chosen[t, n // PEER_TOPK][0], *slot.free])
            asked.append((t, n, slot, ready))

        def dot_product():
            t, n, slot, ready = asked.pop(0)
            junk = work.take()
            s = dve.do(nc.vector.tensor_tensor_reduce, out=junk.ap[:, 0:D], in0=h3[:, t, :],
                       in1=slot.ap[:, 0:D], scale=1.0, scalar=0.0, op0=ALU.mult, op1=ALU.add,
                       accum_out=dot[t][:, n:n + 1], after=[ready, h3_ready, *junk.free])
            junk.free = [s]
            held.append((t, n, slot, s))

        def add_value():
            t, n, slot, dot_ready = held.pop(0)
            h = n // PEER_TOPK
            here = coef[t][:, n:n + 1]
            g = act.do(nc.scalar.activation, here, here, ACT.Gelu_apprx_tanh, after=[dot_ready])
            c = dve.do(nc.vector.scalar_tensor_tensor, out=here, in0=here,
                       scalar=total[t][:, h:h + 1], in1=weight[t][:, n:n + 1], op0=ALU.mult,
                       op1=ALU.mult, after=[g, chosen[t, h][1]])
            if t not in y_unit:
                y_unit[t] = units.take()
            unit, d = y_unit[t], diag.take()
            s = act.do(nc.scalar.activation, d.ap, ident[:, :], ACT.Copy, scale=here,
                       after=[c, *d.free])
            for half in range(2):
                m = pe.do(nc.tensor.matmul, unit.ap[:, half * 512:(half + 1) * 512], d.ap,
                          slot.ap[:, D + half * 512:D + (half + 1) * 512], start=n == 0,
                          stop=n == PICKS - 1, after=[s, *unit.free])
            d.free, slot.free = [m], [m]
            if n == PICKS - 1:
                y = x_res[:, t, :]
                s = dve.do(nc.vector.tensor_tensor, y, unit.ap[:, :], y, ALU.add, after=[m])
                sp.dma(nc.sync.dma_start, out_tm[:, t, :], y, counter=c_out, after=[s])

        def score(i, copied):
            for t in range(TT):
                bank = banks.take()
                after = [*bank.free, copied, keys_ready]
                for j in range(4):
                    s = pe.do(nc.tensor.matmul, bank.ap[:, j * P:(j + 1) * P],
                              pq[i // 2][:, 4 * (i % 2) + j, t * P:(t + 1) * P],
                              keys[:, 4 * i + j, :], start=True, stop=True, after=after)
                    after = []
                d = act.do(nc.scalar.copy, scores[t][:, 4 * i:4 * i + 4, :],
                           bank.ap[:, :].rearrange("p (s n) -> p s n", s=4), after=[s])
                bank.free = [d]
                scored_sides[t, i] = d
            return s

        def score_second():
            uv.buffers.insert(0, row("uv4", big[0][:, :], [score(1, copied)]))
            gather(*picks.pop(0))

        between = {0: [], 1: [], 2: [score_second],
                   3: [lambda: score(2, copied), dot_product, dot_product, dot_product]}
        for i in range(4):
            unit = project(w_query, i * SLOT, xT, between=between[i])
            sides = slice(4 * (i % 2), 4 * (i % 2) + 4)
            copied = act.do(nc.scalar.copy, pq[i // 2][:, sides, :], tiles4(unit.ap[:, :]),
                            after=[unit.ready])
            unit.free = [copied]
            if i == 0:
                score(0, copied)
                beside += [choose(*heads[0]), choose(*heads[1])]
            if i == 1:
                for _ in range(4):
                    gather(*picks.pop(0))
        pq_done = score(3, copied)

        later_rows = [row(f"uv{5 + i}", flat(b.ap[:, :, :]), b.free)
                      for i, b in enumerate(w_raw.buffers)]
        later_rows += [row(f"uv{7 + i}", big[b][:, :], [pq_done]) for i, b in enumerate((1, 7))]
        uv.buffers[0:0] = later_rows
        gather(*picks.pop(0))
        gather(*picks.pop(0))

        for i in range(TT * PICKS):
            if i % PEER_TOPK == 0:
                t, h = heads[i // PEER_TOPK]
                if h % 4 == 0:
                    stage(f"retrieve_t{t}h{h}")
                ahead = i // PEER_TOPK + 2
                steps = choose(*heads[ahead]) if ahead < len(heads) else iter(())
            if picks:
                gather(*picks.pop(0))
            if asked:
                dot_product()
            while len(held) > LAG:
                add_value()
            next(steps, None)
        while held:
            add_value()

        queues = (pe, act, dve, pool, sp)
        for q in queues:
            q.number()
        with nc.Block() as block:
            @block.tensor
            def _(e):
                pe.emit(e)

            @block.scalar
            def _(e):
                act.emit(e)

            @block.vector
            def _(e):
                dve.emit(e)

            @block.gpsimd
            def _(e):
                pool.emit(e)

            @block.sync
            def _(e):
                sp.emit(e)
                e.wait_ge(c_out.sem, c_out.value)


def kernel(**inputs):
    import numpy as np
    import concourse.bacc as bacc
    from concourse.bass_utils import run_bass_kernel_spmd

    a = {n: np.asarray(x) for n, x in inputs.items()}

    def per_channel(name):
        return a[name].reshape(-1, P).T

    def halves(name):
        return np.concatenate([a[name].reshape(64, 1)] * 2, axis=0)

    def on_all(name):
        return np.broadcast_to(a[name].reshape(1, -1), (P, 64))

    def taps(name):
        k, c = a[name].shape[-2:]
        return a[name].reshape(k, c // P, P).transpose(2, 1, 0).reshape(P, -1)

    pack = {}
    for name, n in VECTORS:
        if name in ("conv_dw", "conv_w_2"):
            pack[name] = taps(name)
        elif name.startswith("lambda_"):
            pack[name] = on_all(name)
        elif a[name].size == 64:
            pack[name] = halves(name)
        else:
            pack[name] = per_channel(name)
        assert pack[name].shape == (P, n), name
    arrays = {
        "x": a["x"][0], "mem": a["mem"][0],
        "vectors": np.concatenate([pack[n] for n, _ in VECTORS], axis=1),
        "w_in": a["w_in"][0], "w_conv_proj": a["w_conv_proj"][0],
        "w_diff_proj": a["w_diff_proj"][0], "w_mem_kv": a["w_mem_kv"][0],
        "w_x_proj": a["w_x_proj"][0], "w_out": a["w_out"][0], "w_in_2": a["w_in_2"][0],
        "rg_w_a": a["rg_w_a_2"][0], "rg_w_x": a["rg_w_x_2"][0], "w_out_2": a["w_out_2"][0],
        "norm_ffn": np.broadcast_to(a["norm_ffn_2"][0].reshape(1, D), (P, D)),
        "w_query": a["peer_w_query_2"][0].reshape(D, PEER_SIDES * P),
        "sub_keys_t": a["peer_sub_keys_2"][0].reshape(PEER_SIDES, PEER_KEYS, P).transpose(2, 0, 1),
        "experts": np.concatenate([a["peer_u_2"][0], a["peer_v_2"][0]], axis=1),
    }
    arrays = {f"in_{n}": np.ascontiguousarray(x) for n, x in arrays.items()}
    nc = bacc.Bacc("TRN2", target_bir_lowering=False, num_devices=1)
    aps = [nc.dram_tensor(n, x.shape, mybir.dt.from_np(x.dtype), kind="ExternalInput").ap()
           for n, x in arrays.items()]
    out = nc.dram_tensor("out_x", [T, D], F32, kind="ExternalOutput").ap()
    build(nc, *aps, out)
    r = run_bass_kernel_spmd(nc, [arrays], core_ids=[0])
    return r.results[0]["out_x"].reshape(1, T, D)
```
